# Optimizing a Trainium2 kernel written in Bass

```python
import math
import jax, jax.numpy as jnp
from jax import lax
import numpy as np

D_MODEL = 1024
BATCH = 1
SEQ = 512
DEPTH = 2

CHUNK = 64
Q_BLOCK = 128
N_MIXERS = 2
N_A = (DEPTH + 1) // 2
N_B = DEPTH // 2

MLA_HEADS = 8
MLA_NOPE = 128
MLA_ROPE = 64
MLA_V = 128
MLA_Q_RANK = 384
MLA_KV_RANK = 256
MLA_IN = MLA_Q_RANK + MLA_KV_RANK + MLA_ROPE
ROPE_THETA = 10000.0

DIFF_HEADS = 8
DIFF_HEAD_DIM = 64
DIFF_V = 2 * DIFF_HEAD_DIM
DIFF_IN = 3 * DIFF_HEADS * 2 * DIFF_HEAD_DIM

D_FF = -(-8 * D_MODEL // (3 * 256)) * 256

ALPHA = (2 * DEPTH) ** 0.25
BETA = (8 * DEPTH) ** -0.25
LN_EPS = 1e-5
RMS_EPS = 1e-6
NEG_BIG = -1e30


def _layernorm(x, g, b):
    x32 = x.astype(jnp.float32)
    mu = jnp.mean(x32, axis=-1, keepdims=True)
    var = jnp.mean(jnp.square(x32 - mu), axis=-1, keepdims=True)
    y = (x32 - mu) * lax.rsqrt(var + LN_EPS) * g.astype(jnp.float32) + b.astype(jnp.float32)
    return y.astype(x.dtype)

def _rmsnorm(x, g):
    x32 = x.astype(jnp.float32)
    y = x32 * lax.rsqrt(jnp.mean(jnp.square(x32), axis=-1, keepdims=True) + RMS_EPS)
    return (y * g.astype(jnp.float32)).astype(x.dtype)

def _chunk_mask(q_start, seq):
    q_idx = q_start + jnp.arange(Q_BLOCK)
    k_idx = jnp.arange(seq)
    return (k_idx[None, :] // CHUNK) <= (q_idx[:, None] // CHUNK)

def _rope_tables(seq, dtype):
    inv_freq = ROPE_THETA ** (-jnp.arange(0, MLA_ROPE, 2, dtype=jnp.float32) / MLA_ROPE)
    ang = jnp.arange(seq, dtype=jnp.float32)[:, None] * inv_freq[None, :]
    return jnp.cos(ang).astype(dtype), jnp.sin(ang).astype(dtype)

def _apply_rope(x, cos, sin):
    x1, x2 = jnp.split(x, 2, axis=-1)
    return jnp.concatenate([x1 * cos - x2 * sin, x1 * sin + x2 * cos], axis=-1)

def _to_blocks(t, n_blocks):
    b = t.shape[0]
    t = t.reshape((b, n_blocks, Q_BLOCK) + t.shape[2:])
    return jnp.moveaxis(t, 1, 0)

def _from_blocks(t):
    t = jnp.moveaxis(t, 0, 1)
    return t.reshape((t.shape[0], t.shape[1] * t.shape[2]) + t.shape[3:])

def _mla_mixer(x, w_in, g_q, g_kv, w_uq, w_ukv, w_o):
    b, s, _ = x.shape
    h = x @ w_in
    c_q, c_kv, k_rope = jnp.split(h, [MLA_Q_RANK, MLA_Q_RANK + MLA_KV_RANK], axis=-1)
    c_q = _rmsnorm(c_q, g_q)
    c_kv = _rmsnorm(c_kv, g_kv)
    q = (c_q @ w_uq).reshape(b, s, MLA_HEADS, MLA_NOPE + MLA_ROPE)
    q_nope, q_rope = q[..., :MLA_NOPE], q[..., MLA_NOPE:]
    kv = (c_kv @ w_ukv).reshape(b, s, MLA_HEADS, MLA_NOPE + MLA_V)
    k_nope, v = kv[..., :MLA_NOPE], kv[..., MLA_NOPE:]
    cos, sin = _rope_tables(s, x.dtype)
    q_rope = _apply_rope(q_rope, cos[:, None, :], sin[:, None, :])
    k_rope = _apply_rope(k_rope, cos, sin)
    scale = (MLA_NOPE + MLA_ROPE) ** -0.5
    n_blocks = s // Q_BLOCK

    def block(args):
        i, qn_b, qr_b = args
        logits = (jnp.einsum('bqhd,bkhd->bhqk', qn_b, k_nope, preferred_element_type=jnp.float32)
                  + jnp.einsum('bqhd,bkd->bhqk', qr_b, k_rope, preferred_element_type=jnp.float32))
        logits = jnp.where(_chunk_mask(i * Q_BLOCK, s), logits * scale, NEG_BIG)
        p = jax.nn.softmax(logits, axis=-1)
        o = jnp.einsum('bhqk,bkhd->bqhd', p.astype(v.dtype), v, preferred_element_type=jnp.float32)
        return o.astype(x.dtype)

    o = lax.map(block, (jnp.arange(n_blocks), _to_blocks(q_nope, n_blocks), _to_blocks(q_rope, n_blocks)))
    o = _from_blocks(o).reshape(b, s, MLA_HEADS * MLA_V)
    return o @ w_o

def _diff_mixer(x, w_in, lam_q1, lam_k1, lam_q2, lam_k2, g_sub, w_o, lambda_init):
    b, s, _ = x.shape
    qk_w = DIFF_HEADS * 2 * DIFF_HEAD_DIM
    h = x @ w_in
    q, k, v = jnp.split(h, [qk_w, 2 * qk_w], axis=-1)
    q = q.reshape(b, s, DIFF_HEADS, 2, DIFF_HEAD_DIM)
    k = k.reshape(b, s, DIFF_HEADS, 2, DIFF_HEAD_DIM)
    v = v.reshape(b, s, DIFF_HEADS, DIFF_V)
    f32 = jnp.float32
    lam = (jnp.exp(jnp.sum(lam_q1.astype(f32) * lam_k1.astype(f32)))
           - jnp.exp(jnp.sum(lam_q2.astype(f32) * lam_k2.astype(f32))) + lambda_init)
    slopes = jnp.exp2(-8.0 * jnp.arange(1, DIFF_HEADS + 1, dtype=f32) / DIFF_HEADS)
    scale = DIFF_HEAD_DIM ** -0.5
    n_blocks = s // Q_BLOCK
    k_pos = jnp.arange(s)

    def block(args):
        i, q_b = args
        q_pos = i * Q_BLOCK + jnp.arange(Q_BLOCK)
        dist = jnp.abs(q_pos[:, None] - k_pos[None, :]).astype(f32)
        logits = jnp.einsum('bqhmd,bkhmd->bmhqk', q_b, k, preferred_element_type=f32) * scale
        logits = logits - slopes[:, None, None] * dist
        logits = jnp.where(_chunk_mask(i * Q_BLOCK, s), logits, NEG_BIG)
        p = jax.nn.softmax(logits, axis=-1)
        a = p[:, 0] - lam * p[:, 1]
        o = jnp.einsum('bhqk,bkhe->bqhe', a.astype(v.dtype), v, preferred_element_type=f32)
        return o.astype(x.dtype)

    o = lax.map(block, (jnp.arange(n_blocks), _to_blocks(q, n_blocks)))
    o = _from_blocks(o)
    o = _rmsnorm(o, g_sub) * (1.0 - lambda_init)
    return o.reshape(b, s, DIFF_HEADS * DIFF_V) @ w_o

def _swiglu(x, w_gu, w_down):
    gate, up = jnp.split(x @ w_gu, 2, axis=-1)
    return (jax.nn.silu(gate) * up) @ w_down

def first_inputs(seed: int = 0) -> dict:
    key = jax.random.key(seed)
    ks = jax.random.split(key, 24)
    n = jax.random.normal
    f = jnp.float32
    d = D_MODEL
    return {
        "x": n(ks[0], (BATCH, SEQ, d), f),
        "mla_w_in": n(ks[1], (N_A, d, MLA_IN), f) * d ** -0.5,
        "mla_g_q": 1.0 + 0.02 * n(ks[2], (N_A, MLA_Q_RANK), f),
        "mla_g_kv": 1.0 + 0.02 * n(ks[3], (N_A, MLA_KV_RANK), f),
        "mla_w_uq": n(ks[4], (N_A, MLA_Q_RANK, MLA_HEADS * (MLA_NOPE + MLA_ROPE)), f) * MLA_Q_RANK ** -0.5,
        "mla_w_ukv": n(ks[5], (N_A, MLA_KV_RANK, MLA_HEADS * (MLA_NOPE + MLA_V)), f) * MLA_KV_RANK ** -0.5,
        "mla_w_o": n(ks[6], (N_A, MLA_HEADS * MLA_V, d), f) * (MLA_HEADS * MLA_V) ** -0.5 * BETA,
        "diff_w_in": n(ks[7], (N_B, d, DIFF_IN), f) * d ** -0.5,
        "diff_lam_q1": 0.1 * n(ks[8], (N_B, DIFF_HEAD_DIM), f),
        "diff_lam_k1": 0.1 * n(ks[9], (N_B, DIFF_HEAD_DIM), f),
        "diff_lam_q2": 0.1 * n(ks[10], (N_B, DIFF_HEAD_DIM), f),
        "diff_lam_k2": 0.1 * n(ks[11], (N_B, DIFF_HEAD_DIM), f),
        "diff_g_sub": 1.0 + 0.02 * n(ks[12], (N_B, DIFF_V), f),
        "diff_w_o": n(ks[13], (N_B, DIFF_HEADS * DIFF_V, d), f) * (DIFF_HEADS * DIFF_V) ** -0.5 * BETA,
        "ln_mix_g": 1.0 + 0.02 * n(ks[14], (DEPTH, d), f),
        "ln_mix_b": 0.02 * n(ks[15], (DEPTH, d), f),
        "ffn_w_gu": n(ks[16], (DEPTH, d, 2 * D_FF), f) * d ** -0.5,
        "ffn_w_down": n(ks[17], (DEPTH, D_FF, d), f) * D_FF ** -0.5 * BETA,
        "ln_ffn_g": 1.0 + 0.02 * n(ks[18], (DEPTH, d), f),
        "ln_ffn_b": 0.02 * n(ks[19], (DEPTH, d), f),
    }

def first_block(x, mla_w_in, mla_g_q, mla_g_kv, mla_w_uq, mla_w_ukv, mla_w_o,
              diff_w_in, diff_lam_q1, diff_lam_k1, diff_lam_q2, diff_lam_k2, diff_g_sub, diff_w_o,
              ln_mix_g, ln_mix_b, ffn_w_gu, ffn_w_down, ln_ffn_g, ln_ffn_b):
    h = x
    for i in range(DEPTH):
        j = i // N_MIXERS
        if i % N_MIXERS == 0:
            mix = _mla_mixer(h, mla_w_in[j], mla_g_q[j], mla_g_kv[j], mla_w_uq[j], mla_w_ukv[j], mla_w_o[j])
        else:
            lambda_init = 0.8 - 0.6 * math.exp(-0.3 * i)
            mix = _diff_mixer(h, diff_w_in[j], diff_lam_q1[j], diff_lam_k1[j], diff_lam_q2[j], diff_lam_k2[j],
                              diff_g_sub[j], diff_w_o[j], lambda_init)
        h = _layernorm(ALPHA * h + mix, ln_mix_g[i], ln_mix_b[i])
        h = _layernorm(ALPHA * h + _swiglu(h, ffn_w_gu[i], ffn_w_down[i]), ln_ffn_g[i], ln_ffn_b[i])
    return h


N_EVEN = (DEPTH + 1) // 2
N_ODD = DEPTH // 2

D_A = D_MODEL // 2
A_CONV = 3
D_B = D_MODEL // 2
POOL_WINDOWS = (2, 4, 8, 16)
POOL_GROUPS = len(POOL_WINDOWS)
POOL_GC = D_B // POOL_GROUPS
EV_IN = 3 * D_A + D_B
EV_MIX = D_A + D_B

D_C = D_MODEL // 2
HEAD_DIM = 64
H_C = D_C // HEAD_DIM
D_D = D_MODEL // 2
D_CONV = 31
OD_IN = 3 * D_C + H_C + 2 * D_D
OD_MIX = D_C + D_D

D_FF_2 = int(math.ceil((8 * D_MODEL / 3) / 256) * 256)

ALPHA_2 = (2.0 * DEPTH) ** 0.25
BETA_2 = (8.0 * DEPTH) ** -0.25


def layer_norm(x, g, b):
    x32 = x.astype(jnp.float32)
    mu = jnp.mean(x32, axis=-1, keepdims=True)
    var = jnp.mean(jnp.square(x32 - mu), axis=-1, keepdims=True)
    y = (x32 - mu) * lax.rsqrt(var + LN_EPS)
    return (y * g.astype(jnp.float32) + b.astype(jnp.float32)).astype(x.dtype)

def causal_dwconv(x, w):
    k = w.shape[0]
    return lax.conv_general_dilated(
        x, w[:, None, :].astype(x.dtype), window_strides=(1,), padding=[(k - 1, 0)],
        dimension_numbers=("NWC", "WIO", "NWC"), feature_group_count=x.shape[-1])

def short_gated_conv(p_a, conv_w):
    b_gate = p_a[..., :D_A]
    c_gate = p_a[..., D_A:2 * D_A]
    val = p_a[..., 2 * D_A:]
    return b_gate * causal_dwconv(c_gate * val, conv_w)

def multiscale_pool(u, w_grp, scale):
    bsz, s, _ = u.shape
    u32 = u.astype(jnp.float32).reshape(bsz, s, POOL_GROUPS, POOL_GC)
    cs = jnp.cumsum(u32, axis=1)
    pos = jnp.arange(s)
    pooled = []
    for g, win in enumerate(POOL_WINDOWS):
        c = cs[:, :, g]
        lagged = jnp.pad(c, ((0, 0), (win, 0), (0, 0)))[:, :s]
        cnt = jnp.minimum(pos + 1, win).astype(jnp.float32)[None, :, None]
        pooled.append((c - lagged) / cnt)
    pooled = (jnp.stack(pooled, axis=2) - u32).astype(u.dtype)
    y = jnp.einsum("bsgc,gcd->bsgd", pooled, w_grp).reshape(bsz, s, D_B)
    return y * scale

def forgetting_attention(q, k, v, log_f):
    s_len = q.shape[1]
    cum = jnp.cumsum(log_f.astype(jnp.float32), axis=1).transpose(0, 2, 1)
    scale = 1.0 / math.sqrt(HEAD_DIM)
    outs = []
    for blk in range(s_len // Q_BLOCK):
        q0, q1 = blk * Q_BLOCK, (blk + 1) * Q_BLOCK
        logits = jnp.einsum("bqhd,bkhd->bhqk", q[:, q0:q1], k[:, :q1]).astype(jnp.float32) * scale
        logits = logits + cum[:, :, q0:q1, None] - cum[:, :, None, :q1]
        mask = jnp.arange(q0, q1)[:, None] >= jnp.arange(q1)[None, :]
        logits = jnp.where(mask[None, None], logits, -1e30)
        probs = jax.nn.softmax(logits, axis=-1).astype(v.dtype)
        outs.append(jnp.einsum("bhqk,bkhd->bqhd", probs, v[:, :q1]))
    return jnp.concatenate(outs, axis=1)

def conformer_conv(p_d, dw_w, dw_b, cn_g, cn_b):
    h = p_d[..., :D_D] * jax.nn.sigmoid(p_d[..., D_D:])
    h = causal_dwconv(h, dw_w) + dw_b
    h = layer_norm(h, cn_g, cn_b)
    return jax.nn.silu(h)

def even_mixer(x, w_in, conv_w, pool_w, pool_scale, w_out):
    p = x @ w_in
    y_a = short_gated_conv(p[..., :3 * D_A], conv_w)
    y_b = multiscale_pool(p[..., 3 * D_A:], pool_w, pool_scale)
    return jnp.concatenate([y_a, y_b], axis=-1) @ w_out

def odd_mixer(x, w_in, forget_b, dw_w, dw_b, cn_g, cn_b, w_out):
    bsz, s, _ = x.shape
    p = x @ w_in
    q = p[..., :D_C].reshape(bsz, s, H_C, HEAD_DIM)
    k = p[..., D_C:2 * D_C].reshape(bsz, s, H_C, HEAD_DIM)
    v = p[..., 2 * D_C:3 * D_C].reshape(bsz, s, H_C, HEAD_DIM)
    log_f = jax.nn.log_sigmoid((p[..., 3 * D_C:3 * D_C + H_C] + forget_b).astype(jnp.float32))
    y_c = forgetting_attention(q, k, v, log_f).reshape(bsz, s, D_C)
    y_d = conformer_conv(p[..., 3 * D_C + H_C:], dw_w, dw_b, cn_g, cn_b)
    return jnp.concatenate([y_c, y_d], axis=-1) @ w_out

def swiglu(x, w_in, w_out):
    h = x @ w_in
    return (jax.nn.silu(h[..., :D_FF_2]) * h[..., D_FF_2:]) @ w_out

def second_inputs(seed: int = 0) -> dict:
    key = jax.random.key(seed)
    ks = jax.random.split(key, 24)
    f32 = jnp.float32
    nrm = lambda k, shape, s: jax.random.normal(k, shape, f32) * s
    x = jax.random.normal(ks[0], (BATCH, SEQ, D_MODEL), f32)
    ev_w_in = nrm(ks[1], (N_EVEN, D_MODEL, EV_IN), D_MODEL ** -0.5)
    ev_conv_w = nrm(ks[2], (N_EVEN, A_CONV, D_A), A_CONV ** -0.5)
    ev_pool_w = nrm(ks[3], (N_EVEN, POOL_GROUPS, POOL_GC, POOL_GC), POOL_GC ** -0.5)
    ev_pool_scale = 1.0 + nrm(ks[4], (N_EVEN, D_B), 0.1)
    ev_w_out = nrm(ks[5], (N_EVEN, EV_MIX, D_MODEL), EV_MIX ** -0.5 * BETA_2)
    col_scale = jnp.ones((OD_IN,), f32).at[2 * D_C:3 * D_C].set(BETA_2)
    od_w_in = nrm(ks[6], (N_ODD, D_MODEL, OD_IN), D_MODEL ** -0.5) * col_scale
    od_forget_b = jax.random.uniform(ks[7], (N_ODD, H_C), f32, 1.0, 4.0)
    od_dw_w = nrm(ks[8], (N_ODD, D_CONV, D_D), D_CONV ** -0.5)
    od_dw_b = nrm(ks[9], (N_ODD, D_D), 0.02)
    od_cn_g = 1.0 + nrm(ks[10], (N_ODD, D_D), 0.05)
    od_cn_b = nrm(ks[11], (N_ODD, D_D), 0.02)
    od_w_out = nrm(ks[12], (N_ODD, OD_MIX, D_MODEL), OD_MIX ** -0.5 * BETA_2)
    ln_mix_g = 1.0 + nrm(ks[13], (DEPTH, D_MODEL), 0.05)
    ln_mix_b = nrm(ks[14], (DEPTH, D_MODEL), 0.02)
    ln_ffn_g = 1.0 + nrm(ks[15], (DEPTH, D_MODEL), 0.05)
    ln_ffn_b = nrm(ks[16], (DEPTH, D_MODEL), 0.02)
    ffn_w_in = nrm(ks[17], (DEPTH, D_MODEL, 2 * D_FF_2), D_MODEL ** -0.5)
    ffn_w_out = nrm(ks[18], (DEPTH, D_FF_2, D_MODEL), D_FF_2 ** -0.5 * BETA_2)
    return {"x": x, "ev_w_in": ev_w_in, "ev_conv_w": ev_conv_w, "ev_pool_w": ev_pool_w,
            "ev_pool_scale": ev_pool_scale, "ev_w_out": ev_w_out, "od_w_in": od_w_in,
            "od_forget_b": od_forget_b, "od_dw_w": od_dw_w, "od_dw_b": od_dw_b,
            "od_cn_g": od_cn_g, "od_cn_b": od_cn_b, "od_w_out": od_w_out,
            "ln_mix_g": ln_mix_g, "ln_mix_b": ln_mix_b, "ln_ffn_g": ln_ffn_g,
            "ln_ffn_b": ln_ffn_b, "ffn_w_in": ffn_w_in, "ffn_w_out": ffn_w_out}

def second_block(x, ev_w_in, ev_conv_w, ev_pool_w, ev_pool_scale, ev_w_out, od_w_in,
              od_forget_b, od_dw_w, od_dw_b, od_cn_g, od_cn_b, od_w_out,
              ln_mix_g, ln_mix_b, ln_ffn_g, ln_ffn_b, ffn_w_in, ffn_w_out):
    for layer in range(DEPTH):
        i = layer // 2
        if layer % 2 == 0:
            mix = even_mixer(x, ev_w_in[i], ev_conv_w[i], ev_pool_w[i], ev_pool_scale[i], ev_w_out[i])
        else:
            mix = odd_mixer(x, od_w_in[i], od_forget_b[i], od_dw_w[i], od_dw_b[i],
                            od_cn_g[i], od_cn_b[i], od_w_out[i])
        x = layer_norm(ALPHA_2 * x + mix, ln_mix_g[layer], ln_mix_b[layer])
        x = layer_norm(ALPHA_2 * x + swiglu(x, ffn_w_in[layer], ffn_w_out[layer]),
                       ln_ffn_g[layer], ln_ffn_b[layer])
    return x


def setup_inputs(seed=0):
    out = dict(first_inputs(seed))
    for name, value in second_inputs(seed + 1).items():
        if name != "x":
            out[name + "_2"] = value
    return out


def reference(
    x, mla_w_in, mla_g_q, mla_g_kv, mla_w_uq, mla_w_ukv, mla_w_o, diff_w_in, diff_lam_q1,
    diff_lam_k1, diff_lam_q2, diff_lam_k2, diff_g_sub, diff_w_o, ln_mix_g, ln_mix_b, ffn_w_gu,
    ffn_w_down, ln_ffn_g, ln_ffn_b, ev_w_in_2, ev_conv_w_2, ev_pool_w_2, ev_pool_scale_2,
    ev_w_out_2, od_w_in_2, od_forget_b_2, od_dw_w_2, od_dw_b_2, od_cn_g_2, od_cn_b_2,
    od_w_out_2, ln_mix_g_2, ln_mix_b_2, ln_ffn_g_2, ln_ffn_b_2, ffn_w_in_2, ffn_w_out_2,
):
    x = first_block(
        x, mla_w_in, mla_g_q, mla_g_kv, mla_w_uq, mla_w_ukv, mla_w_o, diff_w_in, diff_lam_q1,
        diff_lam_k1, diff_lam_q2, diff_lam_k2, diff_g_sub, diff_w_o, ln_mix_g, ln_mix_b,
        ffn_w_gu, ffn_w_down, ln_ffn_g, ln_ffn_b,
    )
    return second_block(
        x, ev_w_in_2, ev_conv_w_2, ev_pool_w_2, ev_pool_scale_2, ev_w_out_2, od_w_in_2,
        od_forget_b_2, od_dw_w_2, od_dw_b_2, od_cn_g_2, od_cn_b_2, od_w_out_2, ln_mix_g_2,
        ln_mix_b_2, ln_ffn_g_2, ln_ffn_b_2, ffn_w_in_2, ffn_w_out_2,
    )


_drawn_inputs = setup_inputs


def setup_inputs(seed=0):
    import zlib

    import numpy as np

    out = dict(_drawn_inputs(seed))
    spreads = {}
    factors = {'mla_g_q': 8.0,
     'mla_g_kv': 8.0,
     'diff_lam_k1': 8.0,
     'diff_lam_q2': 8.0,
     'diff_g_sub': 23.6,
     'od_forget_b_2': 39.016,
     'od_dw_b_2': 8.0,
     'od_cn_g_2': 6.058,
     'od_cn_b_2': 8.0,
     'ev_pool_scale_2': 3.378}
    for name, (base, spread) in spreads.items():
        noise = np.random.default_rng([zlib.crc32(name.encode()), seed]).standard_normal(out[name].shape)
        drawn = base * np.exp(spread * noise) if base else spread * noise
        out[name] = __import__('jax').numpy.asarray(drawn.astype(out[name].dtype))
    for name, factor in factors.items():
        out[name] = (out[name] * factor).astype(out[name].dtype)
    return out
```

```python
import math
from contextlib import ExitStack, contextmanager

import concourse.bass as bass
import numpy as np
from concourse import mybir

F32 = mybir.dt.float32
F32R = mybir.dt.float32r
ALU = mybir.AluOpType
ACT = mybir.ActivationFunctionType

P = 128
S = 512
NB = S // P
D = 1024
KD = D // P
D_FF = 2816
HID = (12, 10)
QR, KVR = 384, 256
ROPE, NOPE = 64, 128
SLOT = 3072
ALPHA = 4.0 ** 0.25
LN_EPS, RMS_EPS = 1e-5, 1e-6
NEG = -1e30
BIG = 3.0e38
MLA_SCALE = (NOPE + ROPE) ** -0.5
HD_SCALE = 64 ** -0.5
LAMBDA_INIT = 0.8 - 0.6 * math.exp(-0.3)
TAPS = 31
WINDOWS = (2, 4, 8, 16)
PADC, PADW = TAPS - 1, 16

PCOL, _n = {}, 0
for _name, _w in (("ln_g", 64), ("ln_b", 64), ("g_c", 5), ("g_sub", 1), ("conv_w", 12), ("pool_s", 4),
                  ("dw_w", 4 * TAPS), ("dw_b", 4), ("cn_g", 4), ("cn_b", 4), ("lam", 4), ("f_b", 1)):
    PCOL[_name] = _n
    _n += _w
NPAR = _n
CCOL, _n = {}, 0
for _name, _w in (("ident", P), ("dist", S), ("causal", P), ("invcnt", 64), ("slopes", 8)):
    CCOL[_name] = _n
    _n += _w
NCON = _n
RCOL = {"cos": 0, "sin": S, "mask": 2 * S}

OUT3 = (3072, 3072, 2048)
STREAM = (
    ("mla_in", (3072, 3072, 1024)), ("mla_pair", (2560,) * 4), ("mla_o", OUT3), ("ffn0", None),
    ("diff_in", (3072,) * 8), ("diff_o", OUT3), ("ffn1", None),
    ("ev_in", (2048,) * 8), ("ev_pool", (512,)), ("ev_o", OUT3), ("ffn2", None),
    ("od_f", (1024,)), ("od_conv", (2048,) * 4), ("od_in", (3072,) * 4), ("od_o", OUT3), ("ffn3", None),
)
SRC_BEFORE_LAST = 7 * KD + 5 + KD + 4
STEPS = [(t, k) for t in range(3) for k in range(KD)]
DIFF_SLOTS = (STEPS[0:5], STEPS[5:10], STEPS[10:15], STEPS[15:20], STEPS[20:24])
ODD_SLOTS = (STEPS[0:3], STEPS[3:6], STEPS[6:9], STEPS[9:12], STEPS[12:15], [], STEPS[15:18], STEPS[18:21], STEPS[21:24])
MLA_K = (3, 3, 3, 3, 2, 2, 2, 2)
MLA_SLOTS = tuple([(t, k) for k in range(MLA_K[t])] if t is not None else [] for t in (0, 1, 2, 3, 4, None, 5, 6, 7))


def finished(slot, depth):
    return [t for t, k in slot if k == depth[t] - 1]


class Count:

    def __init__(self):
        self.n, self.reg, self.slope = 0, None, 0

    def at(self, d=0):
        v = self.n + d
        return v if self.reg is None else self.reg * self.slope + v

    def add(self, k=1):
        self.n += k


@contextmanager
def counted_loop(eng, trips, slopes):
    start = {c: c.n for c in slopes}
    with eng.Fori(0, trips) as it:
        for c, k in slopes.items():
            c.reg, c.slope = it, k
        yield it
    for c, k in slopes.items():
        assert c.n - start[c] == k, (c.n - start[c], k)
        c.n, c.reg = start[c] + trips * k, None


def build(nc, xT, par, con, rcon, w, outT):
    ctx = ExitStack()
    with ctx:
        def sb(name, shape, dt=F32, stack=ctx):
            return stack.enter_context(nc.sbuf_tensor(name, shape, dt))

        def sem(name):
            return ctx.enter_context(nc.semaphore(name))

        raw = [sb(f"raw{i}", [P, SLOT]) for i in range(2)]
        whi = [sb(f"whi{i}", [P, SLOT], F32R) for i in range(2)]
        wlo = [sb(f"wlo{i}", [P, SLOT], F32R) for i in range(2)]
        X = sb("X", [P, KD, S])
        XH = sb("XH", [P, KD, S], F32R)
        XL = sb("XL", [P, KD, S], F32R)
        parm = sb("parm", [P, NPAR])
        cons = sb("cons", [P, NCON])
        ones = sb("ones", [P, P])
        eps_ln = sb("eps_ln", [P, 1])
        eps_rms = sb("eps_rms", [P, 1])
        sq = [sb(f"sq{i}", [P, S]) for i in range(2)]
        rstd = sb("rstd", [P, S])
        gsub = sb("gsub", [P, 1])
        lam = sb("lam", [P, 8])
        spare = sb("spare", [1, 8])
        ident = cons[:, CCOL["ident"]:CCOL["ident"] + P]
        dist = cons[:, CCOL["dist"]:CCOL["dist"] + S]
        causal = cons[:, CCOL["causal"]:CCOL["causal"] + P]

        def pcol(name, i=0):
            return parm[:, PCOL[name] + i:PCOL[name] + i + 1]

        st = ExitStack()
        HH = sb("HH", [P, HID[0], S], F32R, st)
        HL = sb("HL", [P, HID[0], S], F32R, st)
        sil = [sb(f"sil{i}", [P, S], F32, st) for i in range(2)]
        hf = [sb(f"hf{i}", [P, S], F32, st) for i in range(2)]
        st.close()

        def attention_buffers(st, tag, maps, y, pt=1):
            a = {}
            a["L"] = [[sb(f"{tag}L{i}{m}", [P, S], F32, st) for m in range(maps)] for i in range(2)]
            a["negmax"] = sb(f"{tag}negmax", [P, 4], F32, st)
            a["rowsum"] = sb(f"{tag}rowsum", [P, 4], F32, st)
            a["rinv"] = sb(f"{tag}rinv", [P, 4], F32, st)
            a["PT"] = sb(f"{tag}PT", [P, NB, S], F32, st)
            if y:
                a["Y"] = sb(f"{tag}Y", [P, KD, S], F32, st)
            return a

        st = ExitStack()
        ML = attention_buffers(st, "m", 1, False)
        rtab = sb("rtab", [P, 3 * S], F32, st)
        CH = sb("CH", [P, 5, S], F32R, st)
        CL = sb("CL", [P, 5, S], F32R, st)
        KR = sb("KR", [P, S], F32, st)
        rt = sb("rt", [P, S], F32, st)
        cf_stack = ExitStack()
        Cf = sb("Cf", [P, 5, S], F32, cf_stack)
        cf_stack.close()
        mQN = [[sb(f"mQN{i}{m}", [P, S], F32, st) for m in range(2)] for i in range(2)]
        mKN = [[sb(f"mKN{i}{m}", [P, S], F32, st) for m in range(2)] for i in range(2)]
        mQR = [sb(f"mQR{i}", [P, S], F32, st) for i in range(2)]
        mV = [[sb(f"mV{i}{m}", [P, NB, P], F32, st) for m in range(2)] for i in range(2)]
        mVT = [sb(f"mVT{m}", [P, S], F32, st) for m in range(2)]
        st.close()

        st = ExitStack()
        DF = attention_buffers(st, "d", 2, True)
        dQ = [sb(f"dQ{i}", [P, S], F32, st) for i in range(2)]
        dK = [sb(f"dK{i}", [P, S], F32, st) for i in range(2)]
        dV = [sb(f"dV{i}", [P, NB, P], F32, st) for i in range(2)]
        dVT = sb("dVT", [P, S], F32, st)
        dB = sb("dB", [P, S], F32, st)
        dO = [sb(f"dO{i}", [P, S], F32, st) for i in range(2)]
        dms = sb("dms", [P, S], F32, st)
        st.close()

        st = ExitStack()
        EY = sb("EY", [P, KD, S], F32, st)
        ec = sb("ec", [P, S], F32, st)
        ez = sb("ez", [P, 2 + S], F32, st)
        eu = [sb(f"eu{i}", [P, PADW + S], F32, st) for i in range(3)]
        EP = sb("EP", [P, 4, S], F32, st)
        EPH = sb("EPH", [P, 4, S], F32R, st)
        EPL = sb("EPL", [P, 4, S], F32R, st)
        st.close()

        st = ExitStack()
        lf_stack = ExitStack()
        lfz, lfa, lfe, lfu, lfl, lfd, lfi, lfr = (sb(f"lf{n}", [8, S], F32, lf_stack) for n in "zaeuldir")
        lf_stack.close()
        FO = attention_buffers(st, "f", 1, True)
        fQ = [sb(f"fQ{i}", [P, S], F32, st) for i in range(2)]
        fK = [sb(f"fK{i}", [P, S], F32, st) for i in range(2)]
        fV = [sb(f"fV{i}", [P, NB, P], F32, st) for i in range(2)]
        fVT = sb("fVT", [P, S], F32, st)
        fB = [sb(f"fB{m}", [P, S], F32, st) for m in range(2)]
        fBD = [sb(f"fBD{m}", [P, NB, P], F32, st) for m in range(2)]
        fz = [sb(f"fz{i}", [P, PADC + S], F32, st) for i in range(4)]
        fsig = sb("fsig", [P, S], F32, st)
        cum = sb("cum", [8, S], F32, st)
        st.close()

        bank = [ctx.enter_context(nc.psum_tensor(f"bank{i}", [P, S], F32)) for i in range(8)]

        x_in = sem("x_in")
        raw_ready = [sem(f"raw_ready{i}") for i in range(2)]
        hi_ready = sem("hi_ready")
        lo_ready = sem("lo_ready")
        w_used = sem("w_used")
        tile_done = sem("tile_done")
        tile_free = sem("tile_free")
        gate_done = sem("gate_done")
        aux_done = sem("aux_done")
        aux_free = sem("aux_free")
        exp_done = sem("exp_done")
        p_ready = sem("p_ready")
        src_ready = sem("src_ready")
        act_hi = sem("act_hi")
        act_lo = sem("act_lo")
        sum_ready = sem("sum_ready")
        dev_ready = sem("dev_ready")
        sq_ready = sem("sq_ready")
        sq_used = sem("sq_used")
        std_ready = sem("std_ready")
        rope_ready = sem("rope_ready")
        cum_ready = sem("cum_ready")
        stat_done = sem("stat_done")
        ms_ready = sem("ms_ready")
        mem_ready = sem("mem_ready")
        small_dve = sem("small_dve")
        small_act = sem("small_act")
        small_pe = sem("small_pe")
        step = sem("step")
        stored = sem("stored")

        block = ctx.enter_context(nc.Block())

        @block.sync
        def _(sp):
            sp.dma_start(X[:], xT.rearrange("t p n -> p t n")).then_inc(x_in, 16)
            sp.dma_start(parm[:], par).then_inc(x_in, 16)
            sp.dma_start(cons[:], con).then_inc(x_in, 16)
            sp.dma_start(rtab[:], rcon).then_inc(x_in, 16)
            unit = Count()

            def load(src, size):
                s = unit.n % 2
                if unit.n >= 2:
                    sp.wait_ge(lo_ready, unit.at(-1))
                sp.dma_start(raw[s][:, 0:size], src).then_inc(raw_ready[s], 16)
                unit.add()

            def load_all(name, n, size, i0=0):
                with counted_loop(sp, n // 2, {unit: 2}) as it:
                    for j in range(2):
                        load(w[name][bass.ds(it * 2 + (i0 + j), 1), :, 0:size].rearrange("o p n -> (o p) n"), size)

            for name, sizes in STREAM:
                if sizes is None:
                    for half in range(2):
                        load_all(name + "_gu", HID[half], 2048, HID[0] * half)
                        load_all(f"{name}_d{half}", 4, 256 * HID[half])
                elif len(sizes) == 8:
                    load_all(name, 8, sizes[0])
                else:
                    for i, size in enumerate(sizes):
                        load(w[name][i, :, 0:size], size)
            for j in range(KD):
                sp.wait_ge(src_ready, SRC_BEFORE_LAST + j + 1)
                sp.dma_start(outT[j], X[:, j, :]).then_inc(stored, 16)
            sp.wait_ge(stored, 16 * KD)

        @block.scalar
        def _(act):
            unit, tiles, srcs, sqs, auxf, gates, devs, small, mss = (Count() for _ in range(9))

            def split_w(size):
                s = unit.n % 2
                arrived = unit.n // 2 * 16 + 16
                if unit.reg is not None:
                    arrived = unit.reg * 16 + arrived
                act.wait_ge(raw_ready[s], arrived)
                if unit.n >= 2:
                    act.wait_ge(w_used, unit.at(-1))
                act.copy(whi[s][:, 0:size], raw[s][:, 0:size]).then_inc(hi_ready, 1)
                unit.add()

            def split_x(dst, src):
                act.wait_ge(src_ready, srcs.at(1))
                act.copy(dst, src).then_inc(act_hi, 1)
                srcs.add()

            def split_at(dst, src, sem_, value):
                act.wait_ge(sem_, value)
                act.copy(dst, src).then_inc(act_hi, 1)

            def square(src, sem_, value):
                act.wait_ge(sem_, value)
                if sqs.n >= 2:
                    act.wait_ge(sq_used, sqs.at(-1))
                act.activation(sq[sqs.n % 2][:], src, ACT.Square).then_inc(sq_ready, 1)
                sqs.add()

            def std(src, scale, eps, n_sq):
                act.wait_ge(sq_used, n_sq)
                act.activation(rstd[:], src, ACT.Sqrt, bias=eps[:], scale=scale).then_inc(std_ready, 1)

            def layer_norm(split=True):
                for j in range(KD):
                    square(X[:, j, :], dev_ready, devs.at(1))
                    devs.add()
                std(bank[7][:], 1.0 / D, eps_ln, sqs.n)
                for j in range(KD if split else 0):
                    split_x(XH[:, j, :], X[:, j, :])

            def ffn(next_size):
                for half in range(2):
                    n = HID[half]

                    def gu_unit(size, hidden):
                        split_w(size)
                        i = gates.n % 2
                        act.wait_ge(tile_done, tiles.at(1))
                        if gates.n >= 2:
                            act.wait_ge(tile_free, tiles.at(-2))
                        act.activation(sil[i][:], bank[2 * i][:], ACT.Silu).then_inc(gate_done, 1)
                        gates.add()
                        tiles.add(2)
                        act.wait_ge(tile_free, tiles.at())
                        act.copy(hidden, hf[i][:]).then_inc(act_hi, 1)

                    with counted_loop(act, (n - 2) // 2, {unit: 2, gates: 2, tiles: 4}) as it:
                        for j in range(2):
                            gu_unit(2048, HH[:, bass.ds(it * 2 + j, 1), :].rearrange("p o n -> p (o n)"))
                    for j in range(n - 2, n):
                        gu_unit(2048 if j < n - 1 else 256 * n, HH[:, j, :])
                    for u in range(4):
                        if u < 3:
                            split_w(256 * n)
                        elif half == 0:
                            split_w(2048)
                        elif next_size:
                            split_w(next_size)
                        tiles.add(2)

            def out_projection(next_size):
                for size in (OUT3[1], OUT3[2], next_size):
                    split_w(size)
                tiles.add(8)

            act.wait_ge(x_in, 64)
            for j in range(KD):
                act.copy(XH[:, j, :], X[:, j, :]).then_inc(act_hi, 1)
            act.wait_ge(small_pe, 1)
            act.activation(lam[:, 4:6], bank[4][:, 0:2], ACT.Exp).then_inc(small_act, 1)
            small.add()

            split_w(3072)
            split_w(3072)
            for j in range(3):
                square(Cf[:, j, :], tile_free, j + 1)
            split_w(1024)
            for j in range(3, 5):
                square(Cf[:, j, :], tile_free, j + 1)
            std(bank[6][:], 1.0 / QR, eps_rms, 3)
            for j in range(3):
                split_x(CH[:, j, :], Cf[:, j, :])
            std(bank[7][:], 1.0 / KVR, eps_rms, 5)
            split_w(2560)
            for j in range(3, 5):
                split_x(CH[:, j, :], Cf[:, j, :])
            tiles.add(7)

            def exp_rows(A, i, m, qb, col):
                act.wait_ge(aux_free, auxf.at(1))
                row = A["L"][i][m][:, 0:(qb + 1) * P]
                act.activation(row, row, ACT.Exp, bias=A["negmax"][:, col:col + 1], scale=-1.0,
                               accum_out=A["rowsum"][:, col:col + 1]).then_inc(exp_done, 1)
                auxf.add()

            split_w(2560)
            tiles.add(8)
            auxf.add(2)
            for p in range(4):
                for j in range(8):
                    exp_rows(ML, j % 2, 0, j % 4, j % 2)
                    if j == 1 and p < 3:
                        split_w(2560 if p < 2 else OUT3[0])
                    if j == 5:
                        auxf.add()
                        split_at(XH[:, 2 * p, :], sq[0][:], aux_free, auxf.at())
                    if j > 0:
                        auxf.add()
                auxf.add()
                if p < 3:
                    auxf.add(2)
                    tiles.add(8)
                auxf.add()
                split_at(XH[:, 2 * p + 1, :], sq[1][:], aux_free, auxf.at())
            out_projection(2048)
            layer_norm()
            ffn(3072)
            layer_norm()

            split_w(3072)
            tiles.add(3)
            auxf.add()

            def inverse_root():
                mss.add()
                act.wait_ge(ms_ready, mss.at())
                act.activation(dms[:], dms[:], ACT.Ln).then_inc(small_act, 1)
                small.add()
                act.wait_ge(small_act, small.at())
                act.activation(dms[:], dms[:], ACT.Exp, scale=-0.5).then_inc(std_ready, 1)

            def diff_head(s, first, last):
                for j in range(4):
                    for m in range(2):
                        exp_rows(DF, j % 2, m, j, 2 * (j % 2) + m)
                    if j == 0 and not last:
                        split_w(3072)
                    if j > 0:
                        auxf.add()
                    if j == 1 and not first:
                        inverse_root()
                auxf.add()
                if not last:
                    auxf.add()
                    tiles.add(3)
                auxf.add()
                square(dO[s][:], aux_free, auxf.at())

            diff_head(0, True, False)
            with counted_loop(act, 3, {unit: 2, tiles: 6, auxf: 28, small: 2, sqs: 2, mss: 2}):
                diff_head(1, False, False)
                diff_head(0, False, False)
            diff_head(1, False, True)
            inverse_root()
            for j in range(KD):
                split_x(XH[:, j, :], DF["Y"][:, j, :])
            out_projection(2048)
            layer_norm()
            ffn(2048)
            layer_norm()

            for u in range(8):
                split_w(2048 if u < 7 else 512)
                tiles.add(2)
            for j in range(4):
                split_x(EPH[:, j, :], EP[:, j, :])
            for j in range(4):
                split_at(XH[:, j, :], EY[:, j, :], tile_free, tiles.at())
            split_w(OUT3[0])
            for j in range(4):
                split_at(XH[:, 4 + j, :], EY[:, 4 + j, :], tile_free, tiles.at(j + 1))
            tiles.add(4)
            out_projection(2048)
            layer_norm()
            ffn(1024)
            layer_norm()

            split_w(2048)
            tiles.add(1)
            act.wait_ge(tile_free, tiles.at())
            act.activation(lfa[:], lfz[:], ACT.Abs).then_inc(small_act, 1)
            small.add()
            act.wait_ge(small_act, small.at())
            act.activation(lfe[:], lfa[:], ACT.Exp, scale=-1.0).then_inc(small_act, 1)
            act.wait_ge(small_dve, 2)
            act.activation(lfl[:], lfu[:], ACT.Ln).then_inc(small_act, 1)
            small.add(2)
            for i in range(4):
                split_w(2048 if i < 3 else 3072)
                act.wait_ge(tile_done, tiles.at(2))
                if i:
                    act.wait_ge(tile_free, tiles.at())
                act.activation(fsig[:], bank[(2 * i + 1) % 4][:], ACT.Sigmoid).then_inc(gate_done, 1)
                gates.add()
                tiles.add(2)
            split_w(3072)
            tiles.add(3)
            auxf.add()
            for g in range(4):
                auxf.add(2)
                for j in range(8):
                    exp_rows(FO, j % 2, 0, j % 4, j % 2)
                    if j == 1 and g < 3:
                        split_w(3072)
                    if j == 5:
                        auxf.add()
                    if j > 0:
                        auxf.add()
                auxf.add()
                if g < 3:
                    auxf.add()
                    tiles.add(3)
                auxf.add()
            for i in range(4):
                square(FO["Y"][:, 4 + i, :], dev_ready, devs.at(1))
                devs.add()
            std(bank[7][:], 1.0 / (D // 2), eps_ln, sqs.n)
            for i in range(4):
                split_at(XH[:, i, :], FO["Y"][:, i, :], aux_free, auxf.at())
            for i in range(4):
                act.wait_ge(small_dve, 3 + i)
                act.activation(FO["Y"][:, 4 + i, :], FO["Y"][:, 4 + i, :], ACT.Silu).then_inc(small_act, 1)
                small.add()
                split_at(XH[:, 4 + i, :], FO["Y"][:, 4 + i, :], small_act, small.at())
            out_projection(2048)
            layer_norm()
            ffn(0)
            layer_norm(split=False)

        @block.gpsimd
        def _(pool):
            unit, his = Count(), Count()

            def split_w(size):
                s = unit.n % 2
                pool.wait_ge(hi_ready, unit.at(1))
                pool.tensor_tensor(wlo[s][:, 0:size], raw[s][:, 0:size], whi[s][:, 0:size].bitcast(F32),
                                   ALU.subtract).then_inc(lo_ready, 1)
                unit.add()

            def split_x(dst, src, hi):
                pool.wait_ge(act_hi, his.at(1))
                pool.tensor_tensor(dst, src, hi.bitcast(F32), ALU.subtract).then_inc(act_lo, 1)
                his.add()

            def split_state():
                for j in range(KD):
                    split_x(XL[:, j, :], X[:, j, :], XH[:, j, :])

            def ffn(next_size):
                for half in range(2):
                    n = HID[half]
                    with counted_loop(pool, (n - 2) // 2, {unit: 2, his: 2}) as it:
                        for j in range(2):
                            split_w(2048)
                            t = bass.ds(j + it * 2, 1)
                            split_x(HL[:, t, :].rearrange("p o n -> p (o n)"), hf[j][:],
                                    HH[:, t, :].rearrange("p o n -> p (o n)"))
                    for j in range(n - 2, n):
                        split_w(2048 if j < n - 1 else 256 * n)
                        split_x(HL[:, j, :], hf[j % 2][:], HH[:, j, :])
                    for u in range(4):
                        if u < 3:
                            split_w(256 * n)
                        elif half == 0:
                            split_w(2048)
                        elif next_size:
                            split_w(next_size)

            pool.memset(ones[:], 1.0)
            pool.memset(eps_ln[:], LN_EPS)
            pool.memset(eps_rms[:], RMS_EPS).then_inc(mem_ready, 1)
            pool.wait_ge(x_in, 64)
            split_state()
            split_w(3072)
            split_w(3072)
            split_w(1024)
            for j in range(3):
                split_x(CL[:, j, :], Cf[:, j, :], CH[:, j, :])
            split_w(2560)
            for j in range(3, 5):
                split_x(CL[:, j, :], Cf[:, j, :], CH[:, j, :])
            split_w(2560)
            for p in range(4):
                if p < 3:
                    split_w(2560 if p < 2 else OUT3[0])
                for m in range(2):
                    split_x(XL[:, 2 * p + m, :], sq[m][:], XH[:, 2 * p + m, :])

            def out_projection(next_size):
                for size in (OUT3[1], OUT3[2], next_size):
                    split_w(size)

            out_projection(2048)
            split_state()
            ffn(3072)
            split_state()
            split_w(3072)
            split_w(3072)
            with counted_loop(pool, 3, {unit: 2}) as it:
                split_w(3072)
                split_w(3072)
            for j in range(KD):
                split_x(XL[:, j, :], DF["Y"][:, j, :], XH[:, j, :])
            out_projection(2048)
            split_state()
            ffn(2048)
            split_state()
            for u in range(8):
                split_w(2048 if u < 7 else 512)
            for j in range(4):
                split_x(EPL[:, j, :], EP[:, j, :], EPH[:, j, :])
            for j in range(KD):
                if j == 4:
                    split_w(OUT3[0])
                split_x(XL[:, j, :], EY[:, j, :], XH[:, j, :])
            out_projection(2048)
            split_state()
            ffn(1024)
            split_state()
            split_w(2048)
            for i in range(4):
                split_w(2048 if i < 3 else 3072)
            split_w(3072)
            for g in range(3):
                split_w(3072)
            for j in range(KD):
                split_x(XL[:, j, :], FO["Y"][:, j, :], XH[:, j, :])
            out_projection(2048)
            split_state()
            ffn(0)

        @block.tensor
        def _(pe):
            unit, tiles, los, aux, sqs, norms, gates, probs = (Count() for _ in range(8))
            last = {b: 0 for b in range(4, 8)}
            fresh = [False]

            def begin_unit():
                pe.wait_ge(lo_ready, unit.at(1))
                s = unit.n % 2
                fresh[0] = unit.n > 0
                unit.add()
                return s

            def product(out, s, off, xh, xl, start, stop):
                ins = pe.matmul(out, whi[s][:, off:off + P], xh, start=start, stop=False)
                if fresh[0]:
                    ins.then_inc(w_used, 1)
                    fresh[0] = False
                pe.matmul(out, whi[s][:, off:off + P], xl, start=False, stop=False)
                return pe.matmul(out, wlo[s][:, off:off + P], xh, start=False, stop=stop)

            def claim(lag):
                if tiles.n >= lag:
                    pe.wait_ge(tile_free, tiles.at(1 - lag))

            def tile(s, b, offs, xh, xl, lag=4, wait_x=False):
                claim(lag)
                for k, off in enumerate(offs):
                    if wait_x:
                        pe.wait_ge(act_lo, los.at(k + 1))
                    ins = product(bank[b][:], s, off, xh[:, k, :], xl[:, k, :], k == 0, k == len(offs) - 1)
                ins.then_inc(tile_done, 1)
                tiles.add()

            def tiles_together(s, nt, xh, xl, depth):
                pe.wait_ge(tile_free, tiles.at())
                for k in range(depth):
                    pe.wait_ge(act_lo, los.at(k + 1))
                    for t in range(nt):
                        ins = product(bank[t][:], s, (k * nt + t) * P, xh[:, k, :], xl[:, k, :], k == 0, k == depth - 1)
                        if k == depth - 1:
                            ins.then_inc(tile_done, 1)
                tiles.add(nt)

            def unit_tiles(nt, b0, xh=XH, xl=XL, depth=KD):
                s = begin_unit()
                for t in range(nt):
                    tile(s, (b0 + t) % 4, [(k * nt + t) * P for k in range(depth)], xh, xl)

            def out_projection():
                s = begin_unit()
                tiles_together(s, 3, XH, XL, KD)
                los.add(KD)
                unit_tiles(3, 3)
                unit_tiles(2, 2)

            def layer_norm():
                pe.wait_ge(sum_ready, norms.at(1))
                pe.matmul(bank[6][:], ones[:], rstd[:], start=True, stop=True).then_inc(stat_done, 1)
                norms.add()
                sum_squares(7, KD)

            def sum_squares(b, n):
                for j in range(n):
                    pe.wait_ge(sq_ready, sqs.at(1))
                    pe.matmul(bank[b][:], ones[:], sq[sqs.n % 2][:], start=j == 0, stop=j == n - 1).then_inc(sq_used, 1)
                    sqs.add()

            def ffn():
                for half in range(2):
                    n = HID[half]
                    if half == 0:
                        s = begin_unit()
                        tiles_together(s, 2, XH, XL, KD)
                        los.add(KD)
                        unit_tiles(2, 2)
                        trips = (n - 2) // 2
                    else:
                        trips = n // 2
                    with counted_loop(pe, trips, {unit: 2, tiles: 4}):
                        unit_tiles(2, 0)
                        unit_tiles(2, 2)
                    with counted_loop(pe, 2, {unit: 2, tiles: 4}):
                        for j in range(2):
                            s = begin_unit()
                            for t in range(2):
                                tile(s, 2 * j + t, [(k * 2 + t) * P for k in range(n)], HH, HL, wait_x=(j, t) == (0, 0))
                    los.add(n)

            def aux_claim(b):
                if last[b] > 0:
                    pe.wait_ge(aux_free, aux.at(last[b] - aux.n))

            def aux_end(ins, b):
                ins.then_inc(aux_done, 1)
                aux.add()
                last[b] = aux.n

            def transposes(dst_bank, src, n, ready, value):
                pe.wait_ge(ready, value)
                aux_claim(dst_bank)
                for b in range(n):
                    ins = pe.transpose(bank[dst_bank][:, b * P:(b + 1) * P], src[:, b * P:(b + 1) * P], ident)
                aux_end(ins, dst_bank)

            def steps(s, slot, depth, offset, xh, xl, banks, lag, xbase=None):
                for t, k in slot:
                    if k == 0:
                        claim(lag)
                    kx = k + (xbase[t] if xbase else 0)
                    ins = product(bank[banks[t]][:], s, offset(t, k), xh[:, kx, :], xl[:, kx, :], k == 0, k == depth[t] - 1)
                    if k == depth[t] - 1:
                        ins.then_inc(tile_done, 1)
                        tiles.add()

            def value_product(A, v, rows, cols, behind):
                pe.wait_ge(aux_free, aux.at(-behind))
                aux_claim(7)
                for kb in range(NB):
                    ins = pe.matmul(bank[7][rows, kb * P:S], v[:, kb, cols], A["PT"][:, kb, kb * P:S],
                                    start=kb == 0, stop=kb == NB - 1)
                aux_end(ins, 7)

            pe.wait_ge(mem_ready, 1)
            pe.wait_ge(small_dve, 1)
            pe.matmul(bank[4][:, 0:2], ones[:], lam[:, 0:2], start=True, stop=True).then_inc(small_pe, 1)

            s = begin_unit()
            tiles_together(s, 3, XH, XL, KD)
            los.add(KD)
            s = begin_unit()
            for t in range(3):
                tile(s, (3, 0, 1)[t], [(k * 3 + t) * P for k in range(KD)], XH, XL)
            sum_squares(6, 3)
            s = begin_unit()
            tile(s, 2, [k * P for k in range(KD)], XH, XL)
            sum_squares(7, 2)
            pe.wait_ge(act_lo, los.at(5))
            los.add(5)

            def mla_offset(t, k):
                return k * 4 * P + t * P if t < 4 else 3 * 4 * P + k * 4 * P + (t - 4) * P

            def mla_steps(s, slot):
                steps(s, slot, MLA_K, mla_offset, CH, CL, (0, 1, 2, 3, 0, 1, 2, 3), 4, (0, 0, 0, 0, 3, 3, 3, 3))

            def mla_values():
                transposes(6, mVT[0], NB, tile_free, tiles.at(-2))
                transposes(6, mVT[1], NB, tile_free, tiles.at())

            pe.wait_ge(tile_free, tiles.at())
            s = begin_unit()
            for slot in MLA_SLOTS:
                mla_steps(s, slot)
            mla_values()
            for p in range(4):
                i = p % 2
                pe.wait_ge(tile_free, tiles.at())
                pe.wait_ge(rope_ready, p + 2)
                if p < 3:
                    s = begin_unit()
                for j in range(8):
                    m, qb = j // 4, j % 4
                    b, n = 4 + j % 2, (qb + 1) * P
                    aux_claim(b)
                    pe.matmul(bank[b][:, 0:n], mQN[i][m][:, qb * P:n], mKN[i][m][:, 0:n], start=True, stop=False)
                    half = slice(64 * m, 64 * m + 64)
                    aux_end(pe.matmul(bank[b][:, 0:n], mQR[i][half, qb * P:n], KR[half, 0:n], start=False, stop=True), b)
                    if p < 3:
                        mla_steps(s, MLA_SLOTS[j])
                    if j == 5:
                        value_product(ML, mV[i][0], slice(0, P), slice(0, P), 1)
                    if j > 0:
                        probs.add()
                        transposes(6, ML["L"][(j - 1) % 2][0], (j - 1) % 4 + 1, p_ready, probs.at())
                if p < 3:
                    mla_steps(s, MLA_SLOTS[8])
                probs.add()
                transposes(6, ML["L"][1][0], NB, p_ready, probs.at())
                if p < 3:
                    mla_values()
                value_product(ML, mV[i][1], slice(0, P), slice(0, P), 2 if p < 3 else 0)
            out_projection()
            layer_norm()
            ffn()
            layer_norm()

            def head_offset(t, k):
                return (k * 3 + t) * P

            def head_steps(s, slot):
                steps(s, slot, (KD,) * 3, head_offset, XH, XL, (0, 1, 2), 3)

            def diff_head(i, first, last_one):
                pe.wait_ge(tile_free, tiles.at())
                if not first:
                    last.update({4: aux.n - 5, 5: aux.n - 4, 6: aux.n - 1, 7: aux.n})
                s = None
                if not last_one:
                    s = begin_unit()
                for j in range(4):
                    n = (j + 1) * P
                    for m in range(2):
                        half = slice(64 * m, 64 * m + 64)
                        aux_claim(4 + m)
                        aux_end(pe.matmul(bank[4 + m][:, 0:n], dQ[i][half, j * P:n], dK[i][half, 0:n], start=True, stop=True), 4 + m)
                    if not last_one:
                        head_steps(s, DIFF_SLOTS[j])
                    if j > 0:
                        probs.add()
                        transposes(6, DF["L"][(j - 1) % 2][0], j, p_ready, probs.at())
                    if j == 1 and not first:
                        sum_squares_of_head()
                if not last_one:
                    head_steps(s, DIFF_SLOTS[4])
                probs.add()
                transposes(6, DF["L"][1][0], NB, p_ready, probs.at())
                if not last_one:
                    transposes(6, dVT, NB, tile_free, tiles.at())
                value_product(DF, dV[i], slice(0, P), slice(0, P), 0 if last_one else 1)

            def sum_squares_of_head():
                aux_claim(7)
                sum_squares(7, 1)

            s = begin_unit()
            tiles_together(s, 3, XH, XL, KD)
            los.add(KD)
            transposes(6, dVT, NB, tile_free, tiles.at())
            diff_head(0, True, False)
            with counted_loop(pe, 3, {unit: 2, tiles: 6, aux: 28, sqs: 2, probs: 8}):
                diff_head(1, False, False)
                diff_head(0, False, False)
            diff_head(1, False, True)
            sum_squares_of_head()
            out_projection()
            layer_norm()
            ffn()
            layer_norm()

            s = begin_unit()
            tiles_together(s, 2, XH, XL, KD)
            los.add(KD)
            unit_tiles(2, 2)
            with counted_loop(pe, 3, {unit: 2, tiles: 4}):
                unit_tiles(2, 0)
                unit_tiles(2, 2)
            s = begin_unit()
            for i in range(4):
                pe.wait_ge(act_lo, los.at(i + 1))
                claim(4)
                product(bank[i][:], s, i * P, EPH[:, i, :], EPL[:, i, :], True, True).then_inc(tile_done, 1)
                tiles.add()
            los.add(4)
            out_projection()
            layer_norm()
            ffn()
            layer_norm()

            s = begin_unit()
            tiles_together(s, 1, XH, XL, KD)
            los.add(KD)
            pe.wait_ge(tile_free, tiles.at())
            for i in range(4):
                unit_tiles(2, 2 * i % 4)
            pe.wait_ge(tile_free, tiles.at())
            s = begin_unit()
            for t in range(3):
                tile(s, t, [(k * 3 + t) * P for k in range(KD)], XH, XL, 3)
            transposes(6, fVT, NB, tile_free, tiles.at())
            for g in range(4):
                i = g % 2
                if g == 0:
                    pe.wait_ge(cum_ready, 1)
                for m in range(2):
                    aux_claim(6 + m)
                    aux_end(pe.matmul(bank[6 + m][:], ident[0:8, 2 * g + m:2 * g + m + 1].to_broadcast([8, P]), cum[:], start=True, stop=True), 6 + m)
                pe.wait_ge(tile_free, tiles.at())
                if g < 3:
                    s = begin_unit()
                for j in range(8):
                    m, qb = j // 4, j % 4
                    b, n = 4 + j % 2, (qb + 1) * P
                    half = slice(64 * m, 64 * m + 64)
                    aux_claim(b)
                    aux_end(pe.matmul(bank[b][:, 0:n], fQ[i][half, qb * P:n], fK[i][half, 0:n], start=True, stop=True), b)
                    if g < 3:
                        head_steps(s, ODD_SLOTS[j])
                    if j == 5:
                        value_product(FO, fV[i], slice(0, 64), slice(0, 64), 1)
                    if j > 0:
                        probs.add()
                        transposes(6, FO["L"][(j - 1) % 2][0], (j - 1) % 4 + 1, p_ready, probs.at())
                if g < 3:
                    head_steps(s, ODD_SLOTS[8])
                probs.add()
                transposes(6, FO["L"][1][0], NB, p_ready, probs.at())
                if g < 3:
                    transposes(6, fVT, NB, tile_free, tiles.at())
                value_product(FO, fV[i], slice(64, P), slice(64, P), 1 if g < 3 else 0)
            pe.wait_ge(sum_ready, norms.at(1))
            pe.matmul(bank[6][:], ones[:], rstd[:], start=True, stop=True).then_inc(stat_done, 1)
            norms.add()
            sum_squares(7, 4)
            out_projection()
            layer_norm()
            ffn()
            layer_norm()

        @block.vector
        def _(dve):
            tiles, aux, los, steps, exps, gates, stds, srcs, norms, smalls = (Count() for _ in range(10))

            def link(ins):
                ins.then_inc(step, 1)
                steps.add()
                dve.wait_ge(step, steps.at())

            def take(op, n=1):
                dve.wait_ge(tile_done, tiles.at(n))
                op().then_inc(tile_free, n)
                tiles.add(n)

            def take_aux(op):
                dve.wait_ge(aux_done, aux.at(1))
                op().then_inc(aux_free, 1)
                aux.add()

            def copy_tile(dst, b):
                take(lambda: dve.tensor_copy(dst, bank[b][:]))

            def mean_over_tiles(T, n):
                norms.add()
                dve.wait_ge(stat_done, norms.at())
                for j in range(n):
                    dve.scalar_tensor_tensor(T[:, j, :], bank[6][:], -1.0 / (n * P), T[:, j, :], ALU.mult, ALU.add)\
                       .then_inc(dev_ready, 1)

            def running_sum(T, j, n):
                if j == 0:
                    return
                ins = dve.tensor_tensor(rstd[:], T[:, 0, :] if j == 1 else rstd[:], T[:, j, :], ALU.add)
                if j < n - 1:
                    link(ins)
                else:
                    ins.then_inc(sum_ready, 1)

            def reciprocal_std():
                stds.add()
                dve.wait_ge(std_ready, stds.at())
                link(dve.reciprocal(rstd[:], rstd[:]))

            def scale_shift(T, n, gname, bname, base, done):
                def mul(j):
                    dve.tensor_tensor(T[:, j, :], T[:, j, :], rstd[:], ALU.mult).then_inc(step, 1)
                    steps.add()
                mul(0)
                for j in range(n):
                    if j + 1 < n:
                        mul(j + 1)
                    dve.wait_ge(step, steps.at(-1 if j + 1 < n else 0))
                    dve.tensor_scalar(T[:, j, :], T[:, j, :], pcol(gname, base + j), pcol(bname, base + j),
                                      ALU.mult, ALU.add).then_inc(done, 1)

            def layer_norm(index):
                mean_over_tiles(X, KD)
                reciprocal_std()
                scale_shift(X, KD, "ln_g", "ln_b", KD * index, src_ready)
                srcs.add(KD)
                los.add(KD)

            def residual(j, b, scale):
                take(lambda: dve.scalar_tensor_tensor(X[:, j, :], X[:, j, :], scale, bank[b][:], ALU.mult, ALU.add))

            def out_projection():
                for j in range(KD):
                    residual(j, j % 4, ALPHA)
                    dve.wait_ge(tile_free, tiles.at())
                    running_sum(X, j, KD)

            def ffn():
                for half in range(2):
                    n = HID[half]
                    with counted_loop(dve, n // 2, {tiles: 4, gates: 2, los: 2}):
                        for i in range(2):
                            dve.wait_ge(gate_done, gates.at(1))
                            dve.wait_ge(act_lo, los.at(-1))
                            take(lambda: dve.tensor_tensor(hf[i][:], sil[i][:], bank[2 * i + 1][:], ALU.mult), 2)
                            gates.add()
                            los.add()
                    for j in range(KD):
                        residual(j, j % 4, ALPHA if half == 0 else 1.0)
                        if half == 1:
                            dve.wait_ge(tile_free, tiles.at())
                            running_sum(X, j, KD)

            def logits(A, i, m, qb, col, b, bias, scale):
                n = (qb + 1) * P
                dve.wait_ge(aux_done, aux.at(1))
                if aux.reg is not None:
                    dve.memset(spare[:, qb * 2 + m:qb * 2 + m + 1], 0.0)
                aux.add()
                dve.tensor_tensor_reduce(
                    out=A["L"][i][m][:, 0:n], in0=bank[b][:, 0:n], in1=bias[:, S - n:S], scale=-scale, scalar=BIG,
                    op0=ALU.add, op1=ALU.min, accum_out=A["negmax"][:, col:col + 1]).then_inc(aux_free, 1)

            def normalise(A, i, qb, col):
                n = (qb + 1) * P
                exps.add()
                dve.wait_ge(exp_done, exps.at())
                link(dve.reciprocal(A["rinv"][:, col:col + 1], A["rowsum"][:, col:col + 1]))
                row = A["L"][i][0][:, 0:n]
                dve.tensor_scalar(row, row, A["rinv"][:, col:col + 1], None, ALU.mult).then_inc(p_ready, 1)

            def keep_transposed(A, qb):
                n = (qb + 1) * P
                take_aux(lambda: dve.tensor_copy(A["PT"][:, 0:qb + 1, qb * P:n],
                                                 bank[6][:, 0:n].rearrange("p (k q) -> p k q", q=P)))

            def keep_values(dst):
                take_aux(lambda: dve.tensor_copy(dst[:].rearrange("p k d -> p (k d)"), bank[6][:]))

            dve.wait_ge(x_in, 64)
            dve.tensor_tensor(lam[:, 0:2], parm[:, PCOL["lam"]:PCOL["lam"] + 4:2], parm[:, PCOL["lam"] + 1:PCOL["lam"] + 4:2],
                              ALU.mult).then_inc(small_dve, 1)
            dve.tensor_scalar(gsub[:], pcol("g_sub"), 1.0 - LAMBDA_INIT, None, ALU.mult)
            los.add(KD)

            cosT, sinT, maskT = (rtab[:, RCOL[n]:RCOL[n] + S] for n in ("cos", "sin", "mask"))
            for j in range(5):
                copy_tile(Cf[:, j, :], j % 4)
            take(lambda: dve.tensor_tensor(KR[:], bank[1][:], cosT, ALU.mult))
            take(lambda: dve.tensor_tensor(rt[:], bank[2][:], sinT, ALU.mult))
            dve.wait_ge(tile_free, tiles.at())
            dve.tensor_tensor(KR[:], KR[:], rt[:], ALU.add).then_inc(rope_ready, 1)
            for part in (range(3), range(3, 5)):
                reciprocal_std()
                for j in part:
                    dve.scalar_tensor_tensor(Cf[:, j, :], Cf[:, j, :], pcol("g_c", j), rstd[:], ALU.mult, ALU.mult)\
                       .then_inc(src_ready, 1)
            srcs.add(5)
            los.add(5)

            def mla_tile(i, t, ropes):
                b = t % 4
                if t < 2:
                    copy_tile(mQN[i][t][:], b)
                elif t == 2:
                    take(lambda: dve.tensor_tensor(mQR[i][:], bank[b][:], cosT, ALU.mult))
                elif t == 3:
                    dve.wait_ge(rope_ready, ropes)
                    take(lambda: dve.tensor_tensor(rt[:], bank[b][:], sinT, ALU.mult))
                    dve.wait_ge(tile_free, tiles.at())
                    dve.tensor_tensor(mQR[i][:], mQR[i][:], rt[:], ALU.add).then_inc(rope_ready, 1)
                else:
                    copy_tile((mKN[i][t // 2 - 2] if t % 2 == 0 else mVT[t // 2 - 2])[:], b)

            for t in range(8):
                mla_tile(0, t, 1)
            keep_values(mV[0][0])
            keep_values(mV[0][1])
            for p in range(4):
                i, o = p % 2, (p + 1) % 2
                for j in range(8):
                    logits(ML, j % 2, 0, j % 4, j % 2, 4 + j % 2, maskT, MLA_SCALE)
                    if j > 0:
                        normalise(ML, (j - 1) % 2, (j - 1) % 4, (j - 1) % 2)
                    for t in finished(MLA_SLOTS[j], MLA_K) if p < 3 else ():
                        mla_tile(o, t, p + 2)
                    if j == 5:
                        if p:
                            dve.wait_ge(act_lo, los.at(-1))
                        take_aux(lambda: dve.tensor_copy(sq[0][:], bank[7][:]))
                        los.add()
                    if j > 0:
                        keep_transposed(ML, (j - 1) % 4)
                normalise(ML, 1, 3, 1)
                for t in finished(MLA_SLOTS[8], MLA_K) if p < 3 else ():
                    mla_tile(o, t, p + 2)
                keep_transposed(ML, 3)
                if p < 3:
                    keep_values(mV[o][0])
                    keep_values(mV[o][1])
                if p:
                    dve.wait_ge(act_lo, los.at(-1))
                take_aux(lambda: dve.tensor_copy(sq[1][:], bank[7][:]))
                los.add()
            out_projection()
            layer_norm(0)
            ffn()
            layer_norm(2)

            smalls.add()
            dve.wait_ge(small_act, smalls.at())
            link(dve.tensor_tensor(lam[:, 6:7], lam[:, 4:5], lam[:, 5:6], ALU.subtract))
            link(dve.tensor_scalar(lam[:, 7:8], lam[:, 6:7], LAMBDA_INIT, None, ALU.add))

            def scale_head(i, head):
                stds.add()
                dve.wait_ge(std_ready, stds.at())
                out = DF["Y"][:, head, :] if isinstance(head, int) else \
                    DF["Y"][:, bass.ds(head, 1), :].rearrange("p o n -> p (o n)")
                dve.scalar_tensor_tensor(out, dO[i][:], gsub[:], dms[:], ALU.mult, ALU.mult).then_inc(src_ready, 1)

            mss = Count()

            def mean_square():
                sqs_seen.add()
                dve.wait_ge(sq_used, sqs_seen.at())
                dve.tensor_scalar(dms[:], bank[7][:], 1.0 / P, RMS_EPS, ALU.mult, ALU.add).then_inc(ms_ready, 1)
                mss.add()

            sqs_seen = Count()
            sqs_seen.add(5 + 2 * KD)

            def diff_head(i, h, first, last_one):
                o = 1 - i
                col = cons[:, CCOL["slopes"] + h:CCOL["slopes"] + h + 1] if isinstance(h, int) else \
                    cons[:, bass.ds(h + CCOL["slopes"], 1)]
                link(dve.tensor_scalar(dB[:], dist, col, None, ALU.mult))
                for j in range(4):
                    for m in range(2):
                        logits(DF, j % 2, m, j, 2 * (j % 2) + m, 4 + m, dB[:], HD_SCALE)
                    if j > 0:
                        combine(j - 1)
                    for t in finished(DIFF_SLOTS[j], (KD,) * 3) if not last_one else ():
                        copy_tile((dQ[o], dK[o], dVT)[t][:], t)
                    if j > 0:
                        keep_transposed(DF, j - 1)
                    if j == 1 and not first:
                        mean_square()
                    if j == 2 and not first:
                        scale_head(o, h - 1)
                combine(3)
                for t in finished(DIFF_SLOTS[4], (KD,) * 3) if not last_one else ():
                    copy_tile((dQ[o], dK[o], dVT)[t][:], t)
                keep_transposed(DF, 3)
                if not last_one:
                    keep_values(dV[o])
                take_aux(lambda: dve.tensor_copy(dO[i][:], bank[7][:]))

            def combine(j):
                n, c = (j + 1) * P, 2 * (j % 2)
                exps.add(2)
                dve.wait_ge(exp_done, exps.at())
                link(dve.reciprocal(DF["rinv"][:, c:c + 2], DF["rowsum"][:, c:c + 2]))
                p0, p1 = (DF["L"][j % 2][m][:, 0:n] for m in range(2))
                link(dve.tensor_scalar(p1, p1, DF["rinv"][:, c + 1:c + 2], lam[:, 7:8], ALU.mult, ALU.mult))
                dve.scalar_tensor_tensor(p0, p0, DF["rinv"][:, c:c + 1], p1, ALU.mult, ALU.subtract).then_inc(p_ready, 1)

            for t in range(3):
                copy_tile((dQ[0], dK[0], dVT)[t][:], t)
            keep_values(dV[0])
            diff_head(0, 0, True, False)
            with counted_loop(dve, 3, {tiles: 6, aux: 28, steps: 18, exps: 16, stds: 2, mss: 2, sqs_seen: 2}) as it:
                diff_head(1, it * 2 + 1, False, False)
                diff_head(0, it * 2 + 2, False, False)
            diff_head(1, 7, False, True)
            mean_square()
            scale_head(1, 7)
            srcs.add(KD)
            los.add(KD)
            smalls.add(KD)
            out_projection()
            layer_norm(1)
            ffn()
            layer_norm(3)

            dve.memset(ez[:, 0:2], 0.0)
            for u in eu:
                dve.memset(u[:, 0:PADW], 0.0)

            def conv_col(k, i):
                return pcol("conv_w", 4 * k + i)

            for i in range(4):
                b = 2 * i % 4
                copy_tile(ec[:], b)
                dve.wait_ge(tile_free, tiles.at())
                take(lambda: dve.tensor_tensor(ez[:, 2:2 + S], bank[b + 1][:], ec[:], ALU.mult))
                dve.wait_ge(tile_free, tiles.at())
                y = EY[:, i, :]
                link(dve.tensor_scalar(y, ez[:, 0:S], conv_col(0, i), None, ALU.mult))
                for k in (1, 2):
                    link(dve.scalar_tensor_tensor(y, ez[:, k:k + S], conv_col(k, i), y, ALU.mult, ALU.add))
            for i in range(4):
                b = 2 * i % 4
                take(lambda: dve.tensor_tensor(EY[:, i, :], bank[b][:], EY[:, i, :], ALU.mult))
                dve.wait_ge(src_ready, srcs.at())
                take(lambda: dve.tensor_copy(eu[0][:, PADW:], bank[b + 1][:]))
                dve.wait_ge(tile_free, tiles.at())
                src = eu[0]
                for d in range(i + 1):
                    dst = eu[1 + d % 2]
                    link(dve.tensor_tensor(dst[:, PADW:], src[:, PADW:], src[:, PADW - 2 ** d:PADW - 2 ** d + S], ALU.add))
                    src = dst
                link(dve.scalar_tensor_tensor(EP[:, i, PADW:], src[:, 2 * PADW:], 1.0 / WINDOWS[i], eu[0][:, 2 * PADW:], ALU.mult, ALU.subtract))
                link(dve.tensor_tensor(EP[:, i, 0:PADW], src[:, PADW:2 * PADW], cons[:, CCOL["invcnt"] + 16 * i:CCOL["invcnt"] + 16 * i + 16], ALU.mult))
                dve.tensor_tensor(EP[:, i, 0:PADW], EP[:, i, 0:PADW], eu[0][:, PADW:2 * PADW], ALU.subtract).then_inc(src_ready, 1)
                srcs.add()
            los.add(4)
            for i in range(4):
                take(lambda: dve.tensor_scalar(EY[:, 4 + i, :], bank[i][:], pcol("pool_s", i), None, ALU.mult))
            los.add(KD)
            out_projection()
            layer_norm(4)
            ffn()
            layer_norm(6)

            take(lambda: dve.tensor_scalar(lfz[:], bank[0][0:8, :], parm[0:8, PCOL["f_b"]:PCOL["f_b"] + 1], None, ALU.add))
            smalls.add(2)
            dve.wait_ge(small_act, smalls.at())
            dve.tensor_scalar(lfu[:], lfe[:], 1.0, None, ALU.add).then_inc(small_dve, 1)
            dve.wait_ge(small_dve, 2)
            link(dve.tensor_scalar(lfd[:], lfu[:], 1.0, None, ALU.subtract))
            link(dve.tensor_scalar(lfi[:], lfd[:], 0.0, None, ALU.is_equal))
            link(dve.tensor_tensor(lfd[:], lfd[:], lfi[:], ALU.add))
            link(dve.reciprocal(lfr[:], lfd[:]))
            link(dve.tensor_tensor(lfr[:], lfe[:], lfr[:], ALU.mult))
            smalls.add()
            dve.wait_ge(small_act, smalls.at())
            link(dve.tensor_tensor(lfr[:], lfl[:], lfr[:], ALU.mult))
            link(dve.tensor_tensor(lfi[:], lfi[:], lfe[:], ALU.mult))
            link(dve.tensor_tensor(lfr[:], lfr[:], lfi[:], ALU.add))
            link(dve.tensor_scalar(lfz[:], lfz[:], 0.0, None, ALU.min))
            link(dve.tensor_tensor(lfz[:], lfz[:], lfr[:], ALU.subtract))
            link(dve.memset(lfd[:], 0.0))
            dve.tensor_tensor_scan(cum[:], lfz[:], lfd[:], 0.0, ALU.add, ALU.add).then_inc(cum_ready, 1)

            for i in range(4):
                dve.memset(fz[i][:, 0:PADC], 0.0)
            for i in range(4):
                dve.wait_ge(gate_done, gates.at(1))
                gates.add()
                take(lambda: dve.tensor_tensor(fz[i][:, PADC:], fsig[:], bank[2 * i % 4][:], ALU.mult), 2)

            def taps(i, first, n):
                y = FO["Y"][:, 4 + i, :]
                for k in range(first, first + n):
                    wk = pcol("dw_w", 4 * k + i)
                    if k == 0:
                        link(dve.tensor_scalar(y, fz[i][:, 0:S], wk, pcol("dw_b", i), ALU.mult, ALU.add))
                    else:
                        link(dve.scalar_tensor_tensor(y, fz[i][:, k:k + S], wk, y, ALU.mult, ALU.add))

            def forget_logits(i, m, qb, col, b):
                n0 = qb * P
                dve.wait_ge(aux_done, aux.at(1))
                first = BIG
                if qb:
                    first = FO["negmax"][:, 2 + col:3 + col]
                    link(dve.tensor_tensor_reduce(
                        out=FO["L"][i][0][:, 0:n0], in0=bank[b][:, 0:n0], in1=fB[m][:, 0:n0], scale=-HD_SCALE, scalar=BIG,
                        op0=ALU.add, op1=ALU.min, accum_out=first))
                take_aux(lambda: dve.tensor_tensor_reduce(
                    out=FO["L"][i][0][:, n0:n0 + P], in0=bank[b][:, n0:n0 + P], in1=fBD[m][:, qb, :], scale=-HD_SCALE,
                    scalar=first, op0=ALU.add, op1=ALU.min, accum_out=FO["negmax"][:, col:col + 1]))

            for t in range(3):
                copy_tile((fQ[0], fK[0], fVT)[t][:], t)
            keep_values(fV[0])
            for g in range(4):
                o = (g + 1) % 2
                for m in range(2):
                    take_aux(lambda: dve.tensor_scalar(fB[m][:], bank[6 + m][:], -1.0 / HD_SCALE, None, ALU.mult))
                    dve.wait_ge(aux_free, aux.at())
                    link(dve.tensor_tensor(fBD[m][:], fB[m][:].rearrange("p (k q) -> p k q", q=P),
                                           causal.unsqueeze(1).to_broadcast([P, NB, P]), ALU.add))
                for j in range(8):
                    forget_logits(j % 2, j // 4, j % 4, j % 2, 4 + j % 2)
                    if j > 0:
                        normalise(FO, (j - 1) % 2, (j - 1) % 4, (j - 1) % 2)
                    for t in finished(ODD_SLOTS[j], (KD,) * 3) if g < 3 else ():
                        copy_tile((fQ[o], fK[o], fVT)[t][:], t)
                    if j == 5:
                        take_aux(lambda: dve.tensor_copy(FO["Y"][0:64, g, :], bank[7][0:64, :]))
                    if j > 0:
                        keep_transposed(FO, (j - 1) % 4)
                    taps(g, 4 * j, min(4, TAPS - 4 * j))
                normalise(FO, 1, 3, 1)
                for t in finished(ODD_SLOTS[8], (KD,) * 3) if g < 3 else ():
                    copy_tile((fQ[o], fK[o], fVT)[t][:], t)
                keep_transposed(FO, 3)
                if g < 3:
                    keep_values(fV[o])
                take_aux(lambda: dve.tensor_copy(FO["Y"][64:P, g, :], bank[7][64:P, :]))
            C = FO["Y"][:, 4:8, :]
            for i in range(4):
                running_sum(C, i, 4)
            mean_over_tiles(C, 4)
            reciprocal_std()
            scale_shift(C, 4, "cn_g", "cn_b", 0, small_dve)
            los.add(KD)
            out_projection()
            layer_norm(5)
            ffn()
            assert srcs.n == SRC_BEFORE_LAST
            layer_norm(7)


def host_layout(inp):
    f = lambda a: np.asarray(a)

    def ktiles(m):
        return m.reshape(m.shape[0] // P, P, m.shape[1]).transpose(1, 0, 2)

    def unit(m, size=None):
        u = ktiles(m).reshape(P, -1)
        return u if size is None or u.shape[1] == size else np.pad(u, ((0, 0), (0, size - u.shape[1])))

    def out3(m):
        return np.stack([unit(m[:, 0:384]), unit(m[:, 384:768]), unit(m[:, 768:1024], 3072)])

    w = {}
    swap = np.r_[32:64, 0:32]
    win = f(inp["mla_w_in"])[0]
    kr = win[:, 640:704]
    w["mla_in"] = np.stack([unit(win[:, 0:384]), unit(np.concatenate([win[:, 384:640], kr, kr], 1)),
                            unit(np.concatenate([kr[:, swap]] * 2, 1), 3072)])
    uq, ukv = f(inp["mla_w_uq"])[0].reshape(QR, 8, 192), f(inp["mla_w_ukv"])[0]
    pairs = []
    for p in range(4):
        a, b = uq[:, 2 * p], uq[:, 2 * p + 1]
        ra, rb = a[:, 128:], b[:, 128:]
        q = np.concatenate([a[:, :128], b[:, :128], ra, rb, ra[:, swap], rb[:, swap]], 1)
        pairs.append(np.concatenate([unit(q), unit(ukv[:, 512 * p:512 * p + 512])], 1))
    w["mla_pair"] = np.stack(pairs)
    w["mla_o"] = out3(f(inp["mla_w_o"])[0])
    ffns = [(f(inp["ffn_w_gu"])[i], f(inp["ffn_w_down"])[i]) for i in range(2)] + \
           [(f(inp["ffn_w_in_2"])[i], f(inp["ffn_w_out_2"])[i]) for i in range(2)]
    for i, (gu, down) in enumerate(ffns):
        g = gu.reshape(KD, P, 2, D_FF // P, P).transpose(3, 1, 0, 2, 4)
        w[f"ffn{i}_gu"] = g.reshape(D_FF // P, P, 2048)
        for half, r0, n in ((0, 0, HID[0]), (1, HID[0], HID[1])):
            d = down[r0 * P:(r0 + n) * P]
            w[f"ffn{i}_d{half}"] = d.reshape(n, P, 4, 256).transpose(2, 1, 0, 3).reshape(4, P, n * 256)
    win = f(inp["diff_w_in"])[0].reshape(KD, P, 3, 8, P).transpose(3, 1, 0, 2, 4)
    w["diff_in"] = win.reshape(8, P, 3072)
    w["diff_o"] = out3(f(inp["diff_w_o"])[0])
    win = f(inp["ev_w_in_2"])[0].reshape(KD, P, 4, 4, P)
    cv = win[:, :, 1:3].transpose(3, 1, 0, 2, 4).reshape(4, P, 2048)
    bu = win[:, :, 0::3].transpose(3, 1, 0, 2, 4).reshape(4, P, 2048)
    w["ev_in"] = np.concatenate([cv, bu])
    w["ev_pool"] = f(inp["ev_pool_w_2"])[0].transpose(1, 0, 2).reshape(1, P, 512)
    w["ev_o"] = out3(f(inp["ev_w_out_2"])[0])
    win = f(inp["od_w_in_2"])[0]
    w["od_f"] = unit(win[:, 1536:1664])[None]
    w["od_conv"] = win[:, 1544:2568].reshape(KD, P, 2, 4, P).transpose(3, 1, 0, 2, 4).reshape(4, P, 2048)
    w["od_in"] = win[:, 0:1536].reshape(KD, P, 3, 4, P).transpose(3, 1, 0, 2, 4).reshape(4, P, 3072)
    w["od_o"] = out3(f(inp["od_w_out_2"])[0])

    cols = lambda a: f(a).reshape(-1, P).T
    pad = lambda a: np.pad(f(a).reshape(-1, 1), ((0, P - f(a).size), (0, 0)))
    par = np.concatenate([
        cols(inp["ln_mix_g"]), cols(inp["ln_ffn_g"]), cols(inp["ln_mix_g_2"]), cols(inp["ln_ffn_g_2"]),
        cols(inp["ln_mix_b"]), cols(inp["ln_ffn_b"]), cols(inp["ln_mix_b_2"]), cols(inp["ln_ffn_b_2"]),
        cols(inp["mla_g_q"]), cols(inp["mla_g_kv"]), cols(inp["diff_g_sub"]), cols(inp["ev_conv_w_2"]),
        cols(inp["ev_pool_scale_2"]), cols(inp["od_dw_w_2"]), cols(inp["od_dw_b_2"]), cols(inp["od_cn_g_2"]),
        cols(inp["od_cn_b_2"]), pad(inp["diff_lam_q1"]), pad(inp["diff_lam_k1"]), pad(inp["diff_lam_q2"]),
        pad(inp["diff_lam_k2"]), pad(inp["od_forget_b_2"])], 1)
    assert par.shape == (P, NPAR)
    return w, par


def constants():
    p = np.arange(P)[:, None]
    con = np.zeros((P, NCON), np.float32)
    con[:, CCOL["ident"]:CCOL["ident"] + P] = np.eye(P)
    x = np.arange(S)[None, :]
    hidden = (x - (S - P)) // 64 > p // 64
    con[:, CCOL["dist"]:CCOL["dist"] + S] = np.where(hidden, 1e32, np.abs(p + (S - P) - x))
    con[:, CCOL["causal"]:CCOL["causal"] + P] = np.where(np.arange(P)[None, :] > p, NEG, 0.0)
    for g, win in enumerate(WINDOWS):
        con[:, CCOL["invcnt"] + 16 * g:CCOL["invcnt"] + 16 * g + 16] = 1.0 / np.minimum(np.arange(16) + 1, win)
    con[:, CCOL["slopes"]:CCOL["slopes"] + 8] = -2.0 ** -np.arange(1, 9) / HD_SCALE
    inv = np.float32(10000.0) ** (-np.arange(0, ROPE, 2, dtype=np.float32) / np.float32(ROPE))
    ang = (np.arange(S, dtype=np.float32)[None, :] * inv[:, None].astype(np.float32)).astype(np.float32)
    cos, sin = np.cos(ang), np.sin(ang)
    rcon = np.concatenate([np.concatenate([cos] * 4), np.concatenate([-sin, sin] * 2),
                           np.where(hidden, NEG, 0.0)], 1).astype(np.float32)
    return con, rcon


def kernel(**inputs):
    import concourse.bacc as bacc
    from concourse.bass_utils import run_bass_kernel_spmd

    w, par = host_layout(inputs)
    con, rcon = constants()
    arrays = {"xT": np.asarray(inputs["x"])[0].T.reshape(KD, P, S), "par": par, "con": con, "rcon": rcon}
    arrays.update({f"w_{k}": v for k, v in w.items()})
    arrays = {k: np.ascontiguousarray(v) for k, v in arrays.items()}
    nc = bacc.Bacc("TRN2", target_bir_lowering=False, num_devices=1)
    ap = {k: nc.dram_tensor(k, v.shape, F32, kind="ExternalInput").ap() for k, v in arrays.items()}
    outT = nc.dram_tensor("outT", (KD, P, S), F32, kind="ExternalOutput").ap()
    build(nc, ap["xT"], ap["par"], ap["con"], ap["rcon"], {k: ap[f"w_{k}"] for k in w}, outT)
    r = run_bass_kernel_spmd(nc, [arrays], core_ids=[0])
    return np.ascontiguousarray(np.asarray(r.results[0]["outT"]).reshape(D, S).T)[None]
```

```python
import math
from contextlib import ExitStack, contextmanager

import concourse.bass as bass
import numpy as np
from concourse import mybir

F32 = mybir.dt.float32
F32R = mybir.dt.float32r
ALU = mybir.AluOpType
ACT = mybir.ActivationFunctionType

P = 128
S = 512
NB = S // P
D = 1024
KD = D // P
D_FF = 2816
HID = (12, 10)
QR, KVR = 384, 256
ROPE, NOPE = 64, 128
SLOT = 3072
ALPHA = 4.0 ** 0.25
LN_EPS, RMS_EPS = 1e-5, 1e-6
NEG = -1e30
LAST_NORM = 7
BIG = 3.0e38
MLA_SCALE = (NOPE + ROPE) ** -0.5
HD_SCALE = 64 ** -0.5
LAMBDA_INIT = 0.8 - 0.6 * math.exp(-0.3)
TAPS = 31
COUNTS = (D, D // 2, QR, KVR, P)
WINDOWS = (2, 4, 8, 16)
PADC, PADW = TAPS - 1, 16

PCOL, _n = {}, 0
for _name, _w in (("ln_g", 64), ("ln_b", 64), ("g_c", 5), ("g_sub", 1), ("conv_w", 12), ("pool_s", 4),
                  ("dw_w", 4 * TAPS), ("dw_b", 4), ("cn_g", 4), ("cn_b", 4), ("lam", 4), ("f_b", 1)):
    PCOL[_name] = _n
    _n += _w
NPAR = _n
CCOL, _n = {}, 0
for _name, _w in (("ident", P), ("dist", S), ("causal", P), ("invcnt", 64), ("slopes", 8)):
    CCOL[_name] = _n
    _n += _w
NCON = _n
RCOL = {"cos": 0, "sin": S, "mask": 2 * S}

OUT3 = (3072, 3072, 2048)
STREAM = (
    ("mla_in", (3072, 3072, 1024)), ("mla_pair", (2560,) * 4), ("mla_o", OUT3), ("ffn0", None),
    ("diff_in", (3072,) * 8), ("diff_o", OUT3), ("ffn1", None),
    ("ev_in", (2048,) * 8), ("ev_pool", (512,)), ("ev_o", OUT3), ("ffn2", None),
    ("od_f", (1024,)), ("od_conv", (2048,) * 4), ("od_in", (3072,) * 4), ("od_o", OUT3), ("ffn3", None),
)
OUT_MLA = ((0,), (), (1,), (2,), (3,), (4,), (), (5,), (6,), (7,))
OUT_DIFF = ((), (0, 1), (2,), (3, 4), (5,), (6, 7))
OUT_ODD = ((), (0,), (), (1,), (2,), (), (), (), (), (3, 4, 5, 6, 7))
LATENTS = 5
SHIFT_FROM = 4
STEPS = [(t, k) for t in range(3) for k in range(KD)]
DIFF_SLOTS = (STEPS[0:5], STEPS[5:10], STEPS[10:15], STEPS[15:20], STEPS[20:24])
ODD_SLOTS = (STEPS[0:3], STEPS[3:6], STEPS[6:9], STEPS[9:12], STEPS[12:15], [], STEPS[15:18], STEPS[18:21], STEPS[21:24])
MLA_K = (3, 3, 3, 3, 2, 2, 2, 2)
MLA_SLOTS = tuple([(t, k) for k in range(MLA_K[t])] if t is not None else [] for t in (0, 1, 2, 3, 4, None, 5, 6, 7))


def finished(slot, depth):
    return [t for t, k in slot if k == depth[t] - 1]


class Count:

    def __init__(self):
        self.n, self.reg, self.slope = 0, None, 0

    def at(self, d=0):
        v = self.n + d
        return v if self.reg is None else self.reg * self.slope + v

    def add(self, k=1):
        self.n += k


@contextmanager
def counted_loop(eng, trips, slopes):
    start = {c: c.n for c in slopes}
    with eng.Fori(0, trips) as it:
        for c, k in slopes.items():
            c.reg, c.slope = it, k
        yield it
    for c, k in slopes.items():
        assert c.n - start[c] == k, (c.n - start[c], k)
        c.n, c.reg = start[c] + trips * k, None


def build(nc, xT, par, con, rcon, w, outT):
    ctx = ExitStack()
    with ctx:
        def sb(name, shape, dt=F32, stack=ctx):
            return stack.enter_context(nc.sbuf_tensor(name, shape, dt))

        def sem(name):
            return ctx.enter_context(nc.semaphore(name))

        raw = [sb(f"raw{i}", [P, SLOT]) for i in range(2)]
        whi = [sb(f"whi{i}", [P, SLOT], F32R) for i in range(2)]
        wlo = [sb(f"wlo{i}", [P, SLOT], F32R) for i in range(2)]
        X = sb("X", [P, KD, S])
        XH = sb("XH", [P, KD, S], F32R)
        XL = sb("XL", [P, KD, S], F32R)
        parm = sb("parm", [P, NPAR])
        cons = sb("cons", [P, NCON])
        ones = sb("ones", [P, P])
        inverse = sb("inverse", [P, len(COUNTS)])
        neg_half = sb("neg_half", [P, NB])
        sq = [sb(f"sq{i}", [P, S]) for i in range(2)]
        shift = sb("shift", [P, S])
        sqt = sb("sqt", [P, S])
        st = sb("st", [P, 4 * NB])
        root = sb("root", [P, NB])
        gsub = sb("gsub", [P, 1])
        lam = sb("lam", [P, 8])
        spare = sb("spare", [1, 8])
        ident = cons[:, CCOL["ident"]:CCOL["ident"] + P]
        dist = cons[:, CCOL["dist"]:CCOL["dist"] + S]
        causal = cons[:, CCOL["causal"]:CCOL["causal"] + P]

        def pcol(name, i=0):
            return parm[:, PCOL[name] + i:PCOL[name] + i + 1]

        ph = ExitStack()
        HH = sb("HH", [P, HID[0], S], F32R, ph)
        HL = sb("HL", [P, HID[0], S], F32R, ph)
        sil = [sb(f"sil{i}", [P, S], F32, ph) for i in range(2)]
        hf = [sb(f"hf{i}", [P, S], F32, ph) for i in range(2)]
        ph.close()

        def attention_buffers(ph, tag, maps, y, pt=1):
            a = {}
            a["L"] = [[sb(f"{tag}L{i}{m}", [P, S], F32, ph) for m in range(maps)] for i in range(2)]
            a["negmax"] = sb(f"{tag}negmax", [P, 4], F32, ph)
            a["rowsum"] = sb(f"{tag}rowsum", [P, 4], F32, ph)
            a["rinv"] = sb(f"{tag}rinv", [P, 4], F32, ph)
            a["PT"] = sb(f"{tag}PT", [P, NB, S], F32, ph)
            if y:
                a["Y"] = sb(f"{tag}Y", [P, KD, S], F32, ph)
            return a

        ph = ExitStack()
        ML = attention_buffers(ph, "m", 1, False)
        rtab = sb("rtab", [P, 3 * S], F32, ph)
        CH = sb("CH", [P, 5, S], F32R, ph)
        CL = sb("CL", [P, 5, S], F32R, ph)
        KR = sb("KR", [P, S], F32, ph)
        rt = sb("rt", [P, S], F32, ph)
        cf_stack = ExitStack()
        Cf = sb("Cf", [P, 5, S], F32, cf_stack)
        cf_stack.close()
        mQN = [[sb(f"mQN{i}{m}", [P, S], F32, ph) for m in range(2)] for i in range(2)]
        mKN = [[sb(f"mKN{i}{m}", [P, S], F32, ph) for m in range(2)] for i in range(2)]
        mQR = [sb(f"mQR{i}", [P, S], F32, ph) for i in range(2)]
        mV = [[sb(f"mV{i}{m}", [P, NB, P], F32, ph) for m in range(2)] for i in range(2)]
        mVT = [sb(f"mVT{m}", [P, S], F32, ph) for m in range(2)]
        ph.close()

        ph = ExitStack()
        DF = attention_buffers(ph, "d", 2, True)
        dQ = [sb(f"dQ{i}", [P, S], F32, ph) for i in range(2)]
        dK = [sb(f"dK{i}", [P, S], F32, ph) for i in range(2)]
        dV = [sb(f"dV{i}", [P, NB, P], F32, ph) for i in range(2)]
        dVT = sb("dVT", [P, S], F32, ph)
        dB = sb("dB", [P, S], F32, ph)
        dO = [sb(f"dO{i}", [P, S], F32, ph) for i in range(2)]
        ph.close()

        ph = ExitStack()
        EY = sb("EY", [P, KD, S], F32, ph)
        ec = sb("ec", [P, S], F32, ph)
        ez = sb("ez", [P, 2 + S], F32, ph)
        eu = [sb(f"eu{i}", [P, PADW + S], F32, ph) for i in range(3)]
        EP = sb("EP", [P, 4, S], F32, ph)
        EPH = sb("EPH", [P, 4, S], F32R, ph)
        EPL = sb("EPL", [P, 4, S], F32R, ph)
        ph.close()

        ph = ExitStack()
        lf_stack = ExitStack()
        lfz, lfa, lfe, lfu, lfl, lfd, lfi, lfr = (sb(f"lf{n}", [8, S], F32, lf_stack) for n in "zaeuldir")
        lf_stack.close()
        FO = attention_buffers(ph, "f", 1, True)
        fQ = [sb(f"fQ{i}", [P, S], F32, ph) for i in range(2)]
        fK = [sb(f"fK{i}", [P, S], F32, ph) for i in range(2)]
        fV = [sb(f"fV{i}", [P, NB, P], F32, ph) for i in range(2)]
        fVT = sb("fVT", [P, S], F32, ph)
        fB = [sb(f"fB{m}", [P, S], F32, ph) for m in range(2)]
        fBD = [sb(f"fBD{m}", [P, NB, P], F32, ph) for m in range(2)]
        fz = [sb(f"fz{i}", [P, PADC + S], F32, ph) for i in range(4)]
        fsig = sb("fsig", [P, S], F32, ph)
        cum = sb("cum", [8, S], F32, ph)
        ph.close()

        bank = [ctx.enter_context(nc.psum_tensor(f"bank{i}", [P, S], F32)) for i in range(8)]

        par_in = sem("par_in")
        raw_ready = [sem(f"raw_ready{i}") for i in range(2)]
        hi_ready = sem("hi_ready")
        lo_ready = sem("lo_ready")
        w_used = sem("w_used")
        tile_done = sem("tile_done")
        tile_free = sem("tile_free")
        gate_done = sem("gate_done")
        aux_done = sem("aux_done")
        aux_free = sem("aux_free")
        exp_done = sem("exp_done")
        p_ready = sem("p_ready")
        src_ready = sem("src_ready")
        act_hi = sem("act_hi")
        act_lo = sem("act_lo")
        x_final = sem("x_final")
        norm_in = sem("norm_in")
        norm_out = sem("norm_out")
        var_ready = sem("var_ready")
        root_ready = sem("root_ready")
        latent_lo = sem("latent_lo")
        first_in = [sem(f"first_in{k}") for k in range(KD)]
        first_hi = sem("first_hi")
        first_lo = sem("first_lo")
        x_split = sem("x_split")
        rope_ready = sem("rope_ready")
        cum_ready = sem("cum_ready")
        mem_ready = sem("mem_ready")
        small_dve = sem("small_dve")
        small_act = sem("small_act")
        small_pe = sem("small_pe")
        step = sem("step")
        stored = sem("stored")

        block = ctx.enter_context(nc.Block())

        @block.sync
        def _(sp):
            chunk = 3 * P
            for k in range(KD):
                sp.dma_start(raw[0][:, k * chunk:(k + 1) * chunk], w["mla_in"][0, :, k * chunk:(k + 1) * chunk])\
                  .then_inc(first_in[k], 16)
                sp.dma_start(X[:, k, :], xT[k]).then_inc(first_in[k], 16)
                if k == 1:
                    sp.dma_start(raw[1][:, 0:3072], w["mla_in"][1]).then_inc(raw_ready[1], 16)
            sp.dma_start(parm[:], par).then_inc(par_in, 16)
            sp.dma_start(cons[:], con).then_inc(par_in, 16)
            sp.dma_start(rtab[:], rcon).then_inc(par_in, 16)
            unit = Count()
            unit.add(2)

            def load(src, size):
                s = unit.n % 2
                if unit.n >= 2:
                    sp.wait_ge(lo_ready, unit.at(-1))
                sp.dma_start(raw[s][:, 0:size], src).then_inc(raw_ready[s], 16)
                unit.add()

            def load_all(name, n, size, i0=0):
                with counted_loop(sp, n // 2, {unit: 2}) as it:
                    for j in range(2):
                        load(w[name][bass.ds(it * 2 + (i0 + j), 1), :, 0:size].rearrange("o p n -> (o p) n"), size)

            for name, sizes in STREAM:
                if sizes is None:
                    for half in range(2):
                        load_all(name + "_gu", HID[half], 2048, HID[0] * half)
                        load_all(f"{name}_d{half}", 4, 256 * HID[half])
                elif len(sizes) == 8:
                    load_all(name, 8, sizes[0])
                else:
                    for i, size in enumerate(sizes):
                        if (name, i) not in (("mla_in", 0), ("mla_in", 1)):
                            load(w[name][i, :, 0:size], size)
            for j in range(KD):
                sp.wait_ge(x_final, 7 * KD + j + 1)
                sp.dma_start(outT[j], X[:, j, :]).then_inc(stored, 16)
            sp.wait_ge(stored, 16 * KD)

        @block.scalar
        def _(act):
            unit, tiles, srcs, auxf, gates, small = (Count() for _ in range(6))

            def split_w(size):
                s = unit.n % 2
                arrived = unit.n // 2 * 16 + 16 * s
                if unit.reg is not None:
                    arrived = unit.reg * 16 + arrived
                act.wait_ge(raw_ready[s], arrived)
                if unit.n >= 2:
                    act.wait_ge(w_used, unit.at(-1))
                act.copy(whi[s][:, 0:size], raw[s][:, 0:size]).then_inc(hi_ready, 1)
                unit.add()

            def split_x(dst, src):
                act.wait_ge(src_ready, srcs.at(1))
                act.copy(dst, src).then_inc(act_hi, 1)
                srcs.add()

            def split_at(dst, src, sem_, value):
                act.wait_ge(sem_, value)
                act.copy(dst, src).then_inc(act_hi, 1)

            def scale_shift(j, norm):
                g, b = pcol("ln_g", KD * norm + j), pcol("ln_b", KD * norm + j)
                act.wait_ge(src_ready, srcs.at(1))
                if norm != LAST_NORM:
                    act.activation(XH[:, j, :], X[:, j, :], ACT.Identity, bias=b, scale=g).then_inc(act_hi, 1)
                act.activation(X[:, j, :], X[:, j, :], ACT.Identity, bias=b, scale=g).then_inc(x_final, 1)
                srcs.add()

            def layer_norm(norm):
                for j in range(KD):
                    scale_shift(j, norm)

            def ffn(next_size):
                for half in range(2):
                    n = HID[half]

                    def gu_unit(size, hidden):
                        split_w(size)
                        i = gates.n % 2
                        act.wait_ge(tile_done, tiles.at(1))
                        if gates.n >= 2:
                            act.wait_ge(tile_free, tiles.at(-2))
                        act.activation(sil[i][:], bank[2 * i][:], ACT.Silu).then_inc(gate_done, 1)
                        gates.add()
                        tiles.add(2)
                        act.wait_ge(tile_free, tiles.at())
                        act.copy(hidden, hf[i][:]).then_inc(act_hi, 1)

                    with counted_loop(act, (n - 2) // 2, {unit: 2, gates: 2, tiles: 4}) as it:
                        for j in range(2):
                            gu_unit(2048, HH[:, bass.ds(it * 2 + j, 1), :].rearrange("p o n -> p (o n)"))
                    for j in range(n - 2, n):
                        gu_unit(2048 if j < n - 1 else 256 * n, HH[:, j, :])
                    for u in range(4):
                        if u < 3:
                            split_w(256 * n)
                        elif half == 0:
                            split_w(2048)
                        elif next_size:
                            split_w(next_size)
                        tiles.add(2)

            def out_projection(next_size):
                for size in (OUT3[1], OUT3[2], next_size):
                    split_w(size)
                tiles.add(8)

            chunk = 3 * P
            for k in range(KD):
                act.wait_ge(first_in[k], 32)
                act.copy(whi[0][:, k * chunk:(k + 1) * chunk], raw[0][:, k * chunk:(k + 1) * chunk])\
                   .then_inc(first_hi if k < KD - 1 else hi_ready, 1)
            unit.add()

            split_w(3072)
            act.wait_ge(small_pe, 1)
            act.activation(lam[:, 4:6], bank[4][:, 0:2], ACT.Exp).then_inc(small_act, 1)
            small.add()
            split_w(1024)
            for j in range(3):
                split_x(CH[:, j, :], Cf[:, j, :])
            split_w(2560)
            for j in range(3, 5):
                split_x(CH[:, j, :], Cf[:, j, :])
            tiles.add(7)

            def exp_rows(A, i, m, qb, col):
                act.wait_ge(aux_free, auxf.at(1))
                row = A["L"][i][m][:, 0:(qb + 1) * P]
                act.activation(row, row, ACT.Exp, bias=A["negmax"][:, col:col + 1], scale=-1.0,
                               accum_out=A["rowsum"][:, col:col + 1]).then_inc(exp_done, 1)
                auxf.add()

            split_w(2560)
            tiles.add(8)
            auxf.add(2)
            for p in range(4):
                for j in range(8):
                    exp_rows(ML, j % 2, 0, j % 4, j % 2)
                    if j == 1 and p < 3:
                        split_w(2560 if p < 2 else OUT3[0])
                    if j == 5:
                        auxf.add()
                        split_at(XH[:, 2 * p, :], sq[0][:], aux_free, auxf.at())
                    if j > 0:
                        auxf.add()
                auxf.add()
                if p < 3:
                    auxf.add(2)
                    tiles.add(8)
                auxf.add()
                split_at(XH[:, 2 * p + 1, :], sq[1][:], aux_free, auxf.at())
            out_projection(2048)
            layer_norm(0)
            ffn(3072)
            layer_norm(2)

            split_w(3072)
            tiles.add(3)
            auxf.add()

            def diff_head(s, first, last):
                for j in range(4):
                    for m in range(2):
                        exp_rows(DF, j % 2, m, j, 2 * (j % 2) + m)
                    if j == 0 and not last:
                        split_w(3072)
                    if j > 0:
                        auxf.add()
                    if last:
                        for k in ((0, 1), (2, 3), (4, 5), (6,))[j]:
                            split_x(XH[:, k, :], DF["Y"][:, k, :])
                auxf.add()
                if not last:
                    auxf.add()
                    tiles.add(3)
                auxf.add()

            diff_head(0, True, False)
            with counted_loop(act, 3, {unit: 2, tiles: 6, auxf: 28}):
                diff_head(1, False, False)
                diff_head(0, False, False)
            diff_head(1, False, True)
            split_x(XH[:, 7, :], DF["Y"][:, 7, :])
            out_projection(2048)
            layer_norm(1)
            ffn(2048)
            layer_norm(3)

            for u in range(8):
                split_w(2048 if u < 7 else 512)
                tiles.add(2)
            for j in range(4):
                split_x(EPH[:, j, :], EP[:, j, :])
            for j in range(4):
                split_at(XH[:, j, :], EY[:, j, :], tile_free, tiles.at())
            split_w(OUT3[0])
            for j in range(4):
                split_at(XH[:, 4 + j, :], EY[:, 4 + j, :], tile_free, tiles.at(j + 1))
            tiles.add(4)
            out_projection(2048)
            layer_norm(4)
            ffn(1024)
            layer_norm(6)

            split_w(2048)
            tiles.add(1)
            act.wait_ge(tile_free, tiles.at())
            act.activation(lfa[:], lfz[:], ACT.Abs).then_inc(small_act, 1)
            small.add()
            act.wait_ge(small_act, small.at())
            act.activation(lfe[:], lfa[:], ACT.Exp, scale=-1.0).then_inc(small_act, 1)
            act.wait_ge(small_dve, 2)
            act.activation(lfl[:], lfu[:], ACT.Ln).then_inc(small_act, 1)
            small.add(2)
            for i in range(4):
                split_w(2048 if i < 3 else 3072)
                act.wait_ge(tile_done, tiles.at(2))
                if i:
                    act.wait_ge(tile_free, tiles.at())
                act.activation(fsig[:], bank[(2 * i + 1) % 4][:], ACT.Sigmoid).then_inc(gate_done, 1)
                gates.add()
                tiles.add(2)
            split_w(3072)
            tiles.add(3)
            auxf.add()
            for g in range(4):
                auxf.add(3 if g == 1 else 2)
                for j in range(8):
                    exp_rows(FO, j % 2, 0, j % 4, j % 2)
                    if j == 1 and g < 3:
                        split_w(3072)
                    if g == 3 and j < 3:
                        split_at(XH[:, j, :], FO["Y"][:, j, :], tile_free, tiles.at())
                    if j == 5:
                        auxf.add()
                    if j > 0:
                        auxf.add()
                auxf.add()
                if g < 3:
                    auxf.add()
                    tiles.add(3)
                auxf.add()
                if g == 3:
                    split_at(XH[:, 3, :], FO["Y"][:, 3, :], aux_free, auxf.at())
            for i in range(4):
                act.wait_ge(src_ready, srcs.at(1))
                srcs.add()
                act.activation(FO["Y"][:, 4 + i, :], FO["Y"][:, 4 + i, :], ACT.Silu, bias=pcol("cn_b", i),
                               scale=pcol("cn_g", i)).then_inc(small_act, 1)
                small.add()
                split_at(XH[:, 4 + i, :], FO["Y"][:, 4 + i, :], small_act, small.at())
            out_projection(2048)
            layer_norm(5)
            ffn(0)
            layer_norm(7)

        @block.gpsimd
        def _(pool):
            unit, his = Count(), Count()

            def split_w(size):
                s = unit.n % 2
                pool.wait_ge(hi_ready, unit.at(1))
                pool.tensor_tensor(wlo[s][:, 0:size], raw[s][:, 0:size], whi[s][:, 0:size].bitcast(F32),
                                   ALU.subtract).then_inc(lo_ready, 1)
                unit.add()

            def split_x(dst, src, hi):
                pool.wait_ge(act_hi, his.at(1))
                pool.tensor_tensor(dst, src, hi.bitcast(F32), ALU.subtract).then_inc(act_lo, 1)
                his.add()

            finals, vars_ = Count(), Count()

            def inverse_root():
                vars_.add()
                pool.wait_ge(var_ready, vars_.at())
                pool.tensor_tensor(root[:], st[:, 2 * NB:3 * NB], neg_half[:], ALU.pow).then_inc(root_ready, 1)

            def layer_norm(split=True):
                inverse_root()
                for j in range(KD if split else 0):
                    pool.wait_ge(x_final, finals.at(1))
                    pool.tensor_tensor(XL[:, j, :], X[:, j, :], XH[:, j, :].bitcast(F32), ALU.subtract).then_inc(act_lo, 1)
                    finals.add()
                    his.add()

            def ffn(next_size):
                for half in range(2):
                    n = HID[half]
                    with counted_loop(pool, (n - 2) // 2, {unit: 2, his: 2}) as it:
                        for j in range(2):
                            split_w(2048)
                            t = bass.ds(j + it * 2, 1)
                            split_x(HL[:, t, :].rearrange("p o n -> p (o n)"), hf[j][:],
                                    HH[:, t, :].rearrange("p o n -> p (o n)"))
                    for j in range(n - 2, n):
                        split_w(2048 if j < n - 1 else 256 * n)
                        split_x(HL[:, j, :], hf[j % 2][:], HH[:, j, :])
                    for u in range(4):
                        if u < 3:
                            split_w(256 * n)
                        elif half == 0:
                            split_w(2048)
                        elif next_size:
                            split_w(next_size)

            pool.memset(ones[:], 1.0)
            pool.memset(neg_half[:], -0.5)
            for i, n in enumerate(COUNTS):
                pool.memset(inverse[:, i:i + 1], 1.0 / n).then_inc(mem_ready, 1)
            chunk = 3 * P
            for k in range(KD):
                part = slice(k * chunk, (k + 1) * chunk)
                if k < KD - 1:
                    pool.wait_ge(first_hi, k + 1)
                else:
                    pool.wait_ge(hi_ready, 1)
                pool.tensor_tensor(wlo[0][:, part], raw[0][:, part], whi[0][:, part].bitcast(F32), ALU.subtract)\
                    .then_inc(first_lo if k < KD - 1 else lo_ready, 1)
            unit.add()
            split_w(3072)
            split_w(1024)
            inverse_root()
            inverse_root()
            his.add(5)
            split_w(2560)
            split_w(2560)
            for p in range(4):
                if p < 3:
                    split_w(2560 if p < 2 else OUT3[0])
                for m in range(2):
                    split_x(XL[:, 2 * p + m, :], sq[m][:], XH[:, 2 * p + m, :])

            def out_projection(next_size):
                for size in (OUT3[1], OUT3[2], next_size):
                    split_w(size)

            out_projection(2048)
            layer_norm()
            ffn(3072)
            layer_norm()
            split_w(3072)
            split_w(3072)
            with counted_loop(pool, 3, {unit: 2, vars_: 2}):
                inverse_root()
                split_w(3072)
                inverse_root()
                split_w(3072)
            for j in range(6):
                split_x(XL[:, j, :], DF["Y"][:, j, :], XH[:, j, :])
                if j == 1:
                    inverse_root()
            split_x(XL[:, 6, :], DF["Y"][:, 6, :], XH[:, 6, :])
            inverse_root()
            split_x(XL[:, 7, :], DF["Y"][:, 7, :], XH[:, 7, :])
            out_projection(2048)
            layer_norm()
            ffn(2048)
            layer_norm()
            for u in range(8):
                split_w(2048 if u < 7 else 512)
            for j in range(4):
                split_x(EPL[:, j, :], EP[:, j, :], EPH[:, j, :])
            for j in range(KD):
                if j == 4:
                    split_w(OUT3[0])
                split_x(XL[:, j, :], EY[:, j, :], XH[:, j, :])
            out_projection(2048)
            layer_norm()
            ffn(1024)
            layer_norm()
            split_w(2048)
            for i in range(4):
                split_w(2048 if i < 3 else 3072)
            split_w(3072)
            for g in range(3):
                split_w(3072)
            for j in range(4):
                split_x(XL[:, j, :], FO["Y"][:, j, :], XH[:, j, :])
            inverse_root()
            for j in range(4, KD):
                split_x(XL[:, j, :], FO["Y"][:, j, :], XH[:, j, :])
            out_projection(2048)
            layer_norm()
            ffn(0)
            layer_norm(split=False)

        @block.tensor
        def _(pe):
            unit, tiles, los, aux, ins_, roots, probs = (Count() for _ in range(7))
            last = {b: 0 for b in range(4, 8)}
            fresh = [False]

            def begin_unit():
                pe.wait_ge(lo_ready, unit.at(1))
                s = unit.n % 2
                fresh[0] = unit.n > 0
                unit.add()
                return s

            def product(out, s, off, xh, xl, start, stop):
                ins = pe.matmul(out, whi[s][:, off:off + P], xh, start=start, stop=False)
                if fresh[0]:
                    ins.then_inc(w_used, 1)
                    fresh[0] = False
                pe.matmul(out, whi[s][:, off:off + P], xl, start=False, stop=False)
                return pe.matmul(out, wlo[s][:, off:off + P], xh, start=False, stop=stop)

            def claim(lag):
                if tiles.n >= lag:
                    pe.wait_ge(tile_free, tiles.at(1 - lag))

            def tile(s, b, offs, xh, xl, lag=4, wait_x=False):
                claim(lag)
                for k, off in enumerate(offs):
                    if wait_x:
                        pe.wait_ge(act_lo, los.at(k + 1))
                    ins = product(bank[b][:], s, off, xh[:, k, :], xl[:, k, :], k == 0, k == len(offs) - 1)
                ins.then_inc(tile_done, 1)
                tiles.add()

            def begin_together():
                s = begin_unit()
                pe.wait_ge(tile_free, tiles.at())
                return s

            def together(s, nt, ks, depth=KD):
                for k in ks:
                    pe.wait_ge(act_hi, los.at(k + 1 + LATENTS))
                    for which in (whi, wlo):
                        for t in range(nt):
                            ins = pe.matmul(bank[t][:], which[s][:, (k * nt + t) * P:(k * nt + t + 1) * P], XH[:, k, :],
                                            start=k == 0 and which is whi, stop=False)
                            if fresh[0]:
                                ins.then_inc(w_used, 1)
                                fresh[0] = False
                    pe.wait_ge(act_lo, los.at(k + 1))
                    for t in range(nt):
                        ins = pe.matmul(bank[t][:], whi[s][:, (k * nt + t) * P:(k * nt + t + 1) * P], XL[:, k, :],
                                        start=False, stop=k == depth - 1)
                        if k == depth - 1:
                            ins.then_inc(tile_done, 1)
                if ks and ks[-1] == depth - 1:
                    tiles.add(nt)
                    los.add(depth)

            def unit_tiles(nt, b0, xh=XH, xl=XL, depth=KD):
                s = begin_unit()
                for t in range(nt):
                    tile(s, (b0 + t) % 4, [(k * nt + t) * P for k in range(depth)], xh, xl)

            def out_projection(s, ks):
                together(s, 3, ks)
                s = begin_unit()
                for t in range(3):
                    tile(s, (3, 0, 1)[t], [(k * 3 + t) * P for k in range(KD)], XH, XL)
                    if t == 0:
                        first_mean()
                unit_tiles(2, 2)

            def first_mean():
                pe.wait_ge(tile_free, tiles.at(1 - SHIFT_FROM))
                pe.matmul(bank[6][:], ones[:], X[:, 0, :], start=True, stop=True).then_inc(norm_out, 1)

            def from_dve():
                ins_.add()
                pe.wait_ge(norm_in, ins_.at())

            def column_sums(b, col, src, n):
                i = COUNTS.index(n)
                for q in range(NB):
                    ins = pe.matmul(bank[b][:, col + q:col + q + 1], src[:, q * P:(q + 1) * P], inverse[:, i:i + 1],
                                    start=True, stop=True)
                return ins

            def spread(b, src):
                for q in range(NB):
                    ins = pe.matmul(bank[b][:, q * P:(q + 1) * P], src[:, q:q + 1].to_broadcast([P, P]), ident,
                                    start=True, stop=True)
                ins.then_inc(norm_out, 1)

            def spread_root(b):
                roots.add()
                pe.wait_ge(root_ready, roots.at())
                spread(b, root)

            def layer_norm(T=X, n=KD):
                from_dve()
                if T is not X:
                    from_dve()
                column_sums(7, 0, sq[0], n * P)
                column_sums(7, NB, sq[1], n * P).then_inc(norm_out, 1)
                if T is X:
                    pe.wait_ge(tile_free, tiles.at())
                column_sums(5, 0, T[:, n - 1, :], n * P)
                if T is X:
                    from_dve()
                column_sums(5, NB, sqt, n * P).then_inc(norm_out, 1)
                spread_root(6)
                from_dve()
                spread(7, st[:, 3 * NB:4 * NB])

            def mean_squares(b, src, n):
                from_dve()
                column_sums(b, 0, src, n).then_inc(norm_out, 1)

            def ffn():
                for half in range(2):
                    n = HID[half]
                    if half == 0:
                        s = begin_together()
                        together(s, 2, range(KD))
                        unit_tiles(2, 2)
                        trips = (n - 2) // 2
                    else:
                        trips = n // 2
                    with counted_loop(pe, trips, {unit: 2, tiles: 4}):
                        unit_tiles(2, 0)
                        unit_tiles(2, 2)

                    def down_unit(j, wait_x=False):
                        s = begin_unit()
                        for t in range(2):
                            tile(s, 2 * j + t, [(k * 2 + t) * P for k in range(n)], HH, HL, wait_x=wait_x and t == 0)

                    for u in range(4):
                        down_unit(u % 2, u == 0)
                        if half == 1 and u == 1:
                            first_mean()
                    los.add(n)

            def aux_claim(b):
                if last[b] > 0:
                    pe.wait_ge(aux_free, aux.at(last[b] - aux.n))

            def aux_end(ins, b):
                ins.then_inc(aux_done, 1)
                aux.add()
                last[b] = aux.n

            def transposes(dst_bank, src, n, ready, value):
                pe.wait_ge(ready, value)
                aux_claim(dst_bank)
                for b in range(n):
                    ins = pe.transpose(bank[dst_bank][:, b * P:(b + 1) * P], src[:, b * P:(b + 1) * P], ident)
                aux_end(ins, dst_bank)

            def steps(s, slot, depth, offset, xh, xl, banks, lag, xbase=None):
                for t, k in slot:
                    if k == 0:
                        claim(lag)
                    kx = k + (xbase[t] if xbase else 0)
                    ins = product(bank[banks[t]][:], s, offset(t, k), xh[:, kx, :], xl[:, kx, :], k == 0, k == depth[t] - 1)
                    if k == depth[t] - 1:
                        ins.then_inc(tile_done, 1)
                        tiles.add()

            def value_product(A, v, rows, cols, behind):
                pe.wait_ge(aux_free, aux.at(-behind))
                aux_claim(7)
                for kb in range(NB):
                    ins = pe.matmul(bank[7][rows, kb * P:S], v[:, kb, cols], A["PT"][:, kb, kb * P:S],
                                    start=kb == 0, stop=kb == NB - 1)
                aux_end(ins, 7)

            for k in range(KD):
                pe.wait_ge(x_split, k + 1)
                if k < KD - 1:
                    pe.wait_ge(first_lo, k + 1)
                else:
                    pe.wait_ge(lo_ready, 1)
                for t in range(3):
                    ins = product(bank[t][:], 0, (k * 3 + t) * P, XH[:, k, :], XL[:, k, :], k == 0, k == KD - 1)
                    if k == KD - 1:
                        ins.then_inc(tile_done, 1)
            unit.add()
            tiles.add(3)
            pe.wait_ge(mem_ready, len(COUNTS))
            pe.wait_ge(small_dve, 1)
            pe.matmul(bank[4][:, 0:2], ones[:], lam[:, 0:2], start=True, stop=True).then_inc(small_pe, 1)
            s = begin_unit()
            for t in range(3):
                tile(s, (3, 0, 1)[t], [(k * 3 + t) * P for k in range(KD)], XH, XL)
                if t == 1:
                    mean_squares(5, sq[1], QR)
            spread_root(6)
            mean_squares(5, sq[0], KVR)
            s = begin_unit()
            claim(4)
            for k in range(KD):
                if k == KD // 2:
                    spread_root(7)
                ins = product(bank[2][:], s, k * P, XH[:, k, :], XL[:, k, :], k == 0, k == KD - 1)
            ins.then_inc(tile_done, 1)
            tiles.add()

            def mla_offset(t, k):
                return k * 4 * P + t * P if t < 4 else 3 * 4 * P + k * 4 * P + (t - 4) * P

            def mla_steps(s, slot, lag=4):
                steps(s, slot, MLA_K, mla_offset, CH, CL, (0, 1, 2, 3, 0, 1, 2, 3), lag, (0, 0, 0, 0, 3, 3, 3, 3))

            def mla_values():
                transposes(6, mVT[0], NB, tile_free, tiles.at(-2))
                transposes(6, mVT[1], NB, tile_free, tiles.at())

            s = begin_unit()
            pe.wait_ge(latent_lo, 3)
            for n_slot, slot in enumerate(MLA_SLOTS):
                if slot == MLA_SLOTS[4]:
                    pe.wait_ge(latent_lo, 5)
                mla_steps(s, slot, 3)
            mla_values()
            for p in range(4):
                i = p % 2
                pe.wait_ge(tile_free, tiles.at())
                pe.wait_ge(rope_ready, p + 2)
                s = begin_unit()
                for j in range(8):
                    m, qb = j // 4, j % 4
                    b, n = 4 + j % 2, (qb + 1) * P
                    aux_claim(b)
                    pe.matmul(bank[b][:, 0:n], mQN[i][m][:, qb * P:n], mKN[i][m][:, 0:n], start=True, stop=False)
                    half = slice(64 * m, 64 * m + 64)
                    aux_end(pe.matmul(bank[b][:, 0:n], mQR[i][half, qb * P:n], KR[half, 0:n], start=False, stop=True), b)
                    if p < 3:
                        mla_steps(s, MLA_SLOTS[j])
                    else:
                        together(s, 3, OUT_MLA[j])
                    if j == 5:
                        value_product(ML, mV[i][0], slice(0, P), slice(0, P), 1)
                    if j > 0:
                        probs.add()
                        transposes(6, ML["L"][(j - 1) % 2][0], (j - 1) % 4 + 1, p_ready, probs.at())
                if p < 3:
                    mla_steps(s, MLA_SLOTS[8])
                else:
                    together(s, 3, OUT_MLA[8])
                probs.add()
                transposes(6, ML["L"][1][0], NB, p_ready, probs.at())
                if p < 3:
                    mla_values()
                value_product(ML, mV[i][1], slice(0, P), slice(0, P), 2 if p < 3 else 0)
            out_projection(s, OUT_MLA[-1])
            layer_norm()
            ffn()
            layer_norm()

            def head_offset(t, k):
                return (k * 3 + t) * P

            def head_steps(s, slot):
                steps(s, slot, (KD,) * 3, head_offset, XH, XL, (0, 1, 2), 3)

            def diff_head(i, first, last_one):
                pe.wait_ge(tile_free, tiles.at())
                if not first:
                    last.update({4: aux.n - 5, 5: aux.n - 4, 6: aux.n - 1, 7: aux.n})
                s = begin_unit()
                for j in range(4):
                    n = (j + 1) * P
                    for m in range(2):
                        half = slice(64 * m, 64 * m + 64)
                        aux_claim(4 + m)
                        aux_end(pe.matmul(bank[4 + m][:, 0:n], dQ[i][half, j * P:n], dK[i][half, 0:n], start=True, stop=True), 4 + m)
                    if last_one:
                        together(s, 3, OUT_DIFF[j])
                    else:
                        head_steps(s, DIFF_SLOTS[j])
                    if j > 0:
                        probs.add()
                        transposes(6, DF["L"][(j - 1) % 2][0], j, p_ready, probs.at())
                    if j == 1 and not first:
                        squares_of_head()
                    if j == 2 and not first:
                        spread_root(7)
                if last_one:
                    together(s, 3, OUT_DIFF[4])
                else:
                    head_steps(s, DIFF_SLOTS[4])
                probs.add()
                transposes(6, DF["L"][1][0], NB, p_ready, probs.at())
                if not last_one:
                    transposes(6, dVT, NB, tile_free, tiles.at())
                value_product(DF, dV[i], slice(0, P), slice(0, P), 0 if last_one else 1)
                return s

            def squares_of_head():
                aux_claim(7)
                mean_squares(7, sqt, P)

            together(begin_together(), 3, range(KD))
            transposes(6, dVT, NB, tile_free, tiles.at())
            diff_head(0, True, False)
            with counted_loop(pe, 3, {unit: 2, tiles: 6, aux: 28, ins_: 2, roots: 2, probs: 8}):
                diff_head(1, False, False)
                diff_head(0, False, False)
            s = diff_head(1, False, True)
            squares_of_head()
            together(s, 3, OUT_DIFF[-1][:-1])
            spread_root(7)
            out_projection(s, OUT_DIFF[-1][-1:])
            layer_norm()
            ffn()
            layer_norm()

            together(begin_together(), 2, range(KD))
            unit_tiles(2, 2)
            with counted_loop(pe, 3, {unit: 2, tiles: 4}):
                unit_tiles(2, 0)
                unit_tiles(2, 2)
            s = begin_unit()
            for i in range(4):
                pe.wait_ge(act_lo, los.at(i + 1))
                claim(4)
                product(bank[i][:], s, i * P, EPH[:, i, :], EPL[:, i, :], True, True).then_inc(tile_done, 1)
                tiles.add()
            los.add(4)
            out_projection(begin_together(), range(KD))
            layer_norm()
            ffn()
            layer_norm()

            together(begin_together(), 1, range(KD))
            pe.wait_ge(tile_free, tiles.at())
            for i in range(4):
                unit_tiles(2, 2 * i % 4)
            pe.wait_ge(tile_free, tiles.at())
            s = begin_unit()
            for t in range(3):
                tile(s, t, [(k * 3 + t) * P for k in range(KD)], XH, XL, 3)
            transposes(6, fVT, NB, tile_free, tiles.at())
            for g in range(4):
                i = g % 2
                if g == 0:
                    pe.wait_ge(cum_ready, 1)
                if g == 1:
                    pe.wait_ge(aux_free, aux.at())
                    aux_end(pe.matmul(bank[5][:], ones[:], FO["Y"][:, 4, :], start=True, stop=True), 5)
                for m in range(2):
                    aux_claim(6 + m)
                    aux_end(pe.matmul(bank[6 + m][:], ident[0:8, 2 * g + m:2 * g + m + 1].to_broadcast([8, P]), cum[:], start=True, stop=True), 6 + m)
                pe.wait_ge(tile_free, tiles.at())
                s = begin_unit()
                for j in range(8):
                    m, qb = j // 4, j % 4
                    b, n = 4 + j % 2, (qb + 1) * P
                    half = slice(64 * m, 64 * m + 64)
                    aux_claim(b)
                    aux_end(pe.matmul(bank[b][:, 0:n], fQ[i][half, qb * P:n], fK[i][half, 0:n], start=True, stop=True), b)
                    if g < 3:
                        head_steps(s, ODD_SLOTS[j])
                    else:
                        together(s, 3, OUT_ODD[j])
                    if j == 5:
                        value_product(FO, fV[i], slice(0, 64), slice(0, 64), 1)
                    if j > 0:
                        probs.add()
                        transposes(6, FO["L"][(j - 1) % 2][0], (j - 1) % 4 + 1, p_ready, probs.at())
                if g < 3:
                    head_steps(s, ODD_SLOTS[8])
                else:
                    together(s, 3, OUT_ODD[8])
                probs.add()
                transposes(6, FO["L"][1][0], NB, p_ready, probs.at())
                if g < 3:
                    transposes(6, fVT, NB, tile_free, tiles.at())
                value_product(FO, fV[i], slice(64, P), slice(64, P), 1 if g < 3 else 0)
            layer_norm(FO["Y"][:, 4:8, :], 4)
            out_projection(s, OUT_ODD[-1])
            layer_norm()
            ffn()
            layer_norm()

        @block.vector
        def _(dve):
            tiles, aux, los, steps, exps, gates, outs, roots, smalls = (Count() for _ in range(9))

            def link(ins):
                ins.then_inc(step, 1)
                steps.add()
                dve.wait_ge(step, steps.at())

            def take(op, n=1):
                dve.wait_ge(tile_done, tiles.at(n))
                op().then_inc(tile_free, n)
                tiles.add(n)

            def take_aux(op):
                dve.wait_ge(aux_done, aux.at(1))
                op().then_inc(aux_free, 1)
                aux.add()

            def copy_tile(dst, b):
                take(lambda: dve.tensor_copy(dst, bank[b][:]))

            def from_pe():
                outs.add()
                dve.wait_ge(norm_out, outs.at())

            def get_shift(b):
                return dve.tensor_scalar(shift[:], bank[b][:], -1.0 / P, None, ALU.mult)

            def accumulate(T, j, n):
                x = T[:, j, :]
                if j == 0:
                    link(dve.tensor_tensor(sq[1][:], x, x, ALU.mult))
                elif j < n - 1:
                    dve.tensor_tensor(sqt[:], x, x, ALU.mult).then_inc(step, 1)
                    steps.add()
                    squared = steps.at()
                    dve.tensor_tensor(sq[0][:], T[:, 0, :] if j == 1 else sq[0][:], x, ALU.add).then_inc(step, 1)
                    steps.add()
                    dve.wait_ge(step, squared)
                    ins = dve.tensor_tensor(sq[1][:], sq[1][:], sqt[:], ALU.add)
                    if j < n - 2:
                        link(ins)
                    else:
                        ins.then_inc(norm_in, 1)
                        dve.wait_ge(step, steps.at())
                else:
                    dve.tensor_tensor(sqt[:], x, x, ALU.mult).then_inc(norm_in, 1)

            def normalise_tiles(T, n, done):
                mean, square, var, nmr = (st[:, i * NB:(i + 1) * NB] for i in range(4))
                from_pe()
                link(dve.tensor_copy(st[:, 0:2 * NB], bank[7][:, 0:2 * NB]))
                from_pe()
                link(dve.tensor_tensor(st[:, 0:2 * NB], st[:, 0:2 * NB], bank[5][:, 0:2 * NB], ALU.add))
                link(dve.tensor_tensor(nmr, mean, mean, ALU.mult))
                link(dve.scalar_tensor_tensor(var, square, LN_EPS, nmr, ALU.add, ALU.subtract))
                dve.tensor_scalar(var, var, LN_EPS, None, ALU.max).then_inc(var_ready, 1)
                roots.add()
                dve.wait_ge(root_ready, roots.at())
                dve.scalar_tensor_tensor(nmr, mean, -1.0, root[:], ALU.mult, ALU.mult).then_inc(norm_in, 1)

                def mul(j):
                    dve.tensor_tensor(T[:, j, :], T[:, j, :], bank[6][:], ALU.mult).then_inc(step, 1)
                    steps.add()
                from_pe()
                mul(0)
                mul(1)
                from_pe()
                for j in range(n):
                    if j > 0 and j + 1 < n:
                        mul(j + 1)
                    dve.wait_ge(step, steps.at(-1 if j + 1 < n else 0))
                    dve.tensor_tensor(T[:, j, :], T[:, j, :], bank[7][:], ALU.add).then_inc(done, 1)

            def layer_norm():
                normalise_tiles(X, KD, src_ready)
                los.add(KD)

            def mean_square_root(b, eps):
                from_pe()
                dve.tensor_scalar(st[:, 2 * NB:3 * NB], bank[b][:, 0:NB], eps, None, ALU.add).then_inc(var_ready, 1)
                roots.add()

            def residual(scale):
                for j in range(KD):
                    x, b = X[:, j, :], j % 4
                    if j == SHIFT_FROM:
                        from_pe()
                        link(get_shift(6))
                        for i in range(SHIFT_FROM):
                            link(dve.tensor_tensor(X[:, i, :], X[:, i, :], shift[:], ALU.add))
                            accumulate(X, i, KD)
                    if j < SHIFT_FROM:
                        take(lambda: dve.scalar_tensor_tensor(x, x, scale, bank[b][:], ALU.mult, ALU.add))
                    else:
                        link(dve.scalar_tensor_tensor(x, x, scale, shift[:], ALU.mult, ALU.add))
                        take(lambda: dve.tensor_tensor(x, x, bank[b][:], ALU.add))
                        dve.wait_ge(tile_free, tiles.at())
                        accumulate(X, j, KD)

            def out_projection():
                residual(ALPHA)

            def ffn():
                for half in range(2):
                    n = HID[half]
                    with counted_loop(dve, n // 2, {tiles: 4, gates: 2, los: 2}):
                        for i in range(2):
                            dve.wait_ge(gate_done, gates.at(1))
                            dve.wait_ge(act_lo, los.at(-1))
                            take(lambda: dve.tensor_tensor(hf[i][:], sil[i][:], bank[2 * i + 1][:], ALU.mult), 2)
                            gates.add()
                            los.add()
                    if half == 0:
                        for j in range(KD):
                            take(lambda: dve.scalar_tensor_tensor(X[:, j, :], X[:, j, :], ALPHA, bank[j % 4][:], ALU.mult, ALU.add))
                    else:
                        residual(1.0)

            def logits(A, i, m, qb, col, b, bias, scale):
                n = (qb + 1) * P
                dve.wait_ge(aux_done, aux.at(1))
                if aux.reg is not None:
                    dve.memset(spare[:, qb * 2 + m:qb * 2 + m + 1], 0.0)
                aux.add()
                dve.tensor_tensor_reduce(
                    out=A["L"][i][m][:, 0:n], in0=bank[b][:, 0:n], in1=bias[:, S - n:S], scale=-scale, scalar=BIG,
                    op0=ALU.add, op1=ALU.min, accum_out=A["negmax"][:, col:col + 1]).then_inc(aux_free, 1)

            def normalise(A, i, qb, col):
                n = (qb + 1) * P
                exps.add()
                dve.wait_ge(exp_done, exps.at())
                link(dve.reciprocal(A["rinv"][:, col:col + 1], A["rowsum"][:, col:col + 1]))
                row = A["L"][i][0][:, 0:n]
                dve.tensor_scalar(row, row, A["rinv"][:, col:col + 1], None, ALU.mult).then_inc(p_ready, 1)

            def keep_transposed(A, qb):
                n = (qb + 1) * P
                take_aux(lambda: dve.tensor_copy(A["PT"][:, 0:qb + 1, qb * P:n],
                                                 bank[6][:, 0:n].rearrange("p (k q) -> p k q", q=P)))

            def keep_values(dst):
                take_aux(lambda: dve.tensor_copy(dst[:].rearrange("p k d -> p (k d)"), bank[6][:]))

            for k in range(KD):
                dve.wait_ge(first_in[k], 32)
                link(dve.tensor_copy(XH[:, k, :], X[:, k, :]))
                dve.tensor_tensor(XL[:, k, :], X[:, k, :], XH[:, k, :].bitcast(F32), ALU.subtract).then_inc(x_split, 1)
            dve.wait_ge(par_in, 48)
            dve.tensor_tensor(lam[:, 0:2], parm[:, PCOL["lam"]:PCOL["lam"] + 4:2], parm[:, PCOL["lam"] + 1:PCOL["lam"] + 4:2],
                              ALU.mult).then_inc(small_dve, 1)
            dve.tensor_scalar(gsub[:], pcol("g_sub"), 1.0 - LAMBDA_INIT, None, ALU.mult)

            cosT, sinT, maskT = (rtab[:, RCOL[n]:RCOL[n] + S] for n in ("cos", "sin", "mask"))

            def latent_squares(js, dst):
                for j in js:
                    c = Cf[:, j, :]
                    ins = dve.tensor_tensor((dst if j == js[0] else sqt)[:], c, c, ALU.mult)
                    link(ins)
                    if j > js[0]:
                        ins = dve.tensor_tensor(dst[:], dst[:], sqt[:], ALU.add)
                        if j == js[-1]:
                            ins.then_inc(norm_in, 1)
                        else:
                            link(ins)

            def latents(js, b):
                for j in js:
                    dve.scalar_tensor_tensor(Cf[:, j, :], Cf[:, j, :], pcol("g_c", j), bank[b][:], ALU.mult, ALU.mult)\
                       .then_inc(src_ready, 1)

            def low_latents(js):
                for j in js:
                    dve.wait_ge(act_hi, j + 1)
                    dve.tensor_tensor(CL[:, j, :], Cf[:, j, :], CH[:, j, :].bitcast(F32), ALU.subtract).then_inc(latent_lo, 1)

            for j in range(3):
                copy_tile(Cf[:, j, :], j)
            dve.wait_ge(tile_free, tiles.at())
            latent_squares((0, 1, 2), sq[1])
            copy_tile(Cf[:, 3, :], 3)
            copy_tile(Cf[:, 4, :], 0)
            mean_square_root(5, RMS_EPS)
            dve.wait_ge(tile_free, tiles.at())
            latent_squares((3, 4), sq[0])
            take(lambda: dve.tensor_tensor(KR[:], bank[1][:], cosT, ALU.mult))
            from_pe()
            mean_square_root(5, RMS_EPS)
            latents((0, 1, 2), 6)
            from_pe()
            latents((3, 4), 7)
            low_latents((0, 1, 2))
            take(lambda: dve.tensor_tensor(rt[:], bank[2][:], sinT, ALU.mult))
            low_latents((3, 4))
            dve.wait_ge(tile_free, tiles.at())
            dve.tensor_tensor(KR[:], KR[:], rt[:], ALU.add).then_inc(rope_ready, 1)

            def mla_tile(i, t, ropes):
                b = t % 4
                if t < 2:
                    copy_tile(mQN[i][t][:], b)
                elif t == 2:
                    take(lambda: dve.tensor_tensor(mQR[i][:], bank[b][:], cosT, ALU.mult))
                elif t == 3:
                    dve.wait_ge(rope_ready, ropes)
                    take(lambda: dve.tensor_tensor(rt[:], bank[b][:], sinT, ALU.mult))
                    dve.wait_ge(tile_free, tiles.at())
                    dve.tensor_tensor(mQR[i][:], mQR[i][:], rt[:], ALU.add).then_inc(rope_ready, 1)
                else:
                    copy_tile((mKN[i][t // 2 - 2] if t % 2 == 0 else mVT[t // 2 - 2])[:], b)

            for t in range(8):
                mla_tile(0, t, 1)
            keep_values(mV[0][0])
            keep_values(mV[0][1])
            for p in range(4):
                i, o = p % 2, (p + 1) % 2
                for j in range(8):
                    logits(ML, j % 2, 0, j % 4, j % 2, 4 + j % 2, maskT, MLA_SCALE)
                    if j > 0:
                        normalise(ML, (j - 1) % 2, (j - 1) % 4, (j - 1) % 2)
                    for t in finished(MLA_SLOTS[j], MLA_K) if p < 3 else ():
                        mla_tile(o, t, p + 2)
                    if j == 5:
                        if p:
                            dve.wait_ge(act_lo, los.at(-1))
                        take_aux(lambda: dve.tensor_copy(sq[0][:], bank[7][:]))
                        los.add()
                    if j > 0:
                        keep_transposed(ML, (j - 1) % 4)
                normalise(ML, 1, 3, 1)
                for t in finished(MLA_SLOTS[8], MLA_K) if p < 3 else ():
                    mla_tile(o, t, p + 2)
                keep_transposed(ML, 3)
                if p < 3:
                    keep_values(mV[o][0])
                    keep_values(mV[o][1])
                if p:
                    dve.wait_ge(act_lo, los.at(-1))
                take_aux(lambda: dve.tensor_copy(sq[1][:], bank[7][:]))
                los.add()
            out_projection()
            layer_norm()
            ffn()
            layer_norm()

            smalls.add()
            dve.wait_ge(small_act, smalls.at())
            link(dve.tensor_tensor(lam[:, 6:7], lam[:, 4:5], lam[:, 5:6], ALU.subtract))
            link(dve.tensor_scalar(lam[:, 7:8], lam[:, 6:7], LAMBDA_INIT, None, ALU.add))

            def scale_head(i, head):
                from_pe()
                out = DF["Y"][:, head, :] if isinstance(head, int) else \
                    DF["Y"][:, bass.ds(head, 1), :].rearrange("p o n -> p (o n)")
                dve.scalar_tensor_tensor(out, dO[i][:], gsub[:], bank[7][:], ALU.mult, ALU.mult).then_inc(src_ready, 1)

            def diff_head(i, h, first, last_one):
                o = 1 - i
                col = cons[:, CCOL["slopes"] + h:CCOL["slopes"] + h + 1] if isinstance(h, int) else \
                    cons[:, bass.ds(h + CCOL["slopes"], 1)]
                link(dve.tensor_scalar(dB[:], dist, col, None, ALU.mult))
                for j in range(4):
                    for m in range(2):
                        logits(DF, j % 2, m, j, 2 * (j % 2) + m, 4 + m, dB[:], HD_SCALE)
                    if j > 0:
                        combine(j - 1)
                    for t in finished(DIFF_SLOTS[j], (KD,) * 3) if not last_one else ():
                        copy_tile((dQ[o], dK[o], dVT)[t][:], t)
                    if j > 0:
                        keep_transposed(DF, j - 1)
                    if j == 1 and not first:
                        mean_square_root(7, RMS_EPS)
                    if j == 2 and not first:
                        scale_head(o, h - 1)
                combine(3)
                for t in finished(DIFF_SLOTS[4], (KD,) * 3) if not last_one else ():
                    copy_tile((dQ[o], dK[o], dVT)[t][:], t)
                keep_transposed(DF, 3)
                if not last_one:
                    keep_values(dV[o])
                take_aux(lambda: dve.tensor_copy(dO[i][:], bank[7][:]))
                dve.wait_ge(aux_free, aux.at())
                dve.tensor_tensor(sqt[:], dO[i][:], dO[i][:], ALU.mult).then_inc(norm_in, 1)

            def combine(j):
                n, c = (j + 1) * P, 2 * (j % 2)
                exps.add(2)
                dve.wait_ge(exp_done, exps.at())
                link(dve.reciprocal(DF["rinv"][:, c:c + 2], DF["rowsum"][:, c:c + 2]))
                p0, p1 = (DF["L"][j % 2][m][:, 0:n] for m in range(2))
                link(dve.tensor_scalar(p1, p1, DF["rinv"][:, c + 1:c + 2], lam[:, 7:8], ALU.mult, ALU.mult))
                dve.scalar_tensor_tensor(p0, p0, DF["rinv"][:, c:c + 1], p1, ALU.mult, ALU.subtract).then_inc(p_ready, 1)

            for t in range(3):
                copy_tile((dQ[0], dK[0], dVT)[t][:], t)
            keep_values(dV[0])
            diff_head(0, 0, True, False)
            with counted_loop(dve, 3, {tiles: 6, aux: 28, steps: 18, exps: 16, outs: 4, roots: 2}) as it:
                diff_head(1, it * 2 + 1, False, False)
                diff_head(0, it * 2 + 2, False, False)
            diff_head(1, 7, False, True)
            mean_square_root(7, RMS_EPS)
            scale_head(1, 7)
            los.add(KD)
            out_projection()
            layer_norm()
            ffn()
            layer_norm()

            dve.memset(ez[:, 0:2], 0.0)
            for u in eu:
                dve.memset(u[:, 0:PADW], 0.0)

            pooled = LATENTS + 5 * KD
            def conv_col(k, i):
                return pcol("conv_w", 4 * k + i)

            for i in range(4):
                b = 2 * i % 4
                copy_tile(ec[:], b)
                dve.wait_ge(tile_free, tiles.at())
                take(lambda: dve.tensor_tensor(ez[:, 2:2 + S], bank[b + 1][:], ec[:], ALU.mult))
                dve.wait_ge(tile_free, tiles.at())
                y = EY[:, i, :]
                link(dve.tensor_scalar(y, ez[:, 0:S], conv_col(0, i), None, ALU.mult))
                for k in (1, 2):
                    link(dve.scalar_tensor_tensor(y, ez[:, k:k + S], conv_col(k, i), y, ALU.mult, ALU.add))
            for i in range(4):
                b = 2 * i % 4
                take(lambda: dve.tensor_tensor(EY[:, i, :], bank[b][:], EY[:, i, :], ALU.mult))
                if i:
                    dve.wait_ge(src_ready, pooled + i)
                take(lambda: dve.tensor_copy(eu[0][:, PADW:], bank[b + 1][:]))
                dve.wait_ge(tile_free, tiles.at())
                src = eu[0]
                for d in range(i + 1):
                    dst = eu[1 + d % 2]
                    link(dve.tensor_tensor(dst[:, PADW:], src[:, PADW:], src[:, PADW - 2 ** d:PADW - 2 ** d + S], ALU.add))
                    src = dst
                link(dve.scalar_tensor_tensor(EP[:, i, PADW:], src[:, 2 * PADW:], 1.0 / WINDOWS[i], eu[0][:, 2 * PADW:], ALU.mult, ALU.subtract))
                link(dve.tensor_tensor(EP[:, i, 0:PADW], src[:, PADW:2 * PADW], cons[:, CCOL["invcnt"] + 16 * i:CCOL["invcnt"] + 16 * i + 16], ALU.mult))
                dve.tensor_tensor(EP[:, i, 0:PADW], EP[:, i, 0:PADW], eu[0][:, PADW:2 * PADW], ALU.subtract).then_inc(src_ready, 1)
            los.add(4)
            for i in range(4):
                take(lambda: dve.tensor_scalar(EY[:, 4 + i, :], bank[i][:], pcol("pool_s", i), None, ALU.mult))
            los.add(KD)
            out_projection()
            layer_norm()
            ffn()
            layer_norm()

            take(lambda: dve.tensor_scalar(lfz[:], bank[0][0:8, :], parm[0:8, PCOL["f_b"]:PCOL["f_b"] + 1], None, ALU.add))
            smalls.add(2)
            dve.wait_ge(small_act, smalls.at())
            dve.tensor_scalar(lfu[:], lfe[:], 1.0, None, ALU.add).then_inc(small_dve, 1)
            dve.wait_ge(small_dve, 2)
            link(dve.tensor_scalar(lfd[:], lfu[:], 1.0, None, ALU.subtract))
            link(dve.tensor_scalar(lfi[:], lfd[:], 0.0, None, ALU.is_equal))
            link(dve.tensor_tensor(lfd[:], lfd[:], lfi[:], ALU.add))
            link(dve.reciprocal(lfr[:], lfd[:]))
            link(dve.tensor_tensor(lfr[:], lfe[:], lfr[:], ALU.mult))
            smalls.add()
            dve.wait_ge(small_act, smalls.at())
            link(dve.tensor_tensor(lfr[:], lfl[:], lfr[:], ALU.mult))
            link(dve.tensor_tensor(lfi[:], lfi[:], lfe[:], ALU.mult))
            link(dve.tensor_tensor(lfr[:], lfr[:], lfi[:], ALU.add))
            link(dve.tensor_scalar(lfz[:], lfz[:], 0.0, None, ALU.min))
            link(dve.tensor_tensor(lfz[:], lfz[:], lfr[:], ALU.subtract))
            link(dve.memset(lfd[:], 0.0))
            dve.tensor_tensor_scan(cum[:], lfz[:], lfd[:], 0.0, ALU.add, ALU.add).then_inc(cum_ready, 1)

            for i in range(4):
                dve.memset(fz[i][:, 0:PADC], 0.0)
            for i in range(4):
                dve.wait_ge(gate_done, gates.at(1))
                gates.add()
                take(lambda: dve.tensor_tensor(fz[i][:, PADC:], fsig[:], bank[2 * i % 4][:], ALU.mult), 2)

            def taps(i, first, n):
                y = FO["Y"][:, 4 + i, :]
                for k in range(first, first + n):
                    wk = pcol("dw_w", 4 * k + i)
                    if k == 0:
                        link(dve.tensor_scalar(y, fz[i][:, 0:S], wk, pcol("dw_b", i), ALU.mult, ALU.add))
                    else:
                        link(dve.scalar_tensor_tensor(y, fz[i][:, k:k + S], wk, y, ALU.mult, ALU.add))

            def forget_logits(i, m, qb, col, b):
                n0 = qb * P
                dve.wait_ge(aux_done, aux.at(1))
                first = BIG
                if qb:
                    first = FO["negmax"][:, 2 + col:3 + col]
                    link(dve.tensor_tensor_reduce(
                        out=FO["L"][i][0][:, 0:n0], in0=bank[b][:, 0:n0], in1=fB[m][:, 0:n0], scale=-HD_SCALE, scalar=BIG,
                        op0=ALU.add, op1=ALU.min, accum_out=first))
                take_aux(lambda: dve.tensor_tensor_reduce(
                    out=FO["L"][i][0][:, n0:n0 + P], in0=bank[b][:, n0:n0 + P], in1=fBD[m][:, qb, :], scale=-HD_SCALE,
                    scalar=first, op0=ALU.add, op1=ALU.min, accum_out=FO["negmax"][:, col:col + 1]))

            C = FO["Y"][:, 4:8, :]
            for t in range(3):
                copy_tile((fQ[0], fK[0], fVT)[t][:], t)
            keep_values(fV[0])
            for g in range(4):
                o = (g + 1) % 2
                if g == 1:
                    take_aux(lambda: get_shift(5))
                    dve.wait_ge(aux_free, aux.at())
                    link(dve.tensor_tensor(C[:, 0, :], C[:, 0, :], shift[:], ALU.add))
                    accumulate(C, 0, 4)
                for m in range(2):
                    take_aux(lambda: dve.tensor_scalar(fB[m][:], bank[6 + m][:], -1.0 / HD_SCALE, None, ALU.mult))
                    dve.wait_ge(aux_free, aux.at())
                    link(dve.tensor_tensor(fBD[m][:], fB[m][:].rearrange("p (k q) -> p k q", q=P),
                                           causal.unsqueeze(1).to_broadcast([P, NB, P]), ALU.add))
                for j in range(8):
                    forget_logits(j % 2, j // 4, j % 4, j % 2, 4 + j % 2)
                    if j > 0:
                        normalise(FO, (j - 1) % 2, (j - 1) % 4, (j - 1) % 2)
                    for t in finished(ODD_SLOTS[j], (KD,) * 3) if g < 3 else ():
                        copy_tile((fQ[o], fK[o], fVT)[t][:], t)
                    if j == 5:
                        take_aux(lambda: dve.tensor_copy(FO["Y"][0:64, g, :], bank[7][0:64, :]))
                    if j > 0:
                        keep_transposed(FO, (j - 1) % 4)
                    taps(g, 4 * j, min(4, TAPS - 4 * j))
                normalise(FO, 1, 3, 1)
                for t in finished(ODD_SLOTS[8], (KD,) * 3) if g < 3 else ():
                    copy_tile((fQ[o], fK[o], fVT)[t][:], t)
                keep_transposed(FO, 3)
                if g < 3:
                    keep_values(fV[o])
                take_aux(lambda: dve.tensor_copy(FO["Y"][64:P, g, :], bank[7][64:P, :]))
                if g:
                    link(dve.tensor_tensor(C[:, g, :], C[:, g, :], shift[:], ALU.add))
                    accumulate(C, g, 4)
            normalise_tiles(C, 4, src_ready)
            los.add(KD)
            out_projection()
            layer_norm()
            ffn()
            layer_norm()


def host_layout(inp):
    f = lambda a: np.asarray(a)

    def ktiles(m):
        return m.reshape(m.shape[0] // P, P, m.shape[1]).transpose(1, 0, 2)

    def unit(m, size=None):
        u = ktiles(m).reshape(P, -1)
        return u if size is None or u.shape[1] == size else np.pad(u, ((0, 0), (0, size - u.shape[1])))

    def out3(m):
        return np.stack([unit(m[:, 0:384]), unit(m[:, 384:768]), unit(m[:, 768:1024], 3072)])

    w = {}
    swap = np.r_[32:64, 0:32]
    win = f(inp["mla_w_in"])[0]
    kr = win[:, 640:704]
    w["mla_in"] = np.stack([unit(win[:, 0:384]), unit(np.concatenate([win[:, 384:640], kr, kr], 1)),
                            unit(np.concatenate([kr[:, swap]] * 2, 1), 3072)])
    uq, ukv = f(inp["mla_w_uq"])[0].reshape(QR, 8, 192), f(inp["mla_w_ukv"])[0]
    pairs = []
    for p in range(4):
        a, b = uq[:, 2 * p], uq[:, 2 * p + 1]
        ra, rb = a[:, 128:], b[:, 128:]
        q = np.concatenate([a[:, :128], b[:, :128], ra, rb, ra[:, swap], rb[:, swap]], 1)
        pairs.append(np.concatenate([unit(q), unit(ukv[:, 512 * p:512 * p + 512])], 1))
    w["mla_pair"] = np.stack(pairs)
    w["mla_o"] = out3(f(inp["mla_w_o"])[0])
    ffns = [(f(inp["ffn_w_gu"])[i], f(inp["ffn_w_down"])[i]) for i in range(2)] + \
           [(f(inp["ffn_w_in_2"])[i], f(inp["ffn_w_out_2"])[i]) for i in range(2)]
    for i, (gu, down) in enumerate(ffns):
        g = gu.reshape(KD, P, 2, D_FF // P, P).transpose(3, 1, 0, 2, 4)
        w[f"ffn{i}_gu"] = g.reshape(D_FF // P, P, 2048)
        for half, r0, n in ((0, 0, HID[0]), (1, HID[0], HID[1])):
            d = down[r0 * P:(r0 + n) * P]
            w[f"ffn{i}_d{half}"] = d.reshape(n, P, 4, 256).transpose(2, 1, 0, 3).reshape(4, P, n * 256)
    win = f(inp["diff_w_in"])[0].reshape(KD, P, 3, 8, P).transpose(3, 1, 0, 2, 4)
    w["diff_in"] = win.reshape(8, P, 3072)
    w["diff_o"] = out3(f(inp["diff_w_o"])[0])
    win = f(inp["ev_w_in_2"])[0].reshape(KD, P, 4, 4, P)
    cv = win[:, :, 1:3].transpose(3, 1, 0, 2, 4).reshape(4, P, 2048)
    bu = win[:, :, 0::3].transpose(3, 1, 0, 2, 4).reshape(4, P, 2048)
    w["ev_in"] = np.concatenate([cv, bu])
    w["ev_pool"] = f(inp["ev_pool_w_2"])[0].transpose(1, 0, 2).reshape(1, P, 512)
    w["ev_o"] = out3(f(inp["ev_w_out_2"])[0])
    win = f(inp["od_w_in_2"])[0]
    w["od_f"] = unit(win[:, 1536:1664])[None]
    w["od_conv"] = win[:, 1544:2568].reshape(KD, P, 2, 4, P).transpose(3, 1, 0, 2, 4).reshape(4, P, 2048)
    w["od_in"] = win[:, 0:1536].reshape(KD, P, 3, 4, P).transpose(3, 1, 0, 2, 4).reshape(4, P, 3072)
    w["od_o"] = out3(f(inp["od_w_out_2"])[0])

    cols = lambda a: f(a).reshape(-1, P).T
    pad = lambda a: np.pad(f(a).reshape(-1, 1), ((0, P - f(a).size), (0, 0)))
    par = np.concatenate([
        cols(inp["ln_mix_g"]), cols(inp["ln_ffn_g"]), cols(inp["ln_mix_g_2"]), cols(inp["ln_ffn_g_2"]),
        cols(inp["ln_mix_b"]), cols(inp["ln_ffn_b"]), cols(inp["ln_mix_b_2"]), cols(inp["ln_ffn_b_2"]),
        cols(inp["mla_g_q"]), cols(inp["mla_g_kv"]), cols(inp["diff_g_sub"]), cols(inp["ev_conv_w_2"]),
        cols(inp["ev_pool_scale_2"]), cols(inp["od_dw_w_2"]), cols(inp["od_dw_b_2"]), cols(inp["od_cn_g_2"]),
        cols(inp["od_cn_b_2"]), pad(inp["diff_lam_q1"]), pad(inp["diff_lam_k1"]), pad(inp["diff_lam_q2"]),
        pad(inp["diff_lam_k2"]), pad(inp["od_forget_b_2"])], 1)
    assert par.shape == (P, NPAR)
    return w, par


def constants():
    p = np.arange(P)[:, None]
    con = np.zeros((P, NCON), np.float32)
    con[:, CCOL["ident"]:CCOL["ident"] + P] = np.eye(P)
    x = np.arange(S)[None, :]
    hidden = (x - (S - P)) // 64 > p // 64
    con[:, CCOL["dist"]:CCOL["dist"] + S] = np.where(hidden, 1e32, np.abs(p + (S - P) - x))
    con[:, CCOL["causal"]:CCOL["causal"] + P] = np.where(np.arange(P)[None, :] > p, NEG, 0.0)
    for g, win in enumerate(WINDOWS):
        con[:, CCOL["invcnt"] + 16 * g:CCOL["invcnt"] + 16 * g + 16] = 1.0 / np.minimum(np.arange(16) + 1, win)
    con[:, CCOL["slopes"]:CCOL["slopes"] + 8] = -2.0 ** -np.arange(1, 9) / HD_SCALE
    inv = np.float32(10000.0) ** (-np.arange(0, ROPE, 2, dtype=np.float32) / np.float32(ROPE))
    ang = (np.arange(S, dtype=np.float32)[None, :] * inv[:, None].astype(np.float32)).astype(np.float32)
    cos, sin = np.cos(ang), np.sin(ang)
    rcon = np.concatenate([np.concatenate([cos] * 4), np.concatenate([-sin, sin] * 2),
                           np.where(hidden, NEG, 0.0)], 1).astype(np.float32)
    return con, rcon


def kernel(**inputs):
    import concourse.bacc as bacc
    from concourse.bass_utils import run_bass_kernel_spmd

    w, par = host_layout(inputs)
    con, rcon = constants()
    arrays = {"xT": np.asarray(inputs["x"])[0].T.reshape(KD, P, S), "par": par, "con": con, "rcon": rcon}
    arrays.update({f"w_{k}": v for k, v in w.items()})
    arrays = {k: np.ascontiguousarray(v) for k, v in arrays.items()}
    nc = bacc.Bacc("TRN2", target_bir_lowering=False, num_devices=1)
    ap = {k: nc.dram_tensor(k, v.shape, F32, kind="ExternalInput").ap() for k, v in arrays.items()}
    outT = nc.dram_tensor("outT", (KD, P, S), F32, kind="ExternalOutput").ap()
    build(nc, ap["xT"], ap["par"], ap["con"], ap["rcon"], {k: ap[f"w_{k}"] for k in w}, outT)
    r = run_bass_kernel_spmd(nc, [arrays], core_ids=[0])
    return np.ascontiguousarray(np.asarray(r.results[0]["outT"]).reshape(D, S).T)[None]
```

```python
import math
from contextlib import ExitStack, contextmanager

import concourse.bass as bass
import numpy as np
from concourse import mybir

F32 = mybir.dt.float32
F32R = mybir.dt.float32r
ALU = mybir.AluOpType
ACT = mybir.ActivationFunctionType

P = 128
S = 512
NB = S // P
D = 1024
KD = D // P
D_FF = 2816
HID = (12, 10)
QR, KVR = 384, 256
ROPE, NOPE = 64, 128
SLOT = 3072
ALPHA = 4.0 ** 0.25
LN_EPS, RMS_EPS = 1e-5, 1e-6
NEG = -1e30
GLU_BANKS = ((0, 1), (3, 0), (1, 2), (3, 0))
LAST_NORM = 7
BIG = 3.0e38
MLA_SCALE = (NOPE + ROPE) ** -0.5
HD_SCALE = 64 ** -0.5
LAMBDA_INIT = 0.8 - 0.6 * math.exp(-0.3)
TAPS = 31
SHARED_TAPS = [(i, k) for i in (2, 3) for k in range(TAPS)]
TAP_RING = 6
COUNTS = (D, D // 2, QR, KVR, P)
WINDOWS = (2, 4, 8, 16)
PADC, PADW = TAPS - 1, 16

PCOL, _n = {}, 0
for _name, _w in (("ln_g", 64), ("ln_b", 64), ("g_c", 5), ("g_sub", 1), ("conv_w", 12), ("pool_s", 4),
                  ("dw_w", 4 * TAPS), ("dw_b", 4), ("cn_g", 4), ("cn_b", 4), ("lam", 4), ("f_b", 1)):
    PCOL[_name] = _n
    _n += _w
NPAR = _n
CCOL, _n = {}, 0
for _name, _w in (("ident", P), ("dist", S), ("causal", P), ("invcnt", 64), ("slopes", 8)):
    CCOL[_name] = _n
    _n += _w
NCON = _n
RCOL = {"cos": 0, "sin": S, "mask": 2 * S}

OUT3 = (3072, 3072, 2048)
STREAM = (
    ("mla_in", (3072, 3072, 1024)), ("mla_pair", (2560,) * 4), ("mla_o", OUT3), ("ffn0", None),
    ("diff_in", (3072,) * 8), ("diff_o", OUT3), ("ffn1", None),
    ("ev_in", (2048,) * 6), ("ev_b", (2560, 2048)), ("ev_o", OUT3), ("ffn2", None),
    ("od_glu0", (2048,)), ("od_f", (1024,)), ("od_glu", (2048,) * 3), ("od_in", (3072,) * 4), ("od_o", OUT3), ("ffn3", None),
)
FIRST_UNIT, _n = {}, 0
for _name, _sizes in STREAM:
    FIRST_UNIT[_name] = _n
    _n += sum(HID) + 8 if _sizes is None else len(_sizes)
OUT_MLA = ((0,), (), (1,), (2,), (3,), (), (), (4,), (), (5,), (6, 7))
OUT_DIFF = ((), (0,), (1, 2), (3,), (), (4,), (5,), (6,), (7,))
OUT_ODD = ((), (), (0,), (), (1,), (), (), (), (), (), (2,), (3,), (4, 5, 6, 7))
LATENTS = 5
SHIFT_FROM = 4
STEPS = [(t, k) for t in range(3) for k in range(KD)]
DIFF_SLOTS = (STEPS[0:5], STEPS[5:10], STEPS[10:15], STEPS[15:19], STEPS[19:22], STEPS[22:24])
ODD_SLOTS = (STEPS[0:3], STEPS[3:6], STEPS[6:9], STEPS[9:12], STEPS[12:15], [], STEPS[15:18], STEPS[18:20], STEPS[20:22],
             STEPS[22:24])
MLA_K = (3, 3, 3, 3, 2, 2, 2, 2)
MLA_SLOTS = tuple([(t, k) for k in range(MLA_K[t])] if t is not None else [] for t in (0, 1, 2, 3, 4, None, 5, 6, 7))


def finished(slot, depth):
    return [t for t, k in slot if k == depth[t] - 1]


class Count:

    def __init__(self):
        self.n, self.reg, self.slope = 0, None, 0

    def at(self, d=0):
        v = self.n + d
        return v if self.reg is None else self.reg * self.slope + v

    def add(self, k=1):
        self.n += k


@contextmanager
def counted_loop(eng, trips, slopes):
    start = {c: c.n for c in slopes}
    with eng.Fori(0, trips) as it:
        for c, k in slopes.items():
            c.reg, c.slope = it, k
        yield it
    for c, k in slopes.items():
        assert c.n - start[c] == k, (c.n - start[c], k)
        c.n, c.reg = start[c] + trips * k, None


def build(nc, xT, par, con, rcon, w, outT):
    ctx = ExitStack()
    with ctx:
        def sb(name, shape, dt=F32, stack=ctx):
            return stack.enter_context(nc.sbuf_tensor(name, shape, dt))

        def sem(name):
            return ctx.enter_context(nc.semaphore(name))

        raw = [sb(f"raw{i}", [P, SLOT]) for i in range(2)]
        whi = [sb(f"whi{i}", [P, SLOT], F32R) for i in range(2)]
        wlo = [sb(f"wlo{i}", [P, SLOT], F32R) for i in range(2)]
        X = sb("X", [P, KD, S])
        XH = sb("XH", [P, KD, S], F32R)
        XL = sb("XL", [P, KD, S], F32R)
        parm = sb("parm", [P, NPAR])
        cons = sb("cons", [P, NCON])
        ones = sb("ones", [P, P])
        inverse = sb("inverse", [P, len(COUNTS)])
        neg_half = sb("neg_half", [P, NB])
        sq = [sb(f"sq{i}", [P, S]) for i in range(2)]
        shift = sb("shift", [P, S])
        relay = sb("relay", [1, 1])
        sqt = sb("sqt", [P, S])
        st = sb("st", [P, 4 * NB])
        root = sb("root", [P, NB])
        gsub = sb("gsub", [P, 1])
        lam = sb("lam", [P, 8])
        spare = sb("spare", [1, 8])
        ident = cons[:, CCOL["ident"]:CCOL["ident"] + P]
        dist = cons[:, CCOL["dist"]:CCOL["dist"] + S]
        causal = cons[:, CCOL["causal"]:CCOL["causal"] + P]

        def pcol(name, i=0):
            return parm[:, PCOL[name] + i:PCOL[name] + i + 1]

        ph = ExitStack()
        HH = sb("HH", [P, HID[0], S], F32R, ph)
        HL = sb("HL", [P, HID[0], S], F32R, ph)
        sil = [sb(f"sil{i}", [P, S], F32, ph) for i in range(2)]
        hf = [sb(f"hf{i}", [P, S], F32, ph) for i in range(2)]
        ph.close()

        def attention_buffers(ph, tag, maps, y, pt=1):
            a = {}
            a["L"] = [[sb(f"{tag}L{i}{m}", [P, S], F32, ph) for m in range(maps)] for i in range(2)]
            a["negmax"] = sb(f"{tag}negmax", [P, 4], F32, ph)
            a["rowsum"] = sb(f"{tag}rowsum", [P, 4], F32, ph)
            a["rinv"] = sb(f"{tag}rinv", [P, 4], F32, ph)
            a["PT"] = sb(f"{tag}PT", [P, NB, S], F32, ph)
            if y:
                a["Y"] = sb(f"{tag}Y", [P, KD, S], F32, ph)
            return a

        ph = ExitStack()
        ML = attention_buffers(ph, "m", 1, False)
        rtab = sb("rtab", [P, 3 * S], F32, ph)
        CH = sb("CH", [P, 5, S], F32R, ph)
        CL = sb("CL", [P, 5, S], F32R, ph)
        KR = sb("KR", [P, S], F32, ph)
        rt = sb("rt", [P, S], F32, ph)
        cf_stack = ExitStack()
        Cf = sb("Cf", [P, 5, S], F32, cf_stack)
        cf_stack.close()
        mQN = [[sb(f"mQN{i}{m}", [P, S], F32, ph) for m in range(2)] for i in range(2)]
        mKN = [[sb(f"mKN{i}{m}", [P, S], F32, ph) for m in range(2)] for i in range(2)]
        mQR = [sb(f"mQR{i}", [P, S], F32, ph) for i in range(2)]
        mV = [[sb(f"mV{i}{m}", [P, NB, P], F32, ph) for m in range(2)] for i in range(2)]
        mVT = [sb(f"mVT{m}", [P, S], F32, ph) for m in range(2)]
        ph.close()

        ph = ExitStack()
        DF = attention_buffers(ph, "d", 2, True)
        dQ = [sb(f"dQ{i}", [P, S], F32, ph) for i in range(2)]
        dK = [sb(f"dK{i}", [P, S], F32, ph) for i in range(2)]
        dV = [sb(f"dV{i}", [P, NB, P], F32, ph) for i in range(2)]
        dVT = sb("dVT", [P, S], F32, ph)
        dB = sb("dB", [P, S], F32, ph)
        dO = [sb(f"dO{i}", [P, S], F32, ph) for i in range(2)]
        ph.close()

        ph = ExitStack()
        EY = sb("EY", [P, KD, S], F32, ph)
        ec = sb("ec", [P, S], F32, ph)
        ez = sb("ez", [P, 2 + S], F32, ph)
        eu = [sb(f"eu{i}", [P, PADW + S], F32, ph) for i in range(3)]
        EP = sb("EP", [P, 4, S], F32, ph)
        EPH = sb("EPH", [P, 4, S], F32R, ph)
        EPL = sb("EPL", [P, 4, S], F32R, ph)
        ph.close()

        ph = ExitStack()
        lf_stack = ExitStack()
        lfz, lfa, lfe, lfu, lfl, lfd, lfi, lfr = (sb(f"lf{n}", [8, S], F32, lf_stack) for n in "zaeuldir")
        lf_stack.close()
        FO = attention_buffers(ph, "f", 1, True)
        fQ = [sb(f"fQ{i}", [P, S], F32, ph) for i in range(2)]
        fK = [sb(f"fK{i}", [P, S], F32, ph) for i in range(2)]
        fV = [sb(f"fV{i}", [P, NB, P], F32, ph) for i in range(2)]
        fVT = sb("fVT", [P, S], F32, ph)
        fB = [sb(f"fB{m}", [P, S], F32, ph) for m in range(2)]
        fBD = [sb(f"fBD{m}", [P, NB, P], F32, ph) for m in range(2)]
        fz = [sb(f"fz{i}", [P, PADC + S], F32, ph) for i in range(4)]
        ftap = [sb(f"ftap{i}", [P, S], F32, ph) for i in range(TAP_RING)]
        fsig = sb("fsig", [P, S], F32, ph)
        cum = sb("cum", [8, S], F32, ph)
        ph.close()

        bank = [ctx.enter_context(nc.psum_tensor(f"bank{i}", [P, S], F32)) for i in range(8)]

        par_in = sem("par_in")
        raw_ready = [sem(f"raw_ready{i}") for i in range(2)]
        hi_ready = sem("hi_ready")
        lo_ready = sem("lo_ready")
        dve_split = sem("dve_split")
        w_used = sem("w_used")
        tile_done = sem("tile_done")
        tile_free = sem("tile_free")
        gate_done = sem("gate_done")
        aux_done = sem("aux_done")
        aux_free = sem("aux_free")
        exp_done = sem("exp_done")
        p_ready = sem("p_ready")
        src_ready = sem("src_ready")
        act_hi = sem("act_hi")
        act_lo = sem("act_lo")
        x_final = sem("x_final")
        norm_in = sem("norm_in")
        norm_out = sem("norm_out")
        var_ready = sem("var_ready")
        root_ready = sem("root_ready")
        latent_lo = sem("latent_lo")
        first_in = [sem(f"first_in{k}") for k in range(KD)]
        first_hi = sem("first_hi")
        first_lo = sem("first_lo")
        x_split = sem("x_split")
        rope_ready = sem("rope_ready")
        tap_ready = sem("tap_ready")
        tap_added = sem("tap_added")
        cum_ready = sem("cum_ready")
        mem_ready = sem("mem_ready")
        small_dve = sem("small_dve")
        small_act = sem("small_act")
        small_pe = sem("small_pe")
        step = sem("step")
        stored = sem("stored")

        block = ctx.enter_context(nc.Block())

        @block.sync
        def _(sp):
            chunk = 3 * P
            for k in range(KD):
                sp.dma_start(raw[0][:, k * chunk:(k + 1) * chunk], w["mla_in"][0, :, k * chunk:(k + 1) * chunk])\
                  .then_inc(first_in[k], 16)
                sp.dma_start(X[:, k, :], xT[k]).then_inc(first_in[k], 16)
            sp.dma_start(raw[1][:, 0:3072], w["mla_in"][1]).then_inc(raw_ready[1], 16)
            sp.dma_start(parm[:], par).then_inc(par_in, 16)
            sp.dma_start(cons[:], con).then_inc(par_in, 16)
            sp.dma_start(rtab[:], rcon).then_inc(par_in, 16)
            unit = Count()
            unit.add(2)

            def load(src, size):
                s = unit.n % 2
                if unit.n >= 2:
                    sp.wait_ge(lo_ready, unit.at(-1))
                sp.dma_start(raw[s][:, 0:size], src).then_inc(raw_ready[s], 16)
                unit.add()

            def load_all(name, n, size, i0=0):
                with counted_loop(sp, n // 2, {unit: 2}) as it:
                    for j in range(2):
                        load(w[name][bass.ds(it * 2 + (i0 + j), 1), :, 0:size].rearrange("o p n -> (o p) n"), size)

            for name, sizes in STREAM:
                if sizes is None:
                    for half in range(2):
                        load_all(name + "_gu", HID[half], 2048, HID[0] * half)
                        load_all(f"{name}_d{half}", 4, 256 * HID[half])
                elif len(sizes) >= 6:
                    load_all(name, len(sizes), sizes[0])
                else:
                    for i, size in enumerate(sizes):
                        if (name, i) not in (("mla_in", 0), ("mla_in", 1)):
                            load(w[name][i, :, 0:size], size)
            for j in range(KD):
                sp.wait_ge(x_final, 7 * KD + j + 1)
                sp.dma_start(outT[j], X[:, j, :]).then_inc(stored, 16)
            sp.wait_ge(stored, 16 * KD)

        @block.scalar
        def _(act):
            unit, tiles, srcs, auxf, gates, small = (Count() for _ in range(6))

            def split_w(size):
                s = unit.n % 2
                arrived = unit.n // 2 * 16 + 16 * s
                if unit.reg is not None:
                    arrived = unit.reg * 16 + arrived
                act.wait_ge(raw_ready[s], arrived)
                if unit.n >= 2:
                    act.wait_ge(w_used, unit.at(-1))
                act.copy(whi[s][:, 0:size], raw[s][:, 0:size]).then_inc(hi_ready, 1)
                unit.add()

            def split_x(dst, src):
                act.wait_ge(src_ready, srcs.at(1))
                act.copy(dst, src).then_inc(act_hi, 1)
                srcs.add()

            def split_at(dst, src, sem_, value):
                act.wait_ge(sem_, value)
                act.copy(dst, src).then_inc(act_hi, 1)

            def scale_shift(j, norm):
                g, b = pcol("ln_g", KD * norm + j), pcol("ln_b", KD * norm + j)
                act.wait_ge(src_ready, srcs.at(1))
                if norm != LAST_NORM:
                    act.activation(XH[:, j, :], X[:, j, :], ACT.Identity, bias=b, scale=g).then_inc(act_hi, 1)
                act.activation(X[:, j, :], X[:, j, :], ACT.Identity, bias=b, scale=g).then_inc(x_final, 1)
                srcs.add()

            def layer_norm(norm):
                for j in range(KD):
                    scale_shift(j, norm)

            def ffn(next_size):
                for half in range(2):
                    n = HID[half]

                    def gu_unit(size, hidden, by_dve=False):
                        if by_dve:
                            unit.add()
                        else:
                            split_w(size)
                        i = gates.n % 2
                        act.wait_ge(tile_done, tiles.at(1))
                        if gates.n >= 2:
                            act.wait_ge(tile_free, tiles.at(-2))
                        act.activation(sil[i][:], bank[2 * i][:], ACT.Silu).then_inc(gate_done, 1)
                        gates.add()
                        tiles.add(2)
                        act.wait_ge(tile_free, tiles.at())
                        act.copy(hidden, hf[i][:]).then_inc(act_hi, 1)

                    peeled = 2 if half == 0 else 0
                    for j in range(peeled):
                        gu_unit(2048, HH[:, j, :], j == 0)
                    with counted_loop(act, (n - 2 - peeled) // 2, {unit: 2, gates: 2, tiles: 4}) as it:
                        for j in range(2):
                            gu_unit(2048, HH[:, bass.ds(it * 2 + (peeled + j), 1), :].rearrange("p o n -> p (o n)"))
                    for j in range(n - 2, n):
                        gu_unit(2048 if j < n - 1 else 256 * n, HH[:, j, :])
                    for u in range(4):
                        if u < 3:
                            split_w(256 * n)
                        elif half == 0:
                            split_w(2048)
                        elif next_size:
                            split_w(next_size)
                        tiles.add(2)

            def out_projection(next_size, begun=True):
                for size in (OUT3[2], next_size) if begun else (OUT3[1], OUT3[2], next_size):
                    split_w(size)
                tiles.add(8)

            chunk = 3 * P
            for k in range(KD):
                act.wait_ge(first_in[k], 32)
                act.copy(whi[0][:, k * chunk:(k + 1) * chunk], raw[0][:, k * chunk:(k + 1) * chunk])\
                   .then_inc(first_hi if k < KD - 1 else hi_ready, 1)
            unit.add()

            unit.add()
            act.wait_ge(small_pe, 1)
            act.activation(lam[:, 4:6], bank[4][:, 0:2], ACT.Exp).then_inc(small_act, 1)
            small.add()
            split_w(1024)
            split_w(2560)
            for j in range(5):
                split_x(CH[:, j, :], Cf[:, j, :])
            tiles.add(7)

            def exp_rows(A, i, m, qb, col):
                act.wait_ge(aux_free, auxf.at(1))
                row = A["L"][i][m][:, 0:(qb + 1) * P]
                act.activation(row, row, ACT.Exp, bias=A["negmax"][:, col:col + 1], scale=-1.0,
                               accum_out=A["rowsum"][:, col:col + 1]).then_inc(exp_done, 1)
                auxf.add()

            split_w(2560)
            tiles.add(8)
            auxf.add(2)
            for p in range(4):
                for j in range(8):
                    exp_rows(ML, j % 2, 0, j % 4, j % 2)
                    if j == 1:
                        split_w((2560, 2560, OUT3[0], OUT3[1])[p])
                    if j == 5:
                        auxf.add()
                        split_at(XH[:, 2 * p, :], sq[0][:], aux_free, auxf.at())
                    if j > 0:
                        auxf.add()
                auxf.add()
                if p < 3:
                    auxf.add(2)
                    tiles.add(8)
                auxf.add()
                split_at(XH[:, 2 * p + 1, :], sq[1][:], aux_free, auxf.at())
            out_projection(2048)
            layer_norm(0)
            ffn(3072)
            layer_norm(2)

            split_w(3072)
            tiles.add(3)
            auxf.add()

            def diff_head(s, first, last):
                def early(ks):
                    act.wait_ge(tile_free, tiles.at())
                    for k in ks:
                        split_x(XH[:, k, :], DF["Y"][:, k, :])

                if last:
                    early((0, 1))
                for j in range(4):
                    for m in range(2):
                        exp_rows(DF, j % 2, m, j, 2 * (j % 2) + m)
                    if j == 0 and not last:
                        split_w(3072)
                    if j > 0:
                        auxf.add()
                    if last:
                        early(((2, 3), (4,), (5,), (6,))[j])
                        if j == 2:
                            split_w(OUT3[1])
                auxf.add()
                if not last:
                    auxf.add()
                    tiles.add(3)
                auxf.add()

            diff_head(0, True, False)
            with counted_loop(act, 3, {unit: 2, tiles: 6, auxf: 28}):
                diff_head(1, False, False)
                diff_head(0, False, False)
            diff_head(1, False, True)
            split_x(XH[:, 7, :], DF["Y"][:, 7, :])
            out_projection(2048)
            layer_norm(1)
            ffn(2048)
            layer_norm(3)

            unit.add()
            for u in range(2, 7):
                split_w(2560 if u == 6 else 2048)
                if u == 3:
                    for j in range(4):
                        split_x(EPH[:, j, :], EP[:, j, :])
            tiles.add(12)
            split_w(2048)
            for j in range(4):
                split_at(EPH[:, j, :], EY[:, 4 + j, :], tile_free, tiles.at(4))
            tiles.add(4)
            split_w(OUT3[0])
            tiles.add(4)
            for j in range(4):
                split_at(XH[:, 4 + j, :], EY[:, j, :], tile_free, tiles.at())
            out_projection(2048, False)
            layer_norm(4)
            ffn(2048)
            layer_norm(6)

            def sigmoid(i):
                act.wait_ge(tile_done, tiles.at(2))
                if i:
                    act.wait_ge(tile_free, tiles.at())
                act.activation(fsig[:], bank[GLU_BANKS[i][1]][:], ACT.Sigmoid).then_inc(gate_done, 1)
                gates.add()
                tiles.add(2)

            unit.add()
            sigmoid(0)
            split_w(2048)
            tiles.add(1)
            act.wait_ge(tile_free, tiles.at())
            act.activation(lfa[:], lfz[:], ACT.Abs).then_inc(small_act, 1)
            small.add()
            act.wait_ge(small_act, small.at())
            act.activation(lfe[:], lfa[:], ACT.Exp, scale=-1.0).then_inc(small_act, 1)
            act.wait_ge(small_dve, 2)
            act.activation(lfl[:], lfu[:], ACT.Ln).then_inc(small_act, 1)
            small.add(2)
            for i in range(1, 4):
                split_w(2048 if i < 3 else 3072)
                sigmoid(i)
            split_w(3072)
            act.wait_ge(tile_free, tiles.at())
            jobs = Count()

            def tap_products(n):
                for i, k in SHARED_TAPS[jobs.n:jobs.n + n]:
                    wk, adds = pcol("dw_w", 4 * k + i), jobs.n - (i - 2) - 1
                    if k == 0:
                        ins = act.activation(FO["Y"][:, 4 + i, :], fz[i][:, 0:S], ACT.Identity, bias=pcol("dw_b", i), scale=wk)
                    else:
                        if adds >= TAP_RING:
                            act.wait_ge(tap_added, adds - TAP_RING + 1)
                        ins = act.activation(ftap[adds % TAP_RING][:], fz[i][:, k:k + S], ACT.Copy, scale=wk)
                    ins.then_inc(tap_ready, 1)
                    jobs.add()

            tap_products(TAP_RING)
            tiles.add(3)
            auxf.add()
            for g in range(4):
                auxf.add(2 if g == 1 else 1)
                if g == 3:
                    split_at(XH[:, 0, :], FO["Y"][:, 0, :], tile_free, tiles.at())
                for j in range(8):
                    exp_rows(FO, j % 2, 0, j % 4, j % 2)
                    if j == 1:
                        auxf.add()
                    if j == (3 if g == 3 else 1):
                        split_w(3072)
                    if g == 3 and j < 2:
                        split_at(XH[:, 1 + j, :], FO["Y"][:, 1 + j, :], tile_free, tiles.at())
                    tap_products(2)
                    if j == 5:
                        auxf.add()
                    if j > 0:
                        auxf.add()
                auxf.add()
                if g < 3:
                    auxf.add()
                    tiles.add(3)
                auxf.add()
                if g == 3:
                    split_at(XH[:, 3, :], FO["Y"][:, 3, :], aux_free, auxf.at())
            for i in range(4):
                act.wait_ge(src_ready, srcs.at(1))
                srcs.add()
                act.activation(FO["Y"][:, 4 + i, :], FO["Y"][:, 4 + i, :], ACT.Silu, bias=pcol("cn_b", i),
                               scale=pcol("cn_g", i)).then_inc(small_act, 1)
                small.add()
                split_at(XH[:, 4 + i, :], FO["Y"][:, 4 + i, :], small_act, small.at())
            out_projection(2048)
            layer_norm(5)
            ffn(0)
            layer_norm(7)

        @block.gpsimd
        def _(pool):
            unit, his, whis = Count(), Count(), Count()

            def split_w(size):
                s = unit.n % 2
                pool.wait_ge(hi_ready, whis.at(1))
                pool.tensor_tensor(wlo[s][:, 0:size], raw[s][:, 0:size], whi[s][:, 0:size].bitcast(F32),
                                   ALU.subtract).then_inc(lo_ready, 1)
                unit.add()
                whis.add()

            relayed = Count()

            def relay_split():
                relayed.add()
                pool.wait_ge(dve_split, relayed.at())
                pool.memset(relay[:], 0.0).then_inc(lo_ready, 1)
                unit.add()

            def split_x(dst, src, hi):
                pool.wait_ge(act_hi, his.at(1))
                pool.tensor_tensor(dst, src, hi.bitcast(F32), ALU.subtract).then_inc(act_lo, 1)
                his.add()

            finals, vars_ = Count(), Count()

            def inverse_root():
                vars_.add()
                pool.wait_ge(var_ready, vars_.at())
                pool.tensor_tensor(root[:], st[:, 2 * NB:3 * NB], neg_half[:], ALU.pow).then_inc(root_ready, 1)

            def layer_norm(split=True):
                inverse_root()
                for j in range(KD if split else 0):
                    pool.wait_ge(x_final, finals.at(1))
                    pool.tensor_tensor(XL[:, j, :], X[:, j, :], XH[:, j, :].bitcast(F32), ALU.subtract).then_inc(act_lo, 1)
                    finals.add()
                    his.add()

            def ffn(next_size):
                for half in range(2):
                    n = HID[half]
                    peeled = 2 if half == 0 else 0
                    for j in range(peeled):
                        if j == 0:
                            relay_split()
                        else:
                            split_w(2048)
                        split_x(HL[:, j, :], hf[j][:], HH[:, j, :])
                    with counted_loop(pool, (n - 2 - peeled) // 2, {unit: 2, whis: 2, his: 2}) as it:
                        for j in range(2):
                            split_w(2048)
                            t = bass.ds(it * 2 + (peeled + j), 1)
                            split_x(HL[:, t, :].rearrange("p o n -> p (o n)"), hf[j][:],
                                    HH[:, t, :].rearrange("p o n -> p (o n)"))
                    for j in range(n - 2, n):
                        split_w(2048 if j < n - 1 else 256 * n)
                        split_x(HL[:, j, :], hf[j % 2][:], HH[:, j, :])
                    for u in range(4):
                        if u < 3:
                            split_w(256 * n)
                        elif half == 0:
                            split_w(2048)
                        elif next_size:
                            split_w(next_size)

            pool.memset(ones[:], 1.0)
            pool.memset(neg_half[:], -0.5)
            for i, n in enumerate(COUNTS):
                pool.memset(inverse[:, i:i + 1], 1.0 / n).then_inc(mem_ready, 1)
            chunk = 3 * P
            for k in range(KD):
                part = slice(k * chunk, (k + 1) * chunk)
                if k < KD - 1:
                    pool.wait_ge(first_hi, k + 1)
                else:
                    pool.wait_ge(hi_ready, 1)
                pool.tensor_tensor(wlo[0][:, part], raw[0][:, part], whi[0][:, part].bitcast(F32), ALU.subtract)\
                    .then_inc(first_lo if k < KD - 1 else lo_ready, 1)
            unit.add()
            whis.add()
            relay_split()
            split_w(1024)
            inverse_root()
            inverse_root()
            his.add(5)
            split_w(2560)
            split_w(2560)
            for p in range(4):
                split_w((2560, 2560, OUT3[0], OUT3[1])[p])
                for m in range(2):
                    split_x(XL[:, 2 * p + m, :], sq[m][:], XH[:, 2 * p + m, :])

            def out_projection(next_size, begun=True):
                for size in (OUT3[2], next_size) if begun else (OUT3[1], OUT3[2], next_size):
                    split_w(size)

            out_projection(2048)
            layer_norm()
            ffn(3072)
            layer_norm()
            split_w(3072)
            split_w(3072)
            with counted_loop(pool, 3, {unit: 2, whis: 2, vars_: 2}):
                inverse_root()
                split_w(3072)
                inverse_root()
                split_w(3072)
            for j in range(6):
                split_x(XL[:, j, :], DF["Y"][:, j, :], XH[:, j, :])
                if j == 1:
                    inverse_root()
            split_w(OUT3[1])
            split_x(XL[:, 6, :], DF["Y"][:, 6, :], XH[:, 6, :])
            inverse_root()
            split_x(XL[:, 7, :], DF["Y"][:, 7, :], XH[:, 7, :])
            out_projection(2048)
            layer_norm()
            ffn(2048)
            layer_norm()
            relay_split()
            for u in range(2, 7):
                split_w(2560 if u == 6 else 2048)
                if u == 3:
                    for j in range(4):
                        split_x(EPL[:, j, :], EP[:, j, :], EPH[:, j, :])
            split_w(2048)
            for j in range(4):
                split_x(EPL[:, j, :], EY[:, 4 + j, :], EPH[:, j, :])
            split_w(OUT3[0])
            for j in range(4):
                split_x(XL[:, 4 + j, :], EY[:, j, :], XH[:, 4 + j, :])
            out_projection(2048, False)
            layer_norm()
            ffn(2048)
            layer_norm()
            relay_split()
            for i in range(3):
                split_w(2048)
            for i in range(2):
                split_w(3072)
            jobs = Count()

            def tap_adds(n):
                for i, k in SHARED_TAPS[jobs.n:jobs.n + n]:
                    adds = jobs.n - (i - 2) - 1
                    jobs.add()
                    if k:
                        c = FO["Y"][:, 4 + i, :]
                        pool.wait_ge(tap_ready, jobs.n)
                        if adds:
                            pool.wait_ge(tap_added, adds)
                        pool.tensor_tensor(c, c, ftap[adds % TAP_RING][:], ALU.add).then_inc(tap_added, 1)

            tap_adds(TAP_RING)
            for g in range(4):
                if g == 3:
                    split_x(XL[:, 0, :], FO["Y"][:, 0, :], XH[:, 0, :])
                for j in range(8):
                    if j == (3 if g == 3 else 1):
                        split_w(3072)
                    if g == 3 and j < 2:
                        split_x(XL[:, 1 + j, :], FO["Y"][:, 1 + j, :], XH[:, 1 + j, :])
                    tap_adds(2)
            split_x(XL[:, 3, :], FO["Y"][:, 3, :], XH[:, 3, :])
            inverse_root()
            for j in range(4, KD):
                split_x(XL[:, j, :], FO["Y"][:, j, :], XH[:, j, :])
            out_projection(2048)
            layer_norm()
            ffn(0)
            layer_norm(split=False)

        @block.tensor
        def _(pe):
            unit, tiles, los, aux, ins_, roots, probs = (Count() for _ in range(7))
            last = {b: 0 for b in range(4, 8)}
            fresh = [False]

            def begin_unit():
                pe.wait_ge(lo_ready, unit.at(1))
                s = unit.n % 2
                fresh[0] = unit.n > 0
                unit.add()
                return s

            def product(out, s, off, xh, xl, start, stop):
                ins = pe.matmul(out, whi[s][:, off:off + P], xh, start=start, stop=False)
                if fresh[0]:
                    ins.then_inc(w_used, 1)
                    fresh[0] = False
                pe.matmul(out, whi[s][:, off:off + P], xl, start=False, stop=False)
                return pe.matmul(out, wlo[s][:, off:off + P], xh, start=False, stop=stop)

            def claim(lag):
                if tiles.n >= lag:
                    pe.wait_ge(tile_free, tiles.at(1 - lag))

            def tile(s, b, offs, xh, xl, lag=4, wait_x=False, first=None):
                claim(lag)
                for k, off in enumerate(offs):
                    if wait_x:
                        pe.wait_ge(act_lo, los.at(k + 1))
                    h, l = first if first and k < 4 else (xh, xl)
                    ins = product(bank[b][:], s, off, h[:, k, :], l[:, k, :], k == 0, k == len(offs) - 1)
                ins.then_inc(tile_done, 1)
                tiles.add()

            def begin_together():
                s = begin_unit()
                pe.wait_ge(tile_free, tiles.at())
                return s

            def together(s, nt, ks, depth=KD, first=(XH, XL)):
                def low(k):
                    xl = (first if k < 4 else (XH, XL))[1]
                    pe.wait_ge(act_lo, los.at(k + 1))
                    for t in range(nt):
                        ins = pe.matmul(bank[t][:], whi[s][:, (k * nt + t) * P:(k * nt + t + 1) * P], xl[:, k, :],
                                        start=False, stop=k == depth - 1)
                        if k == depth - 1:
                            ins.then_inc(tile_done, 1)

                for n, k in enumerate(ks):
                    xh = (first if k < 4 else (XH, XL))[0]
                    pe.wait_ge(act_hi, los.at(k + 1 + LATENTS))
                    for which in (whi, wlo):
                        for t in range(nt):
                            ins = pe.matmul(bank[t][:], which[s][:, (k * nt + t) * P:(k * nt + t + 1) * P], xh[:, k, :],
                                            start=k == 0 and which is whi, stop=False)
                            if fresh[0]:
                                ins.then_inc(w_used, 1)
                                fresh[0] = False
                    if n:
                        low(ks[n - 1])
                if ks:
                    low(ks[-1])
                if ks and ks[-1] == depth - 1:
                    tiles.add(nt)
                    los.add(depth)

            def unit_tiles(nt, b0, xh=XH, xl=XL, depth=KD, first=None):
                s = begin_unit()
                for t in range(nt):
                    tile(s, (b0 + t) % 4, [(k * nt + t) * P for k in range(depth)], xh, xl, first=first)

            def out_projection(s, ks, first=(XH, XL)):
                together(s, 3, ks, first=first)
                s = begin_unit()
                for t in range(3):
                    tile(s, (3, 0, 1)[t], [(k * 3 + t) * P for k in range(KD)], XH, XL, first=first)
                    if t == 0:
                        first_mean()
                unit_tiles(2, 2, first=first)

            def first_mean():
                pe.wait_ge(tile_free, tiles.at(1 - SHIFT_FROM))
                pe.matmul(bank[6][:], ones[:], X[:, 0, :], start=True, stop=True).then_inc(norm_out, 1)

            def from_dve():
                ins_.add()
                pe.wait_ge(norm_in, ins_.at())

            def column_sums(b, col, src, n):
                i = COUNTS.index(n)
                for q in range(NB):
                    ins = pe.matmul(bank[b][:, col + q:col + q + 1], src[:, q * P:(q + 1) * P], inverse[:, i:i + 1],
                                    start=True, stop=True)
                return ins

            def spread(b, src):
                for q in range(NB):
                    ins = pe.matmul(bank[b][:, q * P:(q + 1) * P], src[:, q:q + 1].to_broadcast([P, P]), ident,
                                    start=True, stop=True)
                ins.then_inc(norm_out, 1)

            def spread_root(b):
                roots.add()
                pe.wait_ge(root_ready, roots.at())
                spread(b, root)

            def layer_norm(T=X, n=KD, work=lambda: keep_warm(9)):
                from_dve()
                if T is not X:
                    from_dve()
                column_sums(7, 0, sq[0], n * P)
                column_sums(7, NB, sq[1], n * P).then_inc(norm_out, 1)
                if T is X:
                    pe.wait_ge(tile_free, tiles.at())
                column_sums(5, 0, T[:, n - 1, :], n * P)
                if T is X:
                    from_dve()
                column_sums(5, NB, sqt, n * P).then_inc(norm_out, 1)
                work()
                spread_root(6)
                from_dve()
                spread(7, st[:, 3 * NB:4 * NB])
                keep_warm(7)

            def keep_warm(n):
                for _ in range(n):
                    pe.matmul(bank[4][:, 0:P], ones[:], ident, start=True, stop=True)

            def mean_squares(b, src, n):
                from_dve()
                column_sums(b, 0, src, n).then_inc(norm_out, 1)

            def ffn():
                for half in range(2):
                    n = HID[half]
                    if half == 0:
                        s = begin_together()
                        together(s, 2, range(KD))
                        unit_tiles(2, 2)
                        trips = (n - 2) // 2
                    else:
                        trips = n // 2
                    with counted_loop(pe, trips, {unit: 2, tiles: 4}):
                        unit_tiles(2, 0)
                        unit_tiles(2, 2)

                    def down_unit(j, wait_x=False):
                        s = begin_unit()
                        for t in range(2):
                            tile(s, 2 * j + t, [(k * 2 + t) * P for k in range(n)], HH, HL, wait_x=wait_x and t == 0)

                    for u in range(4):
                        down_unit(u % 2, u == 0)
                        if half == 1 and u == 1:
                            first_mean()
                    los.add(n)

            def aux_claim(b):
                if last[b] > 0:
                    pe.wait_ge(aux_free, aux.at(last[b] - aux.n))

            def aux_end(ins, b):
                ins.then_inc(aux_done, 1)
                aux.add()
                last[b] = aux.n

            def transposes(dst_bank, src, n, ready, value):
                pe.wait_ge(ready, value)
                aux_claim(dst_bank)
                for b in range(n):
                    ins = pe.transpose(bank[dst_bank][:, b * P:(b + 1) * P], src[:, b * P:(b + 1) * P], ident)
                aux_end(ins, dst_bank)

            def steps(s, slot, depth, offset, xh, xl, banks, lag, xbase=None):
                for t, k in slot:
                    if k == 0:
                        claim(lag)
                    kx = k + (xbase[t] if xbase else 0)
                    ins = product(bank[banks[t]][:], s, offset(t, k), xh[:, kx, :], xl[:, kx, :], k == 0, k == depth[t] - 1)
                    if k == depth[t] - 1:
                        ins.then_inc(tile_done, 1)
                        tiles.add()

            def value_product(A, v, rows, cols, behind):
                pe.wait_ge(aux_free, aux.at(-behind))
                aux_claim(7)
                for kb in range(NB):
                    ins = pe.matmul(bank[7][rows, kb * P:S], v[:, kb, cols], A["PT"][:, kb, kb * P:S],
                                    start=kb == 0, stop=kb == NB - 1)
                aux_end(ins, 7)

            for k in range(KD):
                pe.wait_ge(x_split, k + 1)
                if k < KD - 1:
                    pe.wait_ge(first_lo, k + 1)
                else:
                    pe.wait_ge(lo_ready, 1)
                for t in range(3):
                    ins = product(bank[t][:], 0, (k * 3 + t) * P, XH[:, k, :], XL[:, k, :], k == 0, k == KD - 1)
                    if k == KD - 1:
                        ins.then_inc(tile_done, 1)
            unit.add()
            tiles.add(3)
            pe.wait_ge(mem_ready, len(COUNTS))
            pe.wait_ge(small_dve, 1)
            pe.matmul(bank[4][:, 0:2], ones[:], lam[:, 0:2], start=True, stop=True).then_inc(small_pe, 1)
            s = begin_unit()
            for t in range(3):
                tile(s, (3, 0, 1)[t], [(k * 3 + t) * P for k in range(KD)], XH, XL)
                if t == 1:
                    mean_squares(5, sq[1], QR)
            spread_root(6)
            mean_squares(5, sq[0], KVR)
            s = begin_unit()
            claim(4)
            for k in range(KD):
                if k == KD // 2:
                    spread_root(7)
                ins = product(bank[2][:], s, k * P, XH[:, k, :], XL[:, k, :], k == 0, k == KD - 1)
            ins.then_inc(tile_done, 1)
            tiles.add()

            def mla_offset(t, k):
                return k * 4 * P + t * P if t < 4 else 3 * 4 * P + k * 4 * P + (t - 4) * P

            def mla_steps(s, slot, lag=4):
                steps(s, slot, MLA_K, mla_offset, CH, CL, (0, 1, 2, 3, 0, 1, 2, 3), lag, (0, 0, 0, 0, 3, 3, 3, 3))

            s = begin_unit()
            pe.wait_ge(latent_lo, 3)
            for slot in MLA_SLOTS:
                if slot == MLA_SLOTS[4]:
                    pe.wait_ge(latent_lo, 5)
                mla_steps(s, slot, 3)
            transposes(7, mVT[0], NB, tile_free, tiles.at(-2))
            transposes(4, mVT[1], NB, tile_free, tiles.at())
            for p in range(4):
                i = p % 2
                pe.wait_ge(tile_free, tiles.at())
                pe.wait_ge(rope_ready, p + 2)
                s = begin_unit()
                for j in range(8):
                    m, qb = j // 4, j % 4
                    b, n = 4 + j % 2, (qb + 1) * P
                    aux_claim(b)
                    pe.matmul(bank[b][:, 0:n], mQN[i][m][:, qb * P:n], mKN[i][m][:, 0:n], start=True, stop=False)
                    half = slice(64 * m, 64 * m + 64)
                    aux_end(pe.matmul(bank[b][:, 0:n], mQR[i][half, qb * P:n], KR[half, 0:n], start=False, stop=True), b)
                    if p < 3:
                        mla_steps(s, MLA_SLOTS[j])
                    else:
                        together(s, 3, OUT_MLA[j])
                    if j == 5:
                        value_product(ML, mV[i][0], slice(0, P), slice(0, P), 1)
                    if j > 0:
                        probs.add()
                        transposes(6, ML["L"][(j - 1) % 2][0], (j - 1) % 4 + 1, p_ready, probs.at())
                    if j == 7 and p < 3:
                        transposes(7, mVT[0], NB, tile_free, tiles.at(-1))
                if p < 3:
                    mla_steps(s, MLA_SLOTS[8])
                else:
                    together(s, 3, OUT_MLA[8])
                probs.add()
                transposes(6, ML["L"][1][0], NB, p_ready, probs.at())
                if p < 3:
                    transposes(4, mVT[1], NB, tile_free, tiles.at())
                else:
                    together(s, 3, OUT_MLA[9])
                value_product(ML, mV[i][1], slice(0, P), slice(0, P), 1 if p < 3 else 0)
            out_projection(s, OUT_MLA[-1])
            layer_norm()
            ffn()
            layer_norm()

            def head_offset(t, k):
                return (k * 3 + t) * P

            def head_steps(s, slot):
                steps(s, slot, (KD,) * 3, head_offset, XH, XL, (0, 1, 2), 3)

            def diff_head(i, first, last_one):
                pe.wait_ge(tile_free, tiles.at())
                if not first:
                    last.update({4: aux.n - 5, 5: aux.n - 4, 6: aux.n - 1, 7: aux.n})
                s = begin_unit()
                for j in range(4):
                    n = (j + 1) * P
                    for m in range(2):
                        half = slice(64 * m, 64 * m + 64)
                        aux_claim(4 + m)
                        aux_end(pe.matmul(bank[4 + m][:, 0:n], dQ[i][half, j * P:n], dK[i][half, 0:n], start=True, stop=True), 4 + m)
                    if last_one:
                        together(s, 3, OUT_DIFF[j])
                    else:
                        head_steps(s, DIFF_SLOTS[j])
                    if j > 0:
                        probs.add()
                        transposes(6, DF["L"][(j - 1) % 2][0], j, p_ready, probs.at())
                    if j == 1 and not first:
                        squares_of_head()
                    if j == 2 and not first:
                        spread_root(7)
                    if j == 3 and not last_one:
                        transposes(7, dVT, NB, tile_free, tiles.at(-1))
                if last_one:
                    together(s, 3, OUT_DIFF[4])
                else:
                    head_steps(s, DIFF_SLOTS[4])
                probs.add()
                transposes(6, DF["L"][1][0], NB, p_ready, probs.at())
                if last_one:
                    together(s, 3, OUT_DIFF[5])
                else:
                    head_steps(s, DIFF_SLOTS[5])
                value_product(DF, dV[i], slice(0, P), slice(0, P), 0)
                return s

            def squares_of_head():
                aux_claim(7)
                mean_squares(7, sqt, P)

            together(begin_together(), 3, range(KD))
            transposes(6, dVT, NB, tile_free, tiles.at(-2))
            diff_head(0, True, False)
            with counted_loop(pe, 3, {unit: 2, tiles: 6, aux: 28, ins_: 2, roots: 2, probs: 8}):
                diff_head(1, False, False)
                diff_head(0, False, False)
            s = diff_head(1, False, True)
            together(s, 3, OUT_DIFF[6])
            squares_of_head()
            together(s, 3, OUT_DIFF[7])
            spread_root(7)
            out_projection(s, OUT_DIFF[8])
            layer_norm()
            ffn()
            layer_norm()

            together(begin_together(), 2, range(KD))
            unit_tiles(2, 2)
            with counted_loop(pe, 2, {unit: 2, tiles: 4}):
                unit_tiles(2, 0)
                unit_tiles(2, 2)
            s = begin_unit()
            for i in range(4):
                pe.wait_ge(act_lo, los.at(i + 1))
                claim(4)
                product(bank[i][:], s, 2048 + i * P, EPH[:, i, :], EPL[:, i, :], True, True).then_inc(tile_done, 1)
                tiles.add()
            los.add(4)
            for t in range(2):
                tile(s, t, [(k * 2 + t) * P for k in range(KD)], XH, XL)
            unit_tiles(2, 2)
            out_projection(begin_together(), range(KD), (EPH, EPL))
            layer_norm()
            ffn()
            layer_norm()

            together(begin_together(), 2, range(KD))
            unit_tiles(1, 2)
            for i in range(1, 4):
                unit_tiles(2, GLU_BANKS[i][0])
            unit_tiles(3, 1)
            transposes(6, fVT, NB, tile_free, tiles.at(-2))
            for g in range(4):
                i = g % 2
                if g == 0:
                    pe.wait_ge(cum_ready, 1)
                if g == 1:
                    pe.wait_ge(aux_free, aux.at())
                    aux_end(pe.matmul(bank[5][:], ones[:], FO["Y"][:, 4, :], start=True, stop=True), 5)

                def gates(m):
                    aux_claim(6 + m)
                    h = 2 * g + m
                    aux_end(pe.matmul(bank[6 + m][:], ident[0:8, h:h + 1].to_broadcast([8, P]), cum[:], start=True, stop=True), 6 + m)

                gates(0)
                pe.wait_ge(tile_free, tiles.at())
                s = begin_unit()
                for j in range(8):
                    m, qb = j // 4, j % 4
                    b, n = 4 + j % 2, (qb + 1) * P
                    half = slice(64 * m, 64 * m + 64)
                    aux_claim(b)
                    aux_end(pe.matmul(bank[b][:, 0:n], fQ[i][half, qb * P:n], fK[i][half, 0:n], start=True, stop=True), b)
                    if j == 1:
                        gates(1)
                    if g < 3:
                        head_steps(s, ODD_SLOTS[j])
                    else:
                        together(s, 3, OUT_ODD[j])
                    if j == 5:
                        value_product(FO, fV[i], slice(0, 64), slice(0, 64), 1)
                    if j > 0:
                        probs.add()
                        transposes(6, FO["L"][(j - 1) % 2][0], (j - 1) % 4 + 1, p_ready, probs.at())
                    if j == 7 and g < 3:
                        transposes(7, fVT, NB, tile_free, tiles.at(-1))
                if g < 3:
                    head_steps(s, ODD_SLOTS[8])
                else:
                    together(s, 3, OUT_ODD[8])
                probs.add()
                transposes(6, FO["L"][1][0], NB, p_ready, probs.at())
                if g < 3:
                    head_steps(s, ODD_SLOTS[9])
                else:
                    together(s, 3, OUT_ODD[9])
                value_product(FO, fV[i], slice(64, P), slice(64, P), 0)
            together(s, 3, OUT_ODD[10])
            layer_norm(FO["Y"][:, 4:8, :], 4, lambda: together(s, 3, OUT_ODD[11]))
            out_projection(s, OUT_ODD[12])
            layer_norm()
            ffn()
            layer_norm()

        @block.vector
        def _(dve):
            tiles, aux, los, steps, exps, gates, outs, roots, smalls = (Count() for _ in range(9))

            def link(ins):
                ins.then_inc(step, 1)
                steps.add()
                dve.wait_ge(step, steps.at())

            def take(op, n=1):
                dve.wait_ge(tile_done, tiles.at(n))
                op().then_inc(tile_free, n)
                tiles.add(n)

            def take_aux(op):
                dve.wait_ge(aux_done, aux.at(1))
                op().then_inc(aux_free, 1)
                aux.add()

            def copy_tile(dst, b):
                take(lambda: dve.tensor_copy(dst, bank[b][:]))

            def from_pe():
                outs.add()
                dve.wait_ge(norm_out, outs.at())

            def get_shift(b):
                return dve.tensor_scalar(shift[:], bank[b][:], -1.0 / P, None, ALU.mult)

            def accumulate(T, j, n):
                x = T[:, j, :]
                if j == 0:
                    link(dve.tensor_tensor(sq[1][:], x, x, ALU.mult))
                elif j < n - 1:
                    dve.tensor_tensor(sqt[:], x, x, ALU.mult).then_inc(step, 1)
                    steps.add()
                    squared = steps.at()
                    dve.tensor_tensor(sq[0][:], T[:, 0, :] if j == 1 else sq[0][:], x, ALU.add).then_inc(step, 1)
                    steps.add()
                    dve.wait_ge(step, squared)
                    ins = dve.tensor_tensor(sq[1][:], sq[1][:], sqt[:], ALU.add)
                    if j < n - 2:
                        link(ins)
                    else:
                        ins.then_inc(norm_in, 1)
                        dve.wait_ge(step, steps.at())
                else:
                    dve.tensor_tensor(sqt[:], x, x, ALU.mult).then_inc(norm_in, 1)

            def normalise_tiles(T, n, done):
                mean, square, var, nmr = (st[:, i * NB:(i + 1) * NB] for i in range(4))
                from_pe()
                link(dve.tensor_copy(st[:, 0:2 * NB], bank[7][:, 0:2 * NB]))
                from_pe()
                link(dve.tensor_tensor(st[:, 0:2 * NB], st[:, 0:2 * NB], bank[5][:, 0:2 * NB], ALU.add))
                link(dve.tensor_tensor(nmr, mean, mean, ALU.mult))
                link(dve.scalar_tensor_tensor(var, square, LN_EPS, nmr, ALU.add, ALU.subtract))
                dve.tensor_scalar(var, var, LN_EPS, None, ALU.max).then_inc(var_ready, 1)
                roots.add()
                dve.wait_ge(root_ready, roots.at())
                dve.scalar_tensor_tensor(nmr, mean, -1.0, root[:], ALU.mult, ALU.mult).then_inc(norm_in, 1)

                def mul(j):
                    dve.tensor_tensor(T[:, j, :], T[:, j, :], bank[6][:], ALU.mult).then_inc(step, 1)
                    steps.add()
                from_pe()
                mul(0)
                from_pe()
                for j in range(n):
                    ahead = 0 < j < n - 1
                    if ahead:
                        mul(j + 1)
                    dve.wait_ge(step, steps.at(-1 if ahead else 0))
                    dve.tensor_tensor(T[:, j, :], T[:, j, :], bank[7][:], ALU.add).then_inc(done, 1)
                    if j == 0:
                        mul(1)

            def layer_norm(next_phase=None, size=2048):
                normalise_tiles(X, KD, src_ready)
                los.add(KD)
                if next_phase:
                    split_unit(FIRST_UNIT[next_phase] + 1, size)

            def mean_square_root(b, eps):
                from_pe()
                dve.tensor_scalar(st[:, 2 * NB:3 * NB], bank[b][:, 0:NB], eps, None, ALU.add).then_inc(var_ready, 1)
                roots.add()

            def residual(scale):
                for j in range(KD):
                    x, b = X[:, j, :], j % 4
                    if j == SHIFT_FROM:
                        from_pe()
                        link(get_shift(6))
                        for i in range(SHIFT_FROM):
                            link(dve.tensor_tensor(X[:, i, :], X[:, i, :], shift[:], ALU.add))
                            accumulate(X, i, KD)
                    if j < SHIFT_FROM:
                        take(lambda: dve.scalar_tensor_tensor(x, x, scale, bank[b][:], ALU.mult, ALU.add))
                    else:
                        link(dve.scalar_tensor_tensor(x, x, scale, shift[:], ALU.mult, ALU.add))
                        take(lambda: dve.tensor_tensor(x, x, bank[b][:], ALU.add))
                        dve.wait_ge(tile_free, tiles.at())
                        accumulate(X, j, KD)

            def out_projection():
                residual(ALPHA)

            def ffn():
                for half in range(2):
                    n = HID[half]
                    with counted_loop(dve, n // 2, {tiles: 4, gates: 2, los: 2}):
                        for i in range(2):
                            dve.wait_ge(gate_done, gates.at(1))
                            dve.wait_ge(act_lo, los.at(-1))
                            take(lambda: dve.tensor_tensor(hf[i][:], sil[i][:], bank[2 * i + 1][:], ALU.mult), 2)
                            gates.add()
                            los.add()
                    if half == 0:
                        for j in range(KD):
                            take(lambda: dve.scalar_tensor_tensor(X[:, j, :], X[:, j, :], ALPHA, bank[j % 4][:], ALU.mult, ALU.add))
                    else:
                        residual(1.0)

            def logits(A, i, m, qb, col, b, bias, scale):
                n = (qb + 1) * P
                dve.wait_ge(aux_done, aux.at(1))
                if aux.reg is not None:
                    dve.memset(spare[:, qb * 2 + m:qb * 2 + m + 1], 0.0)
                aux.add()
                dve.tensor_tensor_reduce(
                    out=A["L"][i][m][:, 0:n], in0=bank[b][:, 0:n], in1=bias[:, S - n:S], scale=-scale, scalar=BIG,
                    op0=ALU.add, op1=ALU.min, accum_out=A["negmax"][:, col:col + 1]).then_inc(aux_free, 1)

            def normalise(A, i, qb, col):
                n = (qb + 1) * P
                exps.add()
                dve.wait_ge(exp_done, exps.at())
                link(dve.reciprocal(A["rinv"][:, col:col + 1], A["rowsum"][:, col:col + 1]))
                row = A["L"][i][0][:, 0:n]
                dve.tensor_scalar(row, row, A["rinv"][:, col:col + 1], None, ALU.mult).then_inc(p_ready, 1)

            def keep_transposed(A, qb):
                n = (qb + 1) * P
                take_aux(lambda: dve.tensor_copy(A["PT"][:, 0:qb + 1, qb * P:n],
                                                 bank[6][:, 0:n].rearrange("p (k q) -> p k q", q=P)))

            def keep_values(dst, b=6):
                take_aux(lambda: dve.tensor_copy(dst[:].rearrange("p k d -> p (k d)"), bank[b][:]))

            def split_unit(u, size):
                s = u % 2
                dve.wait_ge(raw_ready[s], u // 2 * 16 + 16 * s)
                if u > 1:
                    dve.wait_ge(w_used, u - 1)
                link(dve.tensor_copy(whi[s][:, 0:size], raw[s][:, 0:size]))
                dve.tensor_tensor(wlo[s][:, 0:size], raw[s][:, 0:size], whi[s][:, 0:size].bitcast(F32),
                                  ALU.subtract).then_inc(dve_split, 1)

            for k in range(KD):
                dve.wait_ge(first_in[k], 32)
                link(dve.tensor_copy(XH[:, k, :], X[:, k, :]))
                dve.tensor_tensor(XL[:, k, :], X[:, k, :], XH[:, k, :].bitcast(F32), ALU.subtract).then_inc(x_split, 1)
            split_unit(1, 3072)
            dve.wait_ge(par_in, 48)
            dve.tensor_tensor(lam[:, 0:2], parm[:, PCOL["lam"]:PCOL["lam"] + 4:2], parm[:, PCOL["lam"] + 1:PCOL["lam"] + 4:2],
                              ALU.mult).then_inc(small_dve, 1)
            dve.tensor_scalar(gsub[:], pcol("g_sub"), 1.0 - LAMBDA_INIT, None, ALU.mult)

            cosT, sinT, maskT = (rtab[:, RCOL[n]:RCOL[n] + S] for n in ("cos", "sin", "mask"))

            def latent_squares(js, dst):
                for j in js:
                    c = Cf[:, j, :]
                    ins = dve.tensor_tensor((dst if j == js[0] else sqt)[:], c, c, ALU.mult)
                    link(ins)
                    if j > js[0]:
                        ins = dve.tensor_tensor(dst[:], dst[:], sqt[:], ALU.add)
                        if j == js[-1]:
                            ins.then_inc(norm_in, 1)
                        else:
                            link(ins)

            def latents(js, b):
                for j in js:
                    dve.scalar_tensor_tensor(Cf[:, j, :], Cf[:, j, :], pcol("g_c", j), bank[b][:], ALU.mult, ALU.mult)\
                       .then_inc(src_ready, 1)

            def low_latents(js):
                for j in js:
                    dve.wait_ge(act_hi, j + 1)
                    dve.tensor_tensor(CL[:, j, :], Cf[:, j, :], CH[:, j, :].bitcast(F32), ALU.subtract).then_inc(latent_lo, 1)

            for j in range(3):
                copy_tile(Cf[:, j, :], j)
            dve.wait_ge(tile_free, tiles.at())
            latent_squares((0, 1, 2), sq[1])
            copy_tile(Cf[:, 3, :], 3)
            copy_tile(Cf[:, 4, :], 0)
            mean_square_root(5, RMS_EPS)
            dve.wait_ge(tile_free, tiles.at())
            latent_squares((3, 4), sq[0])
            take(lambda: dve.tensor_tensor(KR[:], bank[1][:], cosT, ALU.mult))
            from_pe()
            mean_square_root(5, RMS_EPS)
            latents((0, 1, 2), 6)
            from_pe()
            latents((3, 4), 7)
            low_latents((0, 1, 2))
            take(lambda: dve.tensor_tensor(rt[:], bank[2][:], sinT, ALU.mult))
            low_latents((3, 4))
            dve.wait_ge(tile_free, tiles.at())
            dve.tensor_tensor(KR[:], KR[:], rt[:], ALU.add).then_inc(rope_ready, 1)

            def mla_tile(i, t, ropes):
                b = t % 4
                if t < 2:
                    copy_tile(mQN[i][t][:], b)
                elif t == 2:
                    take(lambda: dve.tensor_tensor(mQR[i][:], bank[b][:], cosT, ALU.mult))
                elif t == 3:
                    dve.wait_ge(rope_ready, ropes)
                    take(lambda: dve.tensor_tensor(rt[:], bank[b][:], sinT, ALU.mult))
                    dve.wait_ge(tile_free, tiles.at())
                    dve.tensor_tensor(mQR[i][:], mQR[i][:], rt[:], ALU.add).then_inc(rope_ready, 1)
                else:
                    copy_tile((mKN[i][t // 2 - 2] if t % 2 == 0 else mVT[t // 2 - 2])[:], b)

            for t in range(8):
                mla_tile(0, t, 1)
            keep_values(mV[0][0], 7)
            keep_values(mV[0][1], 4)
            for p in range(4):
                i, o = p % 2, (p + 1) % 2
                for j in range(8):
                    if j > 0:
                        normalise(ML, (j - 1) % 2, (j - 1) % 4, (j - 1) % 2)
                    logits(ML, j % 2, 0, j % 4, j % 2, 4 + j % 2, maskT, MLA_SCALE)
                    for t in finished(MLA_SLOTS[j], MLA_K) if p < 3 else ():
                        mla_tile(o, t, p + 2)
                    if j == 5:
                        if p:
                            dve.wait_ge(act_lo, los.at(-1))
                        take_aux(lambda: dve.tensor_copy(sq[0][:], bank[7][:]))
                        los.add()
                    if j > 0:
                        keep_transposed(ML, (j - 1) % 4)
                    if j == 7 and p < 3:
                        keep_values(mV[o][0], 7)
                normalise(ML, 1, 3, 1)
                for t in finished(MLA_SLOTS[8], MLA_K) if p < 3 else ():
                    mla_tile(o, t, p + 2)
                keep_transposed(ML, 3)
                if p < 3:
                    keep_values(mV[o][1], 4)
                if p:
                    dve.wait_ge(act_lo, los.at(-1))
                take_aux(lambda: dve.tensor_copy(sq[1][:], bank[7][:]))
                los.add()
            out_projection()
            layer_norm("ffn0")
            ffn()
            layer_norm()

            smalls.add()
            dve.wait_ge(small_act, smalls.at())
            link(dve.tensor_tensor(lam[:, 6:7], lam[:, 4:5], lam[:, 5:6], ALU.subtract))
            link(dve.tensor_scalar(lam[:, 7:8], lam[:, 6:7], LAMBDA_INIT, None, ALU.add))

            def scale_head(i, head):
                from_pe()
                out = DF["Y"][:, head, :] if isinstance(head, int) else \
                    DF["Y"][:, bass.ds(head, 1), :].rearrange("p o n -> p (o n)")
                dve.scalar_tensor_tensor(out, dO[i][:], gsub[:], bank[7][:], ALU.mult, ALU.mult).then_inc(src_ready, 1)

            def diff_head(i, h, first, last_one):
                o = 1 - i
                col = cons[:, CCOL["slopes"] + h:CCOL["slopes"] + h + 1] if isinstance(h, int) else \
                    cons[:, bass.ds(h + CCOL["slopes"], 1)]
                link(dve.tensor_scalar(dB[:], dist, col, None, ALU.mult))
                for j in range(4):
                    if j > 0:
                        combine(j - 1)
                    for m in range(2):
                        logits(DF, j % 2, m, j, 2 * (j % 2) + m, 4 + m, dB[:], HD_SCALE)
                    for t in finished(DIFF_SLOTS[j], (KD,) * 3) if not last_one else ():
                        copy_tile((dVT, dQ[o], dK[o])[t][:], t)
                    if j > 0:
                        keep_transposed(DF, j - 1)
                    if j == 1 and not first:
                        mean_square_root(7, RMS_EPS)
                    if j == 2 and not first:
                        scale_head(o, h - 1)
                    if j == 3 and not last_one:
                        keep_values(dV[o], 7)
                combine(3)
                for t in finished(DIFF_SLOTS[4], (KD,) * 3) if not last_one else ():
                    copy_tile((dVT, dQ[o], dK[o])[t][:], t)
                keep_transposed(DF, 3)
                for t in finished(DIFF_SLOTS[5], (KD,) * 3) if not last_one else ():
                    copy_tile((dVT, dQ[o], dK[o])[t][:], t)
                take_aux(lambda: dve.tensor_copy(dO[i][:], bank[7][:]))
                dve.wait_ge(aux_free, aux.at())
                dve.tensor_tensor(sqt[:], dO[i][:], dO[i][:], ALU.mult).then_inc(norm_in, 1)

            def combine(j):
                n, c = (j + 1) * P, 2 * (j % 2)
                exps.add(2)
                dve.wait_ge(exp_done, exps.at())
                link(dve.reciprocal(DF["rinv"][:, c:c + 2], DF["rowsum"][:, c:c + 2]))
                p0, p1 = (DF["L"][j % 2][m][:, 0:n] for m in range(2))
                link(dve.tensor_scalar(p1, p1, DF["rinv"][:, c + 1:c + 2], lam[:, 7:8], ALU.mult, ALU.mult))
                dve.scalar_tensor_tensor(p0, p0, DF["rinv"][:, c:c + 1], p1, ALU.mult, ALU.subtract).then_inc(p_ready, 1)

            for t in range(3):
                copy_tile((dVT, dQ[0], dK[0])[t][:], t)
            keep_values(dV[0])
            diff_head(0, 0, True, False)
            with counted_loop(dve, 3, {tiles: 6, aux: 28, steps: 18, exps: 16, outs: 4, roots: 2}) as it:
                diff_head(1, it * 2 + 1, False, False)
                diff_head(0, it * 2 + 2, False, False)
            diff_head(1, 7, False, True)
            mean_square_root(7, RMS_EPS)
            scale_head(1, 7)
            los.add(KD)
            out_projection()
            layer_norm("ffn1")
            ffn()
            layer_norm("ev_in")

            dve.memset(ez[:, 0:2], 0.0)
            for u in eu:
                dve.memset(u[:, 0:PADW], 0.0)

            pooled = LATENTS + 5 * KD
            def conv_col(k, i):
                return pcol("conv_w", 4 * k + i)

            for i in range(4):
                if i:
                    dve.wait_ge(src_ready, pooled + i)
                take(lambda: dve.tensor_copy(eu[0][:, PADW:], bank[i][:]))
                dve.wait_ge(tile_free, tiles.at())
                src = eu[0]
                for d in range(i + 1):
                    dst = eu[1 + d % 2]
                    link(dve.tensor_tensor(dst[:, PADW:], src[:, PADW:], src[:, PADW - 2 ** d:PADW - 2 ** d + S], ALU.add))
                    src = dst
                link(dve.scalar_tensor_tensor(EP[:, i, PADW:], src[:, 2 * PADW:], 1.0 / WINDOWS[i], eu[0][:, 2 * PADW:], ALU.mult, ALU.subtract))
                link(dve.tensor_tensor(EP[:, i, 0:PADW], src[:, PADW:2 * PADW], cons[:, CCOL["invcnt"] + 16 * i:CCOL["invcnt"] + 16 * i + 16], ALU.mult))
                dve.tensor_tensor(EP[:, i, 0:PADW], EP[:, i, 0:PADW], eu[0][:, PADW:2 * PADW], ALU.subtract).then_inc(src_ready, 1)
            for i in range(4):
                b = 2 * i % 4
                copy_tile(ec[:], b)
                dve.wait_ge(tile_free, tiles.at())
                take(lambda: dve.tensor_tensor(ez[:, 2:2 + S], bank[b + 1][:], ec[:], ALU.mult))
                dve.wait_ge(tile_free, tiles.at())
                y = EY[:, i, :]
                link(dve.tensor_scalar(y, ez[:, 0:S], conv_col(0, i), None, ALU.mult))
                for k in (1, 2):
                    link(dve.scalar_tensor_tensor(y, ez[:, k:k + S], conv_col(k, i), y, ALU.mult, ALU.add))
            los.add(4)
            for i in range(4):
                take(lambda: dve.tensor_scalar(EY[:, 4 + i, :], bank[i][:], pcol("pool_s", i), None, ALU.mult))
            for i in range(4):
                take(lambda: dve.tensor_tensor(EY[:, i, :], bank[i][:], EY[:, i, :], ALU.mult))
            los.add(KD)
            out_projection()
            layer_norm("ffn2")
            ffn()
            layer_norm("od_glu0", 1024)

            for i in range(4):
                dve.memset(fz[i][:, 0:PADC], 0.0)

            def glu(i):
                dve.wait_ge(gate_done, gates.at(1))
                gates.add()
                take(lambda: dve.tensor_tensor(fz[i][:, PADC:], fsig[:], bank[GLU_BANKS[i][0]][:], ALU.mult), 2)
                dve.wait_ge(tile_free, tiles.at())

            taps_left = [(i, k) for i in range(2) for k in range(TAPS)]

            def taps(n):
                for _ in range(n):
                    i, k = taps_left.pop(0)
                    y = FO["Y"][:, 4 + i, :]
                    wk = pcol("dw_w", 4 * k + i)
                    if k == 0:
                        link(dve.tensor_scalar(y, fz[i][:, 0:S], wk, pcol("dw_b", i), ALU.mult, ALU.add))
                    else:
                        link(dve.scalar_tensor_tensor(y, fz[i][:, k:k + S], wk, y, ALU.mult, ALU.add))

            glu(0)
            taps(7)

            take(lambda: dve.tensor_scalar(lfz[:], bank[2][0:8, :], parm[0:8, PCOL["f_b"]:PCOL["f_b"] + 1], None, ALU.add))
            smalls.add(2)
            dve.wait_ge(small_act, smalls.at())
            dve.tensor_scalar(lfu[:], lfe[:], 1.0, None, ALU.add).then_inc(small_dve, 1)
            dve.wait_ge(small_dve, 2)
            link(dve.tensor_scalar(lfd[:], lfu[:], 1.0, None, ALU.subtract))
            link(dve.tensor_scalar(lfi[:], lfd[:], 0.0, None, ALU.is_equal))
            link(dve.tensor_tensor(lfd[:], lfd[:], lfi[:], ALU.add))
            link(dve.reciprocal(lfr[:], lfd[:]))
            link(dve.tensor_tensor(lfr[:], lfe[:], lfr[:], ALU.mult))
            smalls.add()
            dve.wait_ge(small_act, smalls.at())
            link(dve.tensor_tensor(lfr[:], lfl[:], lfr[:], ALU.mult))
            link(dve.tensor_tensor(lfi[:], lfi[:], lfe[:], ALU.mult))
            link(dve.tensor_tensor(lfr[:], lfr[:], lfi[:], ALU.add))
            link(dve.tensor_scalar(lfz[:], lfz[:], 0.0, None, ALU.min))
            link(dve.tensor_tensor(lfz[:], lfz[:], lfr[:], ALU.subtract))
            link(dve.memset(lfd[:], 0.0))
            dve.tensor_tensor_scan(cum[:], lfz[:], lfd[:], 0.0, ALU.add, ALU.add).then_inc(cum_ready, 1)

            for i in (1, 2):
                glu(i)
                taps(12)
            glu(3)

            def forget_logits(i, m, qb, col, b):
                n0 = qb * P
                dve.wait_ge(aux_done, aux.at(1))
                first = BIG
                if qb:
                    first = FO["negmax"][:, 2 + col:3 + col]
                    link(dve.tensor_tensor_reduce(
                        out=FO["L"][i][0][:, 0:n0], in0=bank[b][:, 0:n0], in1=fB[m][:, 0:n0], scale=-HD_SCALE, scalar=BIG,
                        op0=ALU.add, op1=ALU.min, accum_out=first))
                take_aux(lambda: dve.tensor_tensor_reduce(
                    out=FO["L"][i][0][:, n0:n0 + P], in0=bank[b][:, n0:n0 + P], in1=fBD[m][:, qb, :], scale=-HD_SCALE,
                    scalar=first, op0=ALU.add, op1=ALU.min, accum_out=FO["negmax"][:, col:col + 1]))

            C = FO["Y"][:, 4:8, :]

            def add_channels(i):
                if i >= 2:
                    dve.wait_ge(tap_added, (i - 1) * (TAPS - 1))
                link(dve.tensor_tensor(C[:, i, :], C[:, i, :], shift[:], ALU.add))
                accumulate(C, i, 4)

            for t in range(3):
                taps((6, 6, 3)[t])
                copy_tile((fVT, fQ[0], fK[0])[t][:], 1 + t)
            keep_values(fV[0])
            for g in range(4):
                o = (g + 1) % 2
                if g == 1:
                    take_aux(lambda: get_shift(5))
                    dve.wait_ge(aux_free, aux.at())
                    link(dve.tensor_tensor(C[:, 0, :], C[:, 0, :], shift[:], ALU.add))
                    accumulate(C, 0, 4)

                def gate_bias(m):
                    take_aux(lambda: dve.tensor_scalar(fB[m][:], bank[6 + m][:], -1.0 / HD_SCALE, None, ALU.mult))
                    dve.wait_ge(aux_free, aux.at())
                    link(dve.tensor_tensor(fBD[m][:], fB[m][:].rearrange("p (k q) -> p k q", q=P),
                                           causal.unsqueeze(1).to_broadcast([P, NB, P]), ALU.add))

                gate_bias(0)
                for j in range(8):
                    if j > 0:
                        normalise(FO, (j - 1) % 2, (j - 1) % 4, (j - 1) % 2)
                    forget_logits(j % 2, j // 4, j % 4, j % 2, 4 + j % 2)
                    if j == 1:
                        gate_bias(1)
                    for t in finished(ODD_SLOTS[j], (KD,) * 3) if g < 3 else ():
                        copy_tile((fVT, fQ[o], fK[o])[t][:], t)
                    if j == 5:
                        take_aux(lambda: dve.tensor_copy(FO["Y"][0:64, g, :], bank[7][0:64, :]))
                    if j > 0:
                        keep_transposed(FO, (j - 1) % 4)
                    if j == 7 and g < 3:
                        keep_values(fV[o], 7)
                    taps(min(1, len(taps_left)))
                    if j == 1 and g > 1:
                        add_channels(g - 1)
                normalise(FO, 1, 3, 1)
                for t in finished(ODD_SLOTS[8], (KD,) * 3) if g < 3 else ():
                    copy_tile((fVT, fQ[o], fK[o])[t][:], t)
                keep_transposed(FO, 3)
                for t in finished(ODD_SLOTS[9], (KD,) * 3) if g < 3 else ():
                    copy_tile((fVT, fQ[o], fK[o])[t][:], t)
                take_aux(lambda: dve.tensor_copy(FO["Y"][64:P, g, :], bank[7][64:P, :]))
            add_channels(3)
            assert not taps_left
            normalise_tiles(C, 4, src_ready)
            los.add(KD)
            out_projection()
            layer_norm("ffn3")
            ffn()
            layer_norm()


def host_layout(inp):
    f = lambda a: np.asarray(a)

    def ktiles(m):
        return m.reshape(m.shape[0] // P, P, m.shape[1]).transpose(1, 0, 2)

    def unit(m, size=None):
        u = ktiles(m).reshape(P, -1)
        return u if size is None or u.shape[1] == size else np.pad(u, ((0, 0), (0, size - u.shape[1])))

    def out3(m):
        return np.stack([unit(m[:, 0:384]), unit(m[:, 384:768]), unit(m[:, 768:1024], 3072)])

    w = {}
    swap = np.r_[32:64, 0:32]
    win = f(inp["mla_w_in"])[0]
    kr = win[:, 640:704]
    w["mla_in"] = np.stack([unit(win[:, 0:384]), unit(np.concatenate([win[:, 384:640], kr, kr], 1)),
                            unit(np.concatenate([kr[:, swap]] * 2, 1), 3072)])
    uq, ukv = f(inp["mla_w_uq"])[0].reshape(QR, 8, 192), f(inp["mla_w_ukv"])[0]
    pairs = []
    for p in range(4):
        a, b = uq[:, 2 * p], uq[:, 2 * p + 1]
        ra, rb = a[:, 128:], b[:, 128:]
        q = np.concatenate([a[:, :128], b[:, :128], ra, rb, ra[:, swap], rb[:, swap]], 1)
        pairs.append(np.concatenate([unit(q), unit(ukv[:, 512 * p:512 * p + 512])], 1))
    w["mla_pair"] = np.stack(pairs)
    w["mla_o"] = out3(f(inp["mla_w_o"])[0])
    ffns = [(f(inp["ffn_w_gu"])[i], f(inp["ffn_w_down"])[i]) for i in range(2)] + \
           [(f(inp["ffn_w_in_2"])[i], f(inp["ffn_w_out_2"])[i]) for i in range(2)]
    for i, (gu, down) in enumerate(ffns):
        g = gu.reshape(KD, P, 2, D_FF // P, P).transpose(3, 1, 0, 2, 4)
        w[f"ffn{i}_gu"] = g.reshape(D_FF // P, P, 2048)
        for half, r0, n in ((0, 0, HID[0]), (1, HID[0], HID[1])):
            d = down[r0 * P:(r0 + n) * P]
            w[f"ffn{i}_d{half}"] = d.reshape(n, P, 4, 256).transpose(2, 1, 0, 3).reshape(4, P, n * 256)
    vqk = np.array([2, 0, 1])
    win = f(inp["diff_w_in"])[0].reshape(KD, P, 3, 8, P)[:, :, vqk].transpose(3, 1, 0, 2, 4)
    w["diff_in"] = win.reshape(8, P, 3072)
    w["diff_o"] = out3(f(inp["diff_w_o"])[0])
    win = f(inp["ev_w_in_2"])[0].reshape(KD, P, 4, 4, P)
    u, b = (win[:, :, i].reshape(KD, P, 2, 2, P).transpose(2, 1, 0, 3, 4).reshape(2, P, 2048) for i in (3, 0))
    cv = win[:, :, 1:3].transpose(3, 1, 0, 2, 4).reshape(4, P, 2048)
    pool = f(inp["ev_pool_w_2"])[0].transpose(1, 0, 2).reshape(P, 512)
    w["ev_in"] = np.concatenate([u, cv])
    w["ev_b"] = np.stack([np.concatenate([b[0], pool], 1), np.pad(b[1], ((0, 0), (0, 512)))])
    m = f(inp["ev_w_out_2"])[0]
    w["ev_o"] = out3(np.concatenate([m[D // 2:], m[:D // 2]]))
    win = f(inp["od_w_in_2"])[0]
    w["od_f"] = unit(win[:, 1536:1664])[None]
    glu = win[:, 1544:2568].reshape(KD, P, 2, 4, P).transpose(3, 1, 0, 2, 4).reshape(4, P, 2048)
    w["od_glu0"], w["od_glu"] = glu[0:1], glu[1:]
    w["od_in"] = win[:, 0:1536].reshape(KD, P, 3, 4, P)[:, :, vqk].transpose(3, 1, 0, 2, 4).reshape(4, P, 3072)
    w["od_o"] = out3(f(inp["od_w_out_2"])[0])

    cols = lambda a: f(a).reshape(-1, P).T
    pad = lambda a: np.pad(f(a).reshape(-1, 1), ((0, P - f(a).size), (0, 0)))
    par = np.concatenate([
        cols(inp["ln_mix_g"]), cols(inp["ln_ffn_g"]), cols(inp["ln_mix_g_2"]), cols(inp["ln_ffn_g_2"]),
        cols(inp["ln_mix_b"]), cols(inp["ln_ffn_b"]), cols(inp["ln_mix_b_2"]), cols(inp["ln_ffn_b_2"]),
        cols(inp["mla_g_q"]), cols(inp["mla_g_kv"]), cols(inp["diff_g_sub"]), cols(inp["ev_conv_w_2"]),
        cols(inp["ev_pool_scale_2"]), cols(inp["od_dw_w_2"]), cols(inp["od_dw_b_2"]), cols(inp["od_cn_g_2"]),
        cols(inp["od_cn_b_2"]), pad(inp["diff_lam_q1"]), pad(inp["diff_lam_k1"]), pad(inp["diff_lam_q2"]),
        pad(inp["diff_lam_k2"]), pad(inp["od_forget_b_2"])], 1)
    assert par.shape == (P, NPAR)
    return w, par


def constants():
    p = np.arange(P)[:, None]
    con = np.zeros((P, NCON), np.float32)
    con[:, CCOL["ident"]:CCOL["ident"] + P] = np.eye(P)
    x = np.arange(S)[None, :]
    hidden = (x - (S - P)) // 64 > p // 64
    con[:, CCOL["dist"]:CCOL["dist"] + S] = np.where(hidden, 1e32, np.abs(p + (S - P) - x))
    con[:, CCOL["causal"]:CCOL["causal"] + P] = np.where(np.arange(P)[None, :] > p, NEG, 0.0)
    for g, win in enumerate(WINDOWS):
        con[:, CCOL["invcnt"] + 16 * g:CCOL["invcnt"] + 16 * g + 16] = 1.0 / np.minimum(np.arange(16) + 1, win)
    con[:, CCOL["slopes"]:CCOL["slopes"] + 8] = -2.0 ** -np.arange(1, 9) / HD_SCALE
    inv = np.float32(10000.0) ** (-np.arange(0, ROPE, 2, dtype=np.float32) / np.float32(ROPE))
    ang = (np.arange(S, dtype=np.float32)[None, :] * inv[:, None].astype(np.float32)).astype(np.float32)
    cos, sin = np.cos(ang), np.sin(ang)
    rcon = np.concatenate([np.concatenate([cos] * 4), np.concatenate([-sin, sin] * 2),
                           np.where(hidden, NEG, 0.0)], 1).astype(np.float32)
    return con, rcon


def kernel(**inputs):
    import concourse.bacc as bacc
    from concourse.bass_utils import run_bass_kernel_spmd

    w, par = host_layout(inputs)
    con, rcon = constants()
    arrays = {"xT": np.asarray(inputs["x"])[0].T.reshape(KD, P, S), "par": par, "con": con, "rcon": rcon}
    arrays.update({f"w_{k}": v for k, v in w.items()})
    arrays = {k: np.ascontiguousarray(v) for k, v in arrays.items()}
    nc = bacc.Bacc("TRN2", target_bir_lowering=False, num_devices=1)
    ap = {k: nc.dram_tensor(k, v.shape, F32, kind="ExternalInput").ap() for k, v in arrays.items()}
    outT = nc.dram_tensor("outT", (KD, P, S), F32, kind="ExternalOutput").ap()
    build(nc, ap["xT"], ap["par"], ap["con"], ap["rcon"], {k: ap[f"w_{k}"] for k in w}, outT)
    r = run_bass_kernel_spmd(nc, [arrays], core_ids=[0])
    return np.ascontiguousarray(np.asarray(r.results[0]["outT"]).reshape(D, S).T)[None]
```
